# Optimizing a Trainium2 kernel written in Bass

```python
import jax, jax.numpy as jnp
from jax import lax
import numpy as np

D_MODEL = 2048
BATCH = 1
SEQ = 256
DEPTH = 1

HEAD_DIM = 128
N_ATTN_HEADS = 8
ATTN_WIDTH = N_ATTN_HEADS * HEAD_DIM
CONV_CHANNELS = D_MODEL - ATTN_WIDTH
CONV_GROUPS = 8
MIX_WIDTH = ATTN_WIDTH + CONV_CHANNELS
IN_COLS = 3 * ATTN_WIDTH + 2 * CONV_CHANNELS
MOBA_BLOCK = 256
MOBA_TOPK = 3
Q_CHUNK = 64
CONV_WIDTH = 31
D_FF = 4 * D_MODEL
RMS_EPS = 1e-6
LN_EPS = 1e-5


def rms_norm(x, g):
    xf = x.astype(jnp.float32)
    y = xf * lax.rsqrt(jnp.mean(xf * xf, axis=-1, keepdims=True) + RMS_EPS)
    return (y * g.astype(jnp.float32)).astype(x.dtype)

def layer_norm(x, g, b):
    xf = x.astype(jnp.float32)
    mu = jnp.mean(xf, axis=-1, keepdims=True)
    var = jnp.mean(jnp.square(xf - mu), axis=-1, keepdims=True)
    y = (xf - mu) * lax.rsqrt(var + LN_EPS)
    return (y * g.astype(jnp.float32) + b.astype(jnp.float32)).astype(x.dtype)

def alibi_slopes(n_heads):
    return jnp.asarray(2.0 ** (-8.0 * np.arange(1, n_heads + 1) / n_heads), dtype=jnp.float32)

def moba_attention(q, k, v):
    B, H, S, Dh = q.shape
    L = MOBA_BLOCK
    n_blocks = -(-S // L)
    pad = n_blocks * L - S
    kp = jnp.pad(k, ((0, 0), (0, 0), (0, pad), (0, 0)))
    vp = jnp.pad(v, ((0, 0), (0, 0), (0, pad), (0, 0)))
    k_blk = kp.reshape(B, H, n_blocks, L, Dh)
    v_blk = vp.reshape(B, H, n_blocks, L, Dh)
    k_mean = jnp.mean(k_blk.astype(jnp.float32), axis=3)
    topk = min(MOBA_TOPK, n_blocks)
    scale = Dh ** -0.5
    slopes = alibi_slopes(H)
    n_chunks = S // Q_CHUNK
    q_chunks = q.reshape(B, H, n_chunks, Q_CHUNK, Dh).transpose(2, 0, 1, 3, 4)
    gather = jax.vmap(jax.vmap(lambda blocks, idx: blocks[idx]))
    neg_inf = -jnp.inf

    def chunk_fn(args):
        c, qc = args
        q0 = c * Q_CHUNK
        blk = q0 // L
        q_pos = q0 + jnp.arange(Q_CHUNK)
        gate = jnp.einsum('bhqd,bhnd->bhqn', qc.astype(jnp.float32), k_mean)
        gate = jnp.where(jnp.arange(n_blocks) < blk, gate, neg_inf)
        _, sel = lax.top_k(gate, topk)
        sel_valid = jnp.arange(topk) < blk
        k_sel = gather(k_blk, sel)
        v_sel = gather(v_blk, sel)
        s_sel = jnp.einsum('bhqd,bhqrld->bhqrl', qc, k_sel,
                           preferred_element_type=jnp.float32) * scale
        k_pos_sel = sel[..., None] * L + jnp.arange(L)
        dist_sel = jnp.abs(q_pos[None, None, :, None, None] - k_pos_sel).astype(jnp.float32)
        s_sel = jnp.where(sel_valid[:, None],
                          s_sel - slopes[None, :, None, None, None] * dist_sel, neg_inf)
        k_own = lax.dynamic_slice_in_dim(kp, blk * L, L, axis=2)
        v_own = lax.dynamic_slice_in_dim(vp, blk * L, L, axis=2)
        s_own = jnp.einsum('bhqd,bhld->bhql', qc, k_own,
                           preferred_element_type=jnp.float32) * scale
        k_pos_own = blk * L + jnp.arange(L)
        dist_own = jnp.abs(q_pos[:, None] - k_pos_own[None, :]).astype(jnp.float32)
        causal = k_pos_own[None, :] <= q_pos[:, None]
        s_own = jnp.where(causal, s_own - slopes[:, None, None] * dist_own, neg_inf)
        s = jnp.concatenate([s_sel.reshape(B, H, Q_CHUNK, topk * L), s_own], axis=-1)
        p = jax.nn.softmax(s, axis=-1)
        p_sel = p[..., :topk * L].reshape(B, H, Q_CHUNK, topk, L).astype(v.dtype)
        p_own = p[..., topk * L:].astype(v.dtype)
        out = (jnp.einsum('bhqrl,bhqrld->bhqd', p_sel, v_sel, preferred_element_type=jnp.float32)
               + jnp.einsum('bhql,bhld->bhqd', p_own, v_own, preferred_element_type=jnp.float32))
        return out.astype(qc.dtype)

    out = lax.map(chunk_fn, (jnp.arange(n_chunks), q_chunks))
    return out.transpose(1, 0, 3, 2, 4).reshape(B, S, H * Dh)

def conformer_conv(u, b_glu, w_dw, b_dw, ln_g, ln_b):
    u = u + b_glu
    val, gt = jnp.split(u, 2, axis=-1)
    h = val * jax.nn.sigmoid(gt)
    C = h.shape[-1]
    rhs = w_dw.reshape(CONV_WIDTH, 1, C)
    y = lax.conv_general_dilated(h, rhs, window_strides=(1,),
                                 padding=[(CONV_WIDTH - 1, 0)],
                                 dimension_numbers=('NWC', 'WIO', 'NWC'),
                                 feature_group_count=C)
    y = layer_norm(y + b_dw, ln_g, ln_b)
    return jax.nn.silu(y)

def first_inputs(seed: int = 0) -> dict:
    key = jax.random.key(seed)
    ks = jax.random.split(key, 14)
    f32 = jnp.float32

    def nrm(k, shape, scale):
        return jax.random.normal(k, shape, f32) * scale

    def gain(k, shape):
        return 1.0 + 0.02 * jax.random.normal(k, shape, f32)

    return {
        'x': nrm(ks[0], (BATCH, SEQ, D_MODEL), 1.0),
        'g_mix_pre': gain(ks[1], (DEPTH, D_MODEL)),
        'w_in': nrm(ks[2], (DEPTH, D_MODEL, IN_COLS), D_MODEL ** -0.5),
        'b_glu': nrm(ks[3], (DEPTH, 2 * CONV_CHANNELS), 0.02),
        'w_dw': nrm(ks[4], (DEPTH, CONV_WIDTH, CONV_CHANNELS), CONV_WIDTH ** -0.5),
        'b_dw': nrm(ks[5], (DEPTH, CONV_CHANNELS), 0.02),
        'ln_conv_g': gain(ks[6], (DEPTH, CONV_CHANNELS)),
        'ln_conv_b': nrm(ks[7], (DEPTH, CONV_CHANNELS), 0.02),
        'w_out': nrm(ks[8], (DEPTH, MIX_WIDTH, D_MODEL), MIX_WIDTH ** -0.5),
        'g_mix_post': gain(ks[9], (DEPTH, D_MODEL)),
        'g_ffn_pre': gain(ks[10], (DEPTH, D_MODEL)),
        'w_ff1': nrm(ks[11], (DEPTH, D_MODEL, D_FF), D_MODEL ** -0.5),
        'w_ff2': nrm(ks[12], (DEPTH, D_FF, D_MODEL), D_FF ** -0.5),
        'g_ffn_post': gain(ks[13], (DEPTH, D_MODEL)),
    }

def first_block(x, g_mix_pre, w_in, b_glu, w_dw, b_dw, ln_conv_g, ln_conv_b, w_out,
              g_mix_post, g_ffn_pre, w_ff1, w_ff2, g_ffn_post):
    B, S, _ = x.shape
    h = x
    for l in range(DEPTH):
        a = rms_norm(h, g_mix_pre[l])
        proj = a @ w_in[l]
        q = proj[..., :ATTN_WIDTH]
        k = proj[..., ATTN_WIDTH:2 * ATTN_WIDTH]
        v = proj[..., 2 * ATTN_WIDTH:3 * ATTN_WIDTH]
        u = proj[..., 3 * ATTN_WIDTH:]
        to_heads = lambda t: t.reshape(B, S, N_ATTN_HEADS, HEAD_DIM).transpose(0, 2, 1, 3)
        attn = moba_attention(to_heads(q), to_heads(k), to_heads(v))
        conv = conformer_conv(u, b_glu[l], w_dw[l], b_dw[l], ln_conv_g[l], ln_conv_b[l])
        mixed = jnp.concatenate([attn, conv], axis=-1) @ w_out[l]
        h = h + rms_norm(mixed, g_mix_post[l])
        f = rms_norm(h, g_ffn_pre[l])
        f = jnp.square(jax.nn.relu(f @ w_ff1[l])) @ w_ff2[l]
        h = h + rms_norm(f, g_ffn_post[l])
    return h


DEPTH_2 = 2

GRID_W = 64
CTX_LEN = 256
HALF_DIM = HEAD_DIM // 2
AXIS_FREQS = HEAD_DIM // 4
ROPE_THETA = 10000.0
N_HEADS_A = 8
N_KV_A = 2
N_HEADS_B = 8
N_KV_B = 2
G_A = N_HEADS_A // N_KV_A
G_B = N_HEADS_B // N_KV_B
Q_BLOCK = 128
WINDOW = 128
BAND = Q_BLOCK + 2 * WINDOW
ATTN_SCALE = HEAD_DIM ** -0.5
NEG_INF = -1e30
Q_W = (N_HEADS_A + N_HEADS_B) * HEAD_DIM
KV_A_W = N_KV_A * HEAD_DIM
KV_B_W = N_KV_B * HEAD_DIM
KV_W = 2 * KV_A_W + 2 * KV_B_W
ATTN_WIDTH_2 = Q_W
EVEN_IN = Q_W + KV_W + ATTN_WIDTH_2
POOL_WIDTH = D_MODEL
POOL_SIZES = (2, 4, 8, 16)
N_POOL_GROUPS = len(POOL_SIZES)
POOL_GROUP = POOL_WIDTH // N_POOL_GROUPS
ODD_IN = 2 * POOL_WIDTH
EPS = 1e-6
N_EVEN = (DEPTH_2 + 1) // 2
N_ODD = DEPTH_2 // 2


def _rmsnorm(x, g):
    xf = x.astype(jnp.float32)
    y = xf * lax.rsqrt(jnp.mean(xf * xf, axis=-1, keepdims=True) + EPS)
    return (y * g.astype(jnp.float32)).astype(x.dtype)

def _modulation(cvec, w, b):
    m = jax.nn.silu(cvec) @ w + b
    m = m[..., None, :]
    return m[..., :D_MODEL], m[..., D_MODEL:2 * D_MODEL], m[..., 2 * D_MODEL:]

def _axial_rope(rows):
    row = jnp.broadcast_to(jnp.arange(rows)[:, None], (rows, GRID_W)).reshape(-1).astype(jnp.float32)
    col = jnp.broadcast_to(jnp.arange(GRID_W)[None, :], (rows, GRID_W)).reshape(-1).astype(jnp.float32)
    inv = ROPE_THETA ** (-jnp.arange(AXIS_FREQS, dtype=jnp.float32) / AXIS_FREQS)
    ang = jnp.concatenate([row[:, None] * inv, col[:, None] * inv], axis=-1)
    return jnp.cos(ang), jnp.sin(ang)

def _rope(x, cos, sin):
    shape = (cos.shape[0],) + (1,) * (x.ndim - 3) + (cos.shape[1],)
    cos = cos.reshape(shape)
    sin = sin.reshape(shape)
    xf = x.astype(jnp.float32)
    x1, x2 = xf[..., :HALF_DIM], xf[..., HALF_DIM:]
    return jnp.concatenate([x1 * cos - x2 * sin, x2 * cos + x1 * sin], axis=-1).astype(x.dtype)

def _split_kv(kv):
    B, L = kv.shape[:2]
    kA = kv[..., :KV_A_W].reshape(B, L, N_KV_A, HEAD_DIM)
    vA = kv[..., KV_A_W:2 * KV_A_W].reshape(B, L, N_KV_A, HEAD_DIM)
    kB = kv[..., 2 * KV_A_W:2 * KV_A_W + KV_B_W].reshape(B, L, N_KV_B, HEAD_DIM)
    vB = kv[..., 2 * KV_A_W + KV_B_W:].reshape(B, L, N_KV_B, HEAD_DIM)
    return kA, vA, kB, vB

def _split_q(q):
    B, L = q.shape[:2]
    q = q.reshape(B, L, N_HEADS_A + N_HEADS_B, HEAD_DIM)
    qA = q[:, :, :N_HEADS_A].reshape(B, L, N_KV_A, G_A, HEAD_DIM)
    qB = q[:, :, N_HEADS_A:].reshape(B, L, N_KV_B, G_B, HEAD_DIM)
    return qA, qB

def _dense_attention(q, k, v):
    B, L = q.shape[:2]
    nb = L // Q_BLOCK

    def block(n):
        qb = lax.dynamic_slice_in_dim(q, n * Q_BLOCK, Q_BLOCK, axis=1)
        s = jnp.einsum('bqkgd,bskd->bkgqs', qb, k).astype(jnp.float32) * ATTN_SCALE
        p = jax.nn.softmax(s, axis=-1).astype(v.dtype)
        return jnp.einsum('bkgqs,bskd->bqkgd', p, v)

    o = lax.map(block, jnp.arange(nb))
    return jnp.moveaxis(o, 0, 1).reshape(B, L, -1)

def _window_attention(q, k, v, kc, vc, sink):
    B, L, KV, G, _ = q.shape
    C = kc.shape[1]
    nb = L // Q_BLOCK
    pad = ((0, 0), (WINDOW, WINDOW), (0, 0), (0, 0))
    kp = jnp.pad(k, pad)
    vp = jnp.pad(v, pad)
    sink_l = sink.astype(jnp.float32).reshape(1, KV, G, 1, 1)

    def block(n):
        start = n * Q_BLOCK
        qb = lax.dynamic_slice_in_dim(q, start, Q_BLOCK, axis=1)
        kb = lax.dynamic_slice_in_dim(kp, start, BAND, axis=1)
        vb = lax.dynamic_slice_in_dim(vp, start, BAND, axis=1)
        qpos = start + jnp.arange(Q_BLOCK)
        kpos = start - WINDOW + jnp.arange(BAND)
        valid = (jnp.abs(kpos[None, :] - qpos[:, None]) <= WINDOW) & (kpos >= 0)[None, :] & (kpos < L)[None, :]
        s_band = jnp.einsum('bqkgd,bjkd->bkgqj', qb, kb).astype(jnp.float32) * ATTN_SCALE
        s_band = jnp.where(valid, s_band, NEG_INF)
        s_ctx = jnp.einsum('bqkgd,bckd->bkgqc', qb, kc).astype(jnp.float32) * ATTN_SCALE
        s_sink = jnp.broadcast_to(sink_l, s_ctx.shape[:-1] + (1,))
        p = jax.nn.softmax(jnp.concatenate([s_band, s_ctx, s_sink], axis=-1), axis=-1).astype(v.dtype)
        return (jnp.einsum('bkgqj,bjkd->bqkgd', p[..., :BAND], vb)
                + jnp.einsum('bkgqc,bckd->bqkgd', p[..., BAND:BAND + C], vc))

    o = lax.map(block, jnp.arange(nb))
    return jnp.moveaxis(o, 0, 1).reshape(B, L, -1)

def _ctx_attention(q, k, v, sink=None):
    B, C = q.shape[:2]
    s = jnp.einsum('bqkgd,bckd->bkgqc', q, k).astype(jnp.float32) * ATTN_SCALE
    if sink is not None:
        KV, G = q.shape[2], q.shape[3]
        s_sink = jnp.broadcast_to(sink.astype(jnp.float32).reshape(1, KV, G, 1, 1), s.shape[:-1] + (1,))
        p = jax.nn.softmax(jnp.concatenate([s, s_sink], axis=-1), axis=-1)[..., :C]
    else:
        p = jax.nn.softmax(s, axis=-1)
    return jnp.einsum('bkgqc,bckd->bqkgd', p.astype(v.dtype), v).reshape(B, C, -1)

def _attention_layer(x, ctx, cos, sin, c, c_ctx, mod_w, mod_b, pre_g, post_g, w_in, q_norm, k_norm, sink, w_out, need_ctx_out):
    shift, scale, gate = _modulation(c, mod_w, mod_b)
    shift_c, scale_c, gate_c = _modulation(c_ctx, mod_w, mod_b)
    h = _rmsnorm(x, pre_g) * (1 + scale) + shift
    hc = _rmsnorm(ctx, pre_g) * (1 + scale_c) + shift_c

    proj = h @ w_in
    qA, qB = _split_q(proj[..., :Q_W])
    kA, vA, kB, vB = _split_kv(proj[..., Q_W:Q_W + KV_W])
    z = proj[..., Q_W + KV_W:]

    kA_c, vA_c, kB_c, vB_c = _split_kv(hc @ w_in[:, Q_W:Q_W + KV_W])
    kA_c = _rmsnorm(kA_c, k_norm)

    qA = _rope(_rmsnorm(qA, q_norm), cos, sin)
    kA = _rope(_rmsnorm(kA, k_norm), cos, sin)
    outA = _dense_attention(qA, jnp.concatenate([kA, kA_c], axis=1), jnp.concatenate([vA, vA_c], axis=1))

    outB = _window_attention(_rope(qB, cos, sin), _rope(kB, cos, sin), vB, kB_c, vB_c, sink)

    y = jnp.concatenate([outA, outB], axis=-1) * jax.nn.silu(z)
    x = x + gate * _rmsnorm(y @ w_out, post_g)

    if need_ctx_out:
        qA_c, qB_c = _split_q(hc @ w_in[:, :Q_W])
        z_c = hc @ w_in[:, Q_W + KV_W:]
        oA_c = _ctx_attention(_rmsnorm(qA_c, q_norm), kA_c, vA_c)
        oB_c = _ctx_attention(qB_c, kB_c, vB_c, sink)
        yc = jnp.concatenate([oA_c, oB_c], axis=-1) * jax.nn.silu(z_c)
        ctx = ctx + gate_c * _rmsnorm(yc @ w_out, post_g)
    return x, ctx

def _multiscale_pool(u, pool_w, pool_scale):
    B, L, _ = u.shape
    uf = u.astype(jnp.float32)
    cs = jnp.concatenate([jnp.zeros_like(uf[:, :1]), lax.cumsum(uf, axis=1)], axis=1)
    t = jnp.arange(L)
    outs = []
    for g, w in enumerate(POOL_SIZES):
        lo = jnp.clip(t - w // 2, 0, L)
        hi = jnp.clip(t + w // 2, 0, L)
        csg = cs[..., g * POOL_GROUP:(g + 1) * POOL_GROUP]
        mean = (jnp.take(csg, hi, axis=1) - jnp.take(csg, lo, axis=1)) / (hi - lo).astype(jnp.float32)[:, None]
        outs.append(mean - uf[..., g * POOL_GROUP:(g + 1) * POOL_GROUP])
    pooled = jnp.stack(outs, axis=2).astype(u.dtype)
    mixed = jnp.einsum('blgc,gcd->blgd', pooled, pool_w).reshape(B, L, POOL_WIDTH)
    return mixed * pool_scale

def _pool_layer(x, ctx, c, c_ctx, mod_w, mod_b, pre_g, post_g, w_in, pool_w, pool_scale, w_out, need_ctx_out):
    shift, scale, gate = _modulation(c, mod_w, mod_b)
    h = _rmsnorm(x, pre_g) * (1 + scale) + shift
    proj = h @ w_in
    y = _multiscale_pool(proj[..., :POOL_WIDTH], pool_w, pool_scale) * jax.nn.silu(proj[..., POOL_WIDTH:])
    x = x + gate * _rmsnorm(y @ w_out, post_g)
    if need_ctx_out:
        shift_c, scale_c, gate_c = _modulation(c_ctx, mod_w, mod_b)
        hc = _rmsnorm(ctx, pre_g) * (1 + scale_c) + shift_c
        pc = hc @ w_in
        yc = _multiscale_pool(pc[..., :POOL_WIDTH], pool_w, pool_scale) * jax.nn.silu(pc[..., POOL_WIDTH:])
        ctx = ctx + gate_c * _rmsnorm(yc @ w_out, post_g)
    return x, ctx

def second_inputs(seed: int = 0) -> dict:
    key = jax.random.key(seed)
    ks = jax.random.split(key, 24)
    f32 = jnp.float32

    def nrm(k, shape, s):
        return jax.random.normal(k, shape, f32) * s

    return {
        'x': nrm(ks[0], (BATCH, SEQ, D_MODEL), 1.0),
        'c': nrm(ks[1], (BATCH, D_MODEL), 1.0),
        'ctx': nrm(ks[2], (BATCH, CTX_LEN, D_MODEL), 1.0),
        'c_ctx': nrm(ks[3], (D_MODEL,), 1.0),
        'ev_mod_w': nrm(ks[4], (N_EVEN, D_MODEL, 3 * D_MODEL), 0.5 * D_MODEL ** -0.5),
        'ev_mod_b': nrm(ks[5], (N_EVEN, 3 * D_MODEL), 0.02),
        'ev_pre_g': 1.0 + nrm(ks[6], (N_EVEN, D_MODEL), 0.05),
        'ev_post_g': 1.0 + nrm(ks[7], (N_EVEN, D_MODEL), 0.05),
        'ev_w_in': nrm(ks[8], (N_EVEN, D_MODEL, EVEN_IN), D_MODEL ** -0.5),
        'ev_q_norm': 1.0 + nrm(ks[9], (N_EVEN, HEAD_DIM), 0.05),
        'ev_k_norm': 1.0 + nrm(ks[10], (N_EVEN, HEAD_DIM), 0.05),
        'ev_sink': nrm(ks[11], (N_EVEN, N_HEADS_B), 0.5),
        'ev_w_out': nrm(ks[12], (N_EVEN, ATTN_WIDTH_2, D_MODEL), ATTN_WIDTH_2 ** -0.5),
        'od_mod_w': nrm(ks[13], (N_ODD, D_MODEL, 3 * D_MODEL), 0.5 * D_MODEL ** -0.5),
        'od_mod_b': nrm(ks[14], (N_ODD, 3 * D_MODEL), 0.02),
        'od_pre_g': 1.0 + nrm(ks[15], (N_ODD, D_MODEL), 0.05),
        'od_post_g': 1.0 + nrm(ks[16], (N_ODD, D_MODEL), 0.05),
        'od_w_in': nrm(ks[17], (N_ODD, D_MODEL, ODD_IN), D_MODEL ** -0.5),
        'od_pool_w': nrm(ks[18], (N_ODD, N_POOL_GROUPS, POOL_GROUP, POOL_GROUP), POOL_GROUP ** -0.5),
        'od_pool_scale': 1.0 + nrm(ks[19], (N_ODD, POOL_WIDTH), 0.1),
        'od_w_out': nrm(ks[20], (N_ODD, POOL_WIDTH, D_MODEL), POOL_WIDTH ** -0.5),
    }

def second_block(x, c, ctx, c_ctx, ev_mod_w, ev_mod_b, ev_pre_g, ev_post_g, ev_w_in, ev_q_norm, ev_k_norm, ev_sink, ev_w_out,
              od_mod_w, od_mod_b, od_pre_g, od_post_g, od_w_in, od_pool_w, od_pool_scale, od_w_out):
    ROWS = x.shape[1] // GRID_W
    cos, sin = _axial_rope(ROWS)
    for i in range(DEPTH_2):
        need_ctx_out = any(j % 2 == 0 for j in range(i + 1, DEPTH_2))
        if i % 2 == 0:
            e = i // 2
            x, ctx = _attention_layer(x, ctx, cos, sin, c, c_ctx, ev_mod_w[e], ev_mod_b[e], ev_pre_g[e], ev_post_g[e],
                                      ev_w_in[e], ev_q_norm[e], ev_k_norm[e], ev_sink[e], ev_w_out[e], need_ctx_out)
        else:
            o = i // 2
            x, ctx = _pool_layer(x, ctx, c, c_ctx, od_mod_w[o], od_mod_b[o], od_pre_g[o], od_post_g[o],
                                 od_w_in[o], od_pool_w[o], od_pool_scale[o], od_w_out[o], need_ctx_out)
    return x


def setup_inputs(seed=0):
    out = dict(first_inputs(seed))
    for name, value in second_inputs(seed + 1).items():
        if name != "x":
            out[name + "_2"] = value
    return out


def reference(
    x, g_mix_pre, w_in, b_glu, w_dw, b_dw, ln_conv_g, ln_conv_b, w_out, g_mix_post, g_ffn_pre,
    w_ff1, w_ff2, g_ffn_post, c_2, ctx_2, c_ctx_2, ev_mod_w_2, ev_mod_b_2, ev_pre_g_2,
    ev_post_g_2, ev_w_in_2, ev_q_norm_2, ev_k_norm_2, ev_sink_2, ev_w_out_2, od_mod_w_2,
    od_mod_b_2, od_pre_g_2, od_post_g_2, od_w_in_2, od_pool_w_2, od_pool_scale_2, od_w_out_2,
):
    x = first_block(
        x, g_mix_pre, w_in, b_glu, w_dw, b_dw, ln_conv_g, ln_conv_b, w_out, g_mix_post,
        g_ffn_pre, w_ff1, w_ff2, g_ffn_post,
    )
    return second_block(
        x, c_2, ctx_2, c_ctx_2, ev_mod_w_2, ev_mod_b_2, ev_pre_g_2, ev_post_g_2, ev_w_in_2,
        ev_q_norm_2, ev_k_norm_2, ev_sink_2, ev_w_out_2, od_mod_w_2, od_mod_b_2, od_pre_g_2,
        od_post_g_2, od_w_in_2, od_pool_w_2, od_pool_scale_2, od_w_out_2,
    )


_drawn_inputs = setup_inputs


def setup_inputs(seed=0):
    import zlib

    import numpy as np

    out = dict(_drawn_inputs(seed))
    spreads = {}
    factors = {'g_mix_pre': 2.945,
     'b_glu': 3.598,
     'ln_conv_g': 3.406,
     'ln_conv_b': 4.214,
     'g_mix_post': 3.649,
     'g_ffn_pre': 4.186,
     'g_ffn_post': 4.714,
     'ev_mod_b_2': 3.235,
     'ev_pre_g_2': 5.105,
     'ev_post_g_2': 22.478,
     'ev_q_norm_2': 8.0,
     'ev_k_norm_2': 8.0,
     'ev_sink_2': 8.0,
     'od_mod_b_2': 4.494,
     'od_pre_g_2': 4.745,
     'od_post_g_2': 23.053,
     'od_pool_scale_2': 3.255}
    for name, (base, spread) in spreads.items():
        noise = np.random.default_rng([zlib.crc32(name.encode()), seed]).standard_normal(out[name].shape)
        drawn = base * np.exp(spread * noise) if base else spread * noise
        out[name] = __import__('jax').numpy.asarray(drawn.astype(out[name].dtype))
    for name, factor in factors.items():
        out[name] = (out[name] * factor).astype(out[name].dtype)
    return out
```

```python
import math
from contextlib import ExitStack

import numpy as np

import concourse.bass as bass
import concourse.mybir as mybir

F32 = mybir.dt.float32
F32R = mybir.dt.float32r
ACT = mybir.ActivationFunctionType
ALU = mybir.AluOpType
AX = mybir.AxisListType

P = 128
T = 256
TT = T // P
D = 2048
KT = D // P
BW = 512
NBLK = D // BW
STEPS = 8
KPS = KT // STEPS
SLOTS = 4
FT = BW // P
HEADS = 8
HD = 128
CONV_TILES = 8
TAPS = 31
PAD = TAPS - 1
SCALE = HD ** -0.5
RMS_EPS = 1e-6
LN_EPS = 1e-5
POOL_PAD = 16
POOL_SIZES = (2, 4, 8, 16)
WINDOW = 128
GRID_W = 64
FF_GROUPS = 4
MH = D // 2

PRODUCTS = [("u", 4, 4), ("qk", 4, 4), ("v", 2, 2), ("out", 4, 4), ("ff", 8 * FF_GROUPS, 8 * FF_GROUPS),
            ("evq", 4, 4), ("evkv", 2, 4), ("evz", 4, 4), ("evo", 4, 4),
            ("odu", 4, 4), ("odg", 4, 4), ("pool", 1, 4), ("odo", 4, 4)]
BLOCK, ACC = {}, {}
_b = _a = 0
for _name, _nb, _na in PRODUCTS:
    BLOCK[_name], ACC[_name] = _b, _a
    _b, _a = _b + _nb, _a + _na
LAST_BLOCK = _b - 1

MOD_UNITS = [("ev_gate", 1), ("ev_shift", 2), ("ev_scale", 2), ("od_shift", 1), ("od_scale", 1), ("od_gate", 1)]
MOD_STEP0, MOD_LOAD0, MOD_END = {}, {}, {}
_n = _l = 0
for _name, _v in MOD_UNITS:
    MOD_STEP0[_name] = _n + 4
    MOD_LOAD0[_name] = _l
    _n += 4 + 2 * KT * _v
    _l += 2 * KT
    MOD_END[_name] = _n

COLS = [("g_mix_pre", 16), ("b_glu", 16), ("b_dw", 8), ("ln_g", 8), ("ln_b", 8), ("g_ffn_pre", 16),
        ("c", 16), ("c_ctx", 16), ("ev_mod_b", 48), ("ev_pre_g", 16), ("ev_post_g", 16),
        ("od_mod_b", 48), ("od_pre_g", 16), ("od_post_g", 16), ("pool_scale", 16), ("sink", 8),
        ("slope", 8), ("w_dw", CONV_TILES * TAPS)]
COL = {}
_c = 0
for _name, _n in COLS:
    COL[_name] = _c
    _c += _n
NCOLS = _c

R0, R1, R2, R3, SCRATCH = 0, 4096, 8192, 10240, 11008
HPAD = T + PAD
UPAD = T + 2 * POOL_PAD


def build_program(nc, io, out):
    weights = {n: io[n].rearrange("(t p) n -> p t n", p=P)
               for n in ("w_in", "w_out", "w_ff1", "w_ff2", "ev_w_in", "ev_w_out", "od_w_in", "od_w_out", "od_pool_w")}
    mod_w = {"ev": io["ev_mod_w"].rearrange("(t p) n -> p t n", p=P),
             "od": io["od_mod_w"].rearrange("(t p) n -> p t n", p=P)}
    tok = lambda ap: ap.rearrange("(t p) n -> p t n", p=P)

    with ExitStack() as ctx:
        def sb(name, shape, dt=F32):
            return ctx.enter_context(nc.sbuf_tensor(name, shape, dt))

        def sem(name):
            return ctx.enter_context(nc.semaphore(name))

        raw = sb("raw", [P, 4, 4, BW])
        w_hi = sb("w_hi", [P, SLOTS, KPS, BW], F32R)
        w_lo = sb("w_lo", [P, SLOTS, KPS, BW], F32R)
        mod_raw = sb("mod_raw", [P, 2, MH])
        mod_sum = sb("mod_sum", [P, 2, D])
        a_hi = sb("a_hi", [P, KT, T], F32R)
        a_lo = sb("a_lo", [P, KT, T], F32R)
        b_hi = sb("b_hi", [P, KT, T], F32R)
        b_lo = sb("b_lo", [P, KT, T], F32R)
        scratch = sb("scratch", [P, SCRATCH])
        cols = sb("cols", [P, NCOLS])
        ident = sb("ident", [P, P])
        ones = sb("ones", [P, P])
        qk_gain = sb("qk_gain", [P, 2, HD])
        table = sb("table", [P, 1024])
        silu_c = sb("silu_c", [P, 2, KT])
        neg_sink = sb("neg_sink", [P, HEADS])
        mod_cols = sb("mod_cols", [P, 8, KT])
        ssq_part = sb("ssq_part", [P, TT, NBLK])
        norm_s = sb("norm_s", [P, 8])
        head_s = sb("head_s", [P, 16])
        soft = sb("soft", [P, 2, 8])
        ln_rstd = sb("ln_rstd", [P, T])
        head_o = sb("head_o", [P, 2, T])
        EV_GATE, EV_SHIFT, EV_SHIFT_C, EV_SCALE, EV_SCALE_C, OD_SHIFT, OD_SCALE, OD_GATE = range(8)

        acc = [ctx.enter_context(nc.psum_tensor(f"acc{i}", [P, 1024], F32)) for i in range(2)]
        aux = ctx.enter_context(nc.psum_tensor("aux", [P, 4, 512], F32))
        h_dram = nc.dram_tensor("h_spill", (T, D), F32, kind="Internal").ap()

        def view(off, *shape):
            n = math.prod(shape)
            v = scratch[:, off:off + n]
            if len(shape) == 2:
                v = v.rearrange("p (a b) -> p a b", a=shape[0])
            elif len(shape) == 3:
                v = v.rearrange("p (a b c) -> p a b c", a=shape[0], b=shape[1])
            return v

        Y = view(R0, TT, D)
        X = view(R1, TT, D)
        grow = view(R2, D)
        junk = view(R3, 512).bitcast(mybir.dt.bfloat16).rearrange("p (t n) -> p t n", t=TT)
        qk_T = view(R0, 2 * HEADS, T)
        conv_in = view(R1, CONV_TILES, HPAD)
        v_tok1 = view(R1 + CONV_TILES * HPAD, TT, HEADS * HD)
        o = R1 + CONV_TILES * HPAD + TT * HEADS * HD
        sig = view(o, FT, T)
        prob1 = view(o, 2, TT, T)
        prob_T1 = view(o + 4 * T, TT, T)
        q_stage1 = view(o + 6 * T, 2, T)
        v_stage1 = view(o + 8 * T, 2, TT, HD)
        conv_y = mod_sum[:, 1, :].rearrange("p (c t) -> p c t", c=CONV_TILES)
        conv_sq = view(R1, CONV_TILES, T)
        ff_sum = Y
        relu = view(R2, FT, T)
        hid = view(R2 + FT * T, FT, T)
        q_T = view(R0, 16, T)
        k_T = view(R1, 4, 512)
        v_tok2 = view(R1 + 2048, 4, 512)
        q_sb = [view(R2 + 1024 * i, 1024) for i in range(2)]
        ctx_junk = mod_sum[:, 1, :].bitcast(mybir.dt.bfloat16).rearrange("p (t n) -> p t n", t=TT)
        rope_t = [mod_sum[:, 1, 1024 * i:1024 * (i + 1)] for i in range(2)]
        prob2 = mod_sum[:, 1, :].rearrange("p (b t k) -> p b t k", b=2, t=TT)
        prob_T2 = view(R2, 4, T)
        q_stage2 = view(R2 + 1024, 2, T)
        v_stage2 = view(R2 + 1536, 2, 4, HD)
        gated = view(R2, FT, T)
        mod_tmp = view(R2, 4, T)
        silu_g = view(R0, KT, T)
        u_pad = view(R2, FT, UPAD)
        win_a = view(R2 + FT * UPAD, FT, UPAD)
        win_b = mod_sum[:, 1, 0:FT * UPAD].rearrange("p (c t) -> p c t", c=FT)
        pooled = view(R0, FT, T)

        def col(name, i, n=1):
            c = COL[name]
            return cols[:, bass.ds(c + i, n)] if not isinstance(i, int) else cols[:, c + i:c + i + n]

        dist_neg = table[:, 0:512].rearrange("p (t k) -> p t k", t=TT)
        rope_cos = table[:, 0:256].rearrange("p (t d) -> p t d", t=TT)
        rope_sin = table[:, 256:512].rearrange("p (t d) -> p t d", t=TT)
        band = table[:, 512:1024].rearrange("p (t k) -> p t k", t=TT)
        inv_cnt = table[:, :].rearrange("p (g t) -> p g t", g=4)

        raw_in = [sem(f"raw_in{q}") for q in range(4)]
        hi_ready = sem("hi_ready")
        split_done = sem("split_done")
        step_done = sem("step_done")
        acc_free = sem("acc_free")
        mod_in = [sem(f"mod_in{i}") for i in range(2)]
        mod_acc = sem("mod_acc")
        mod_summed = sem("mod_summed")
        mod_cols_ready = sem("mod_cols_ready")
        const_in = sem("const_in")
        x_in = sem("x_in")
        grow_in = sem("grow_in")
        table_in = sem("table_in")
        h_out = sem("h_out")
        silu_ready = sem("silu_ready")
        dve_self = sem("dve_self")
        ssq_ready = sem("ssq_ready")
        var_ready = sem("var_ready")
        std_ready = sem("std_ready")
        h_ready = sem("h_ready")
        xn_ready = sem("xn_ready")
        tr_done = sem("tr_done")
        norm_hi = sem("norm_hi")
        norm_tmp = sem("norm_tmp")
        a_ready = sem("a_ready")
        pad_ready = sem("pad_ready")
        conv_tap = sem("conv_tap")
        conv_sq_ready = sem("conv_sq_ready")
        ln_sum = sem("ln_sum")
        ln_act = sem("ln_act")
        mix_hi = sem("mix_hi")
        mix_ready = sem("mix_ready")
        staged = sem("staged")
        scores = sem("scores")
        biased = sem("biased")
        head_max = sem("head_max")
        neg_max = sem("neg_max")
        exp_done = sem("exp_done")
        sum_ready = sem("sum_ready")
        inv_ready = sem("inv_ready")
        prob_ready = sem("prob_ready")
        prob_tr = sem("prob_tr")
        prob_T_ready = sem("prob_T_ready")
        pv_done = sem("pv_done")
        head_copied = sem("head_copied")
        head_out = sem("head_out")
        y_ready = sem("y_ready")
        hid_sq = sem("hid_sq")
        hid_hi = sem("hid_hi")
        hid_ready = sem("hid_ready")
        ff_zero = sem("ff_zero")
        q_sq = sem("q_sq")
        head_var = sem("head_var")
        head_std = sem("head_std")
        q_roped = sem("q_roped")
        q_tr = sem("q_tr")
        q_T_ready = sem("q_T_ready")
        z_mul = sem("z_mul")
        z_hi = sem("z_hi")
        z_ready = sem("z_ready")
        u_zero = sem("u_zero")
        u_pooled = sem("u_pooled")
        u_hi = sem("u_hi")
        u_ready = sem("u_ready")
        p_hi = sem("p_hi")
        p_ready = sem("p_ready")
        diag_ready = sem("diag_ready")
        row_sum = sem("row_sum")
        row_ready = sem("row_ready")
        out_done = sem("out_done")

        block = ctx.enter_context(nc.Block())

        HEAD1, HEAD2 = 0, HEADS

        @block.sync
        def _(sp):
            def load_block(b, w, row_tile, column):
                for q in range(4):
                    sp.wait_ge(split_done, 8 * b + 2 * q + 2)
                    sp.dma_start(raw[:, q], w[:, row_tile(4 * q), column]).then_inc(raw_in[q], 16)

            def rows(first=0):
                return lambda k: slice(first + k, first + k + 4)

            def load_mod(unit, layer, part, kt, l, vectors):
                for half in range(2):
                    sp.wait_ge(mod_acc, MOD_STEP0[unit] + vectors * (l + half) - (2 if vectors == 2 else 1))
                    sp.dma_start(mod_raw[:, half, :],
                                 mod_w[layer][:, kt, part * D + half * MH:part * D + (half + 1) * MH]
                                 ).then_inc(mod_in[half], 16)

            one = lambda i: bass.ds(i, 1)
            sp.dma_start(X, tok(io["x"])).then_inc(x_in, 16)
            sp.dma_start(ident[:], io["ident"]).then_inc(const_in, 16)
            sp.dma_start(cols[:], io["cols"]).then_inc(const_in, 16)
            sp.dma_start(qk_gain[:, 0, :], io["q_norm"].partition_broadcast(P)).then_inc(const_in, 16)
            sp.dma_start(qk_gain[:, 1, :], io["k_norm"].partition_broadcast(P)).then_inc(const_in, 16)
            sp.dma_start(table[:, 0:512], io["dist_neg"]).then_inc(table_in, 16)

            W = weights["w_in"]
            with sp.Fori(0, 2) as i:
                for par, c0 in ((0, 4096), (1, 3072)):
                    load_block(BLOCK["u"] + 2 * i + par, W, rows(), bass.ds(c0 + BW * i, BW))
                    for k in range(2):
                        kt = 2 * (2 * i + par) + k
                        load_mod("ev_gate", "ev", 2, one(kt), 2 * kt, 1)
            with sp.Fori(0, 4) as i:
                load_block(BLOCK["qk"] + i, W, rows(), bass.ds(BW * i, BW))
            with sp.Fori(0, 2) as i:
                load_block(BLOCK["v"] + i, W, rows(), bass.ds(D + BW * i, BW))
            W = weights["w_out"]

            def out_block(i):
                load_block(BLOCK["out"] + i, W, rows(), bass.ds(BW * i, BW))
                for k in range(2):
                    kt = 8 + 2 * i + k
                    load_mod("ev_gate", "ev", 2, one(kt), 2 * kt, 1)

            load_block(BLOCK["out"], W, rows(), slice(0, BW))
            sp.wait_ge(mix_ready, 16)
            sp.dma_start(X, tok(io["x"])).then_inc(x_in, 16)
            sp.dma_start(grow, io["g_mix_post"].partition_broadcast(P)).then_inc(grow_in, 16)
            for k in range(2):
                load_mod("ev_gate", "ev", 2, slice(8 + k, 9 + k), 2 * (8 + k), 1)
            with sp.Fori(1, 4) as i:
                out_block(i)
            for g0, unit, part in ((0, "ev_shift", 0), (2, "ev_scale", 1)):
                with sp.Fori(0, 2) as g:
                    for half, W in ((0, weights["w_ff1"]), (1, weights["w_ff2"])):
                        with sp.Fori(0, 4) as i:
                            b = BLOCK["ff"] + 8 * (g + g0) + 4 * half + i
                            if half == 0:
                                load_block(b, W, rows(), bass.ds(D * (g + g0) + BW * i, BW))
                            else:
                                load_block(b, W, lambda k: bass.ds(KT * (g + g0) + k, 4), bass.ds(BW * i, BW))
                            kt = 8 * g + 4 * half + i
                            load_mod(unit, "ev", part, one(kt), 2 * kt, 2)
            sp.wait_ge(hid_ready, 4 * FF_GROUPS)
            sp.dma_start(grow, io["g_ffn_post"].partition_broadcast(P)).then_inc(grow_in, 16)
            sp.dma_start(table[:], io["ev_table"]).then_inc(table_in, 16)
            W = weights["ev_w_in"]
            load_block(BLOCK["evq"], W, rows(), slice(0, BW))
            sp.wait_ge(h_ready, 4)
            sp.dma_start(tok(h_dram), X).then_inc(h_out, 16)
            sp.wait_ge(tr_done, 24)
            sp.dma_start(Y, tok(io["ctx"])).then_inc(x_in, 16)
            for k in range(2):
                load_mod("od_shift", "od", 0, slice(k, k + 1), 2 * k, 1)
            for b in range(1, 4):
                load_block(BLOCK["evq"] + b, W, rows(), slice(BW * b, BW * (b + 1)))
                for k in range(2 * b, 2 * b + 2):
                    load_mod("od_shift", "od", 0, slice(k, k + 1), 2 * k, 1)
            for b in range(2):
                load_block(BLOCK["evkv"] + b, W, rows(), slice(D + BW * b, D + BW * (b + 1)))
                for k in range(8 + 3 * b, 11 + 4 * b):
                    load_mod("od_shift", "od", 0, slice(k, k + 1), 2 * k, 1)
            load_block(BLOCK["evz"], W, rows(), slice(D + 1024, D + 1024 + BW))
            load_mod("od_shift", "od", 0, slice(KT - 1, KT), 2 * (KT - 1), 1)
            for k in range(2):
                load_mod("od_scale", "od", 1, slice(k, k + 1), 2 * k, 1)
            with sp.Fori(1, 4) as i:
                load_block(BLOCK["evz"] + i, W, rows(), bass.ds(D + 1024 + BW * i, BW))
                for k in range(2):
                    load_mod("od_scale", "od", 1, one(2 * i + k), 2 * (2 * i + k), 1)
            W = weights["ev_w_out"]
            load_block(BLOCK["evo"], W, rows(), slice(0, BW))
            sp.wait_ge(h_out, 16)
            sp.wait_ge(head_out, 2 + 16)
            sp.dma_start(X, tok(h_dram)).then_inc(x_in, 16)
            sp.dma_start(table[:], io["od_table"]).then_inc(table_in, 16)
            for k in range(2):
                load_mod("od_scale", "od", 1, slice(8 + k, 9 + k), 2 * (8 + k), 1)
            with sp.Fori(1, 4) as i:
                load_block(BLOCK["evo"] + i, W, rows(), bass.ds(BW * i, BW))
                for k in range(2):
                    load_mod("od_scale", "od", 1, one(8 + 2 * i + k), 2 * (8 + 2 * i + k), 1)
            W = weights["od_w_in"]
            with sp.Fori(0, 8) as i:
                load_block(BLOCK["odu"] + i, W, rows(), bass.ds(BW * i, BW))
                for k in range(2):
                    load_mod("od_gate", "od", 2, one(2 * i + k), 2 * (2 * i + k), 1)
            load_block(BLOCK["pool"], weights["od_pool_w"], rows(), slice(0, BW))
            with sp.Fori(0, 4) as i:
                load_block(BLOCK["odo"] + i, weights["od_w_out"], rows(), bass.ds(BW * i, BW))
            for tt in range(TT):
                sp.wait_ge(h_ready, 7 + tt)
                sp.dma_start(out[tt * P:(tt + 1) * P, :], X[:, tt, :]).then_inc(out_done, 16)
            sp.wait_ge(out_done, 32)

        @block.gpsimd
        def _(pool):
            nc.gpsimd.memset(ones[:], 1.0).then_inc(pad_ready, 1)

            def stage(n, q_src, q_stage, v_src, v_stage, par):
                pool.wait_ge(pv_done, n + 1)
                nc.gpsimd.tensor_copy(q_stage[:, par, :], q_src)
                nc.gpsimd.tensor_copy(v_stage[:, par], v_src).then_inc(staged, 1)

            pool.wait_ge(acc_free, 2 + ACC["out"])
            with pool.Fori(0, 2) as i:
                for j in range(4):
                    h = 4 * i + j
                    stage(HEAD1 + h, qk_T[:, bass.ds(h, 1), :].rearrange("p a t -> p (a t)"), q_stage1,
                          v_tok1[:, :, bass.ds(h * HD, HD)], v_stage1, j % 2)
            pool.wait_ge(q_T_ready, 6)
            with pool.Fori(0, 4) as i:
                for j in range(4):
                    h = 4 * i + j
                    stage(HEAD2 + h, q_T[:, bass.ds(h, 1), :].rearrange("p a t -> p (a t)"), q_stage2,
                          v_tok2[:, :, bass.ds(i * HD, HD)], v_stage2, j % 2)

        @block.scalar
        def _(act):
            def split_hi(b, steps):
                for s in steps:
                    act.wait_ge(step_done, 8 * b + s + 1)
                    if s % 2 == 0:
                        act.wait_ge(raw_in[s // 2], 16 * (b + 1))
                    nc.scalar.activation(w_hi[:, s % SLOTS], raw[:, s // 2, KPS * (s % 2):KPS * (s % 2) + KPS, :],
                                         ACT.Copy).then_inc(hi_ready, 1)

            def run_ahead(b):
                split_hi(b, range(4, 8))
                split_hi(b + 1, range(4))

            def block_done(b):
                act.wait_ge(step_done, 4 + 8 * (b + 1))

            def sums_of_squares(src, product):
                for tt in range(TT):
                    nc.scalar.activation(product(tt), src(tt), ACT.Square, accum_out=norm_s[:, tt:tt + 1]).then_inc(ssq_ready, 1)

            def root(n):
                act.wait_ge(var_ready, n + 1)
                nc.scalar.activation(norm_s[:, 4:6], norm_s[:, 2:4], ACT.Sqrt).then_inc(std_ready, 1)

            def norm_round(m, dst):
                for k in range(KT):
                    act.wait_ge(norm_tmp, KT * m + k + 1)
                    nc.scalar.activation(dst[:, k, :], mod_tmp[:, k % 4, :], ACT.Copy).then_inc(norm_hi, 1)

            def squares_out(i, par, src):
                for tt in range(TT):
                    c = ssq_part[:, tt, bass.ds(i, 1)] if not isinstance(i, int) else ssq_part[:, tt, i:i + 1]
                    last = nc.scalar.activation(junk[:, tt, :], src(tt), ACT.Square, accum_out=c)
                return last

            def row_block(name, i, par):
                b = BLOCK[name] + i
                block_done(b)
                act.wait_ge(acc_free, 2 + ACC[name] + i)
                dst = Y[:, :, bass.ds(BW * i, BW)] if not isinstance(i, int) else Y[:, :, BW * i:BW * (i + 1)]
                nc.scalar.activation(dst, acc[par][:, :].rearrange("p (t n) -> p t n", t=TT), ACT.Copy).then_inc(y_ready, 1)
                squares_out(i, par, lambda tt: acc[par][:, BW * tt:BW * (tt + 1)]).then_inc(acc_free, 1)

            def attention(n0, iters, keys, prob, prob_T, emit, sink_of):
                kt = keys // P
                with act.Fori(0, iters) as i:
                    for j in range(4):
                        n = n0 + 4 * i + j
                        p = j % 2
                        act.wait_ge(neg_max, n + 1)
                        for tt in range(TT):
                            e = nc.scalar.activation(prob[:, p, tt, :], acc[p][:, keys * tt:keys * (tt + 1)], ACT.Exp,
                                                     bias=soft[:, p, 2 + tt:3 + tt], scale=SCALE,
                                                     accum_out=soft[:, p, 4 + tt:5 + tt])
                        if sink_of:
                            e = nc.scalar.activation(soft[:, p, 6:8], soft[:, p, 2:4], ACT.Exp, bias=sink_of(i, j))
                        e.then_inc(exp_done, 1)
                        act.wait_ge(prob_tr, n + 1)
                        nc.scalar.activation(prob_T, aux[:, 0:kt // 2, :].rearrange("p a (k t) -> p (a k) t", t=T),
                                             ACT.Copy).then_inc(prob_T_ready, 1)
                        emit(n, 4 * i + j, p)

            act.wait_ge(const_in, 64)
            nc.scalar.activation(silu_c[:].rearrange("p a k -> p (a k)"), col("c", 0, 2 * KT), ACT.Silu).then_inc(silu_ready, 1)
            act.wait_ge(x_in, 16)
            sums_of_squares(lambda tt: X[:, tt, :], lambda tt: Y[:, tt, :])
            split_hi(0, range(4))
            root(0)
            norm_round(0, a_hi)
            with act.Fori(0, 2) as i:
                b = BLOCK["u"] + 2 * i
                run_ahead(b)
                block_done(b)
                act.wait_ge(acc_free, 2 + 2 * i)
                for f in range(FT):
                    e = nc.scalar.activation(sig[:, f, :], acc[0][:, T * f:T * (f + 1)], ACT.Sigmoid,
                                             bias=col("b_glu", 8 + 4 * i + f))
                e.then_inc(acc_free, 1)
                run_ahead(b + 1)
            with act.Fori(0, 2) as i:
                for par in range(2):
                    b = BLOCK["qk"] + 2 * i + par
                    run_ahead(b)
                    block_done(b)
                    nc.scalar.activation(qk_T[:, bass.ds(8 * i + 4 * par, FT), :],
                                         acc[par][:, :].rearrange("p (f t) -> p f t", f=FT), ACT.Copy).then_inc(acc_free, 1)
            for par in range(2):
                b = BLOCK["v"] + par
                run_ahead(b)
                block_done(b)
                nc.scalar.activation(v_tok1[:, :, BW * par:BW * (par + 1)],
                                     acc[par][:, :].rearrange("p (t n) -> p t n", t=TT), ACT.Copy).then_inc(acc_free, 1)
            act.wait_ge(ln_act, 1)
            nc.scalar.activation(conv_sq, conv_y, ACT.Square).then_inc(conv_sq_ready, 1)
            act.wait_ge(ln_act, 2)
            nc.scalar.activation(ln_rstd[:], ln_rstd[:], ACT.Sqrt).then_inc(conv_sq_ready, 1)
            act.wait_ge(ln_act, 3)
            for k in range(CONV_TILES):
                nc.scalar.activation(conv_sq[:, k, :], conv_y[:, k, :], ACT.Silu, bias=col("ln_b", k),
                                     scale=col("ln_g", k)).then_inc(conv_sq_ready, 1)
            for k in range(CONV_TILES):
                act.wait_ge(conv_sq_ready, 3 + k)
                nc.scalar.activation(b_hi[:, HEADS + k, :], conv_sq[:, k, :], ACT.Copy).then_inc(mix_hi, 1)

            def emit1(n, h, p):
                act.wait_ge(pv_done, n + 3)
                nc.scalar.activation(head_o[:, p, :], aux[:, 2 + p, 0:T], ACT.Copy).then_inc(head_copied, 1)
                act.wait_ge(head_copied, n + 1)
                nc.scalar.activation(b_hi[:, bass.ds(h, 1), :], head_o[:, p:p + 1, :], ACT.Copy).then_inc(mix_hi, 1)

            attention(HEAD1, 2, T, prob1, prob_T1, emit1, None)
            with act.Fori(0, 2) as i:
                for par in range(2):
                    run_ahead(BLOCK["out"] + 2 * i + par)
                    row_block("out", 2 * i + par, par)

            def post_then_norm(post, pre):
                root(post)
                for tt in range(TT):
                    act.wait_ge(h_ready, 2 * ((post + 1) // 2) - 1 + tt)
                    nc.scalar.activation(Y[:, tt, :], X[:, tt, :], ACT.Square,
                                         accum_out=norm_s[:, tt:tt + 1]).then_inc(ssq_ready, 1)
                root(pre)

            post_then_norm(1, 2)
            norm_round(1, a_hi)
            for g0 in (0, 2):
                with act.Fori(0, 2) as g:
                    with act.Fori(0, 2) as i:
                        for par in range(2):
                            bi = 2 * i + par
                            b = BLOCK["ff"] + 8 * (g + g0) + bi
                            m = 4 * (g + g0) + bi
                            run_ahead(b)
                            block_done(b)
                            nc.scalar.activation(relu, acc[par][:, :].rearrange("p (f t) -> p f t", f=FT),
                                                 ACT.Relu).then_inc(acc_free, 1)
                            act.wait_ge(hid_sq, m + 1)
                            nc.scalar.activation(b_hi[:, bass.ds(4 * bi, FT), :], hid, ACT.Copy).then_inc(hid_hi, 1)
                    with act.Fori(0, 2) as i:
                        for par in range(2):
                            bi = 2 * i + par
                            b = BLOCK["ff"] + 8 * (g + g0) + 4 + bi
                            run_ahead(b)
                            act.wait_ge(acc_free, 2 + ACC["ff"] + 8 * (g + g0) + 4 + bi + 1)
                            act.wait_ge(y_ready, NBLK + 4 * (g + g0) + bi)
                            squares_out(bi, par, lambda tt: ff_sum[:, tt, bass.ds(BW * bi, BW)]).then_inc(y_ready, 1)
            post_then_norm(3, 4)
            norm_round(2, a_hi)
            act.wait_ge(x_in, 48)
            for tt in range(TT):
                nc.scalar.activation(ctx_junk[:, tt, :], Y[:, tt, :], ACT.Square,
                                     accum_out=norm_s[:, tt:tt + 1]).then_inc(ssq_ready, 1)
            root(5)
            norm_round(3, b_hi)

            def q_block(b, par, n, heads_normed):
                block_done(b)
                nc.scalar.activation(q_sb[n % 2], acc[par][:, :], ACT.Copy).then_inc(acc_free, 1)

            def head_norm(n, src, m):
                act.wait_ge(acc_free, 2 + ACC["evq"] + (m + 1 if m < 2 else 6))
                if m:
                    act.wait_ge(q_roped, 1 if m == 1 else 4)
                nc.scalar.activation(rope_t[0], src, ACT.Square).then_inc(q_sq, 1)
                act.wait_ge(head_var, m + 1)
                nc.scalar.activation(head_s[:, 8:16], head_s[:, 0:8], ACT.Sqrt).then_inc(head_std, 1)

            def q_out(n):
                act.wait_ge(q_tr, n + 1)
                dst = (q_T[:, FT * n:FT * (n + 1), :] if n < 4 else k_T[:, 2 * (n - 4):2 * (n - 4) + 2, :])
                nc.scalar.activation(dst, aux[:, 0:2, :] if n >= 4 else
                                     aux[:, 0:2, :].rearrange("p a (h t) -> p (a h) t", t=T), ACT.Copy).then_inc(q_T_ready, 1)

            for n in range(4):
                b = BLOCK["evq"] + n
                run_ahead(b)
                q_block(b, n % 2, n, n < 2)
                if n < 2:
                    head_norm(n, q_sb[n % 2], n)
                if n >= 1:
                    q_out(n - 1)
            for m in range(2):
                n = 4 + m
                b = BLOCK["evkv"] + m
                run_ahead(b)
                block_done(b)
                kv = q_sb[n % 2].rearrange("p (t n) -> p t n", t=4)
                for side in range(2):
                    a4 = acc[side][:, :].rearrange("p (t n) -> p t n", t=TT)
                    nc.scalar.activation(kv[:, 2 * side:2 * side + 2, :], a4[:, :, 0:256], ACT.Copy)
                    nc.scalar.activation(v_tok2[:, 2 * side:2 * side + 2, 256 * m:256 * (m + 1)], a4[:, :, 256:512],
                                         ACT.Copy).then_inc(acc_free, 1)
                if m == 0:
                    head_norm(n, q_sb[n % 2], 2)
                q_out(n - 1)
            q_out(5)

            def emit2(n, h, p):
                act.wait_ge(pv_done, n + 3)
                nc.scalar.activation(q_T[:, bass.ds(h, 1), :], aux[:, 2 + p, 0:T].rearrange("p (a t) -> p a t", a=1),
                                     ACT.Copy).then_inc(head_out, 1)

            attention(HEAD2, 2, 512, prob2, prob_T2, emit2, None)
            attention(HEAD2 + 8, 2, 512, prob2, prob_T2, lambda n, h, p: emit2(n, 8 + h, p),
                      lambda i, j: col("sink", 4 * i + j))
            with act.Fori(0, 2) as i:
                for par in range(2):
                    bi = 2 * i + par
                    b = BLOCK["evz"] + bi
                    run_ahead(b)
                    block_done(b)
                    nc.scalar.activation(gated, acc[par][:, :].rearrange("p (f t) -> p f t", f=FT), ACT.Silu).then_inc(acc_free, 1)
                    act.wait_ge(z_mul, bi + 1)
                    nc.scalar.activation(b_hi[:, bass.ds(4 * bi, FT), :], gated, ACT.Copy).then_inc(z_hi, 1)

            def gate_row(g):
                for j in range(4):
                    act.wait_ge(row_sum, 4 * g + j + 1)
                    nc.scalar.activation(grow[:, BW * j:BW * (j + 1)], aux[:, j, :], ACT.Copy).then_inc(row_ready, 1)

            gate_row(0)
            with act.Fori(0, 2) as i:
                for par in range(2):
                    run_ahead(BLOCK["evo"] + 2 * i + par)
                    row_block("evo", 2 * i + par, par)
            root(6)
            for tt in range(TT):
                act.wait_ge(h_ready, 5 + tt)
                nc.scalar.activation(Y[:, tt, :], X[:, tt, :], ACT.Square,
                                     accum_out=norm_s[:, tt:tt + 1]).then_inc(ssq_ready, 1)
            root(7)
            norm_round(4, a_hi)
            for g in range(4):
                b = BLOCK["odu"] + g
                run_ahead(b)
                block_done(b)
                act.wait_ge(u_zero, 1)
                if g:
                    act.wait_ge(u_pooled, g)
                nc.scalar.activation(u_pad[:, :, POOL_PAD:POOL_PAD + T],
                                     acc[g % 2][:, :].rearrange("p (f t) -> p f t", f=FT), ACT.Copy).then_inc(acc_free, 1)
                act.wait_ge(u_pooled, g + 1)
                nc.scalar.activation(b_hi[:, FT * g:FT * (g + 1), :], pooled, ACT.Copy).then_inc(u_hi, 1)
            with act.Fori(0, 2) as i:
                for par in range(2):
                    bi = 2 * i + par
                    b = BLOCK["odg"] + bi
                    run_ahead(b)
                    block_done(b)
                    nc.scalar.activation(silu_g[:, bass.ds(4 * bi, FT), :], acc[par][:, :].rearrange("p (f t) -> p f t", f=FT),
                                         ACT.Silu).then_inc(acc_free, 1)
            b = BLOCK["pool"]
            for g in range(4):
                split_hi(b + (g >= 2), range(4 + 2 * g, 6 + 2 * g) if g < 2 else range(2 * g - 4, 2 * g - 2))
                act.wait_ge(acc_free, 2 + ACC["pool"] + g + 1)
                nc.scalar.activation(a_hi[:, FT * g:FT * (g + 1), :], gated, ACT.Copy).then_inc(p_hi, 1)
            gate_row(1)
            for n in range(4):
                b = BLOCK["odo"] + n
                split_hi(b, range(4, 8))
                if b < LAST_BLOCK:
                    split_hi(b + 1, range(4))
                row_block("odo", n, n % 2)
            root(8)

        @block.vector
        def _(dve):
            chain = [0]

            def link(ins):
                chain[0] += 1
                ins.then_inc(dve_self, 1)
                dve.wait_ge(dve_self, chain[0])

            def split_lo(b, steps):
                for s in steps:
                    dve.wait_ge(hi_ready, 8 * b + s + 1)
                    nc.vector.tensor_tensor(w_lo[:, s % SLOTS], raw[:, s // 2, KPS * (s % 2):KPS * (s % 2) + KPS, :],
                                            w_hi[:, s % SLOTS].bitcast(F32), ALU.subtract).then_inc(split_done, 1)

            def run_ahead(b, between=None):
                for m in range(4):
                    split_lo(b + (m >= 2), (4, 5) if m == 0 else (6, 7) if m == 1 else (0, 1) if m == 2 else (2, 3))
                    if between:
                        between(m)

            def block_done(b):
                dve.wait_ge(step_done, 4 + 8 * (b + 1))

            def mod_step(unit, layer_vecs, kt, half, v, n, back, load):
                dve.wait_ge(mod_in[half], 16 * (load + 1))
                dve.wait_ge(mod_acc, n + 1 - back)
                c = silu_c[:, layer_vecs[v], bass.ds(kt, 1)] if not isinstance(kt, int) else silu_c[:, layer_vecs[v], kt:kt + 1]
                s = mod_sum[:, v, MH * half:MH * (half + 1)]
                nc.vector.scalar_tensor_tensor(s, mod_raw[:, half, :], c, s, ALU.mult, ALU.add).then_inc(mod_acc, 1)

            def single(unit, kt0):
                base = MOD_LOAD0[unit] // 2

                def go(m):
                    kt = kt0 + m // 2
                    mod_step(unit, (0,), kt, m % 2, 0, MOD_STEP0[unit] + 2 * kt + m % 2, 2, base + kt)
                return go

            def both(unit, kt):
                base = MOD_LOAD0[unit] // 2

                def go(m):
                    mod_step(unit, (0, 1), kt, m // 2, m % 2, MOD_STEP0[unit] + 4 * kt + m, 4, base + kt)
                return go

            def mod_zero(what):
                nc.vector.memset(what, 0.0).then_inc(mod_acc, 4)

            def mod_out(u, biases):
                dve.wait_ge(mod_summed, u + 1)
                for v, (dst, bias) in enumerate(biases):
                    e = nc.vector.tensor_tensor(mod_cols[:, dst, :], aux[:, 3, KT * v:KT * (v + 1)], bias, ALU.add)
                e.then_inc(mod_cols_ready, 1)
                dve.wait_ge(mod_cols_ready, u + 1)

            def mean_eps(n):
                nc.vector.tensor_scalar(norm_s[:, 2:4], norm_s[:, 0:2], 1.0 / D, RMS_EPS, ALU.mult, ALU.add).then_inc(var_ready, 1)
                dve.wait_ge(std_ready, n + 1)
                link(nc.vector.reciprocal(norm_s[:, 6:8], norm_s[:, 4:6]))

            def normed_rows(src):
                for tt in range(TT):
                    nc.vector.tensor_scalar(Y[:, tt, :], src[:, tt, :], norm_s[:, 6 + tt:7 + tt], None,
                                            ALU.mult).then_inc(xn_ready, 1)

            def norm_split(m, scale, shift, hi, lo):
                def modulate(k):
                    if k % 2 == 0:
                        dve.wait_ge(tr_done, KT // 2 * m + k // 2 + 1)
                    if m or k > 3:
                        dve.wait_ge(a_ready, KT * m + k - 3)
                    ps = aux[:, (k // 2) % 4, T * (k % 2):T * (k % 2) + T]
                    if shift is None:
                        e = nc.vector.tensor_scalar(mod_tmp[:, k % 4, :], ps, scale[:, k:k + 1], None, ALU.mult)
                    else:
                        e = nc.vector.tensor_scalar(mod_tmp[:, k % 4, :], ps, scale[:, k:k + 1], shift[:, k:k + 1],
                                                    ALU.mult, ALU.add)
                    e.then_inc(norm_tmp, 1)

                def split(k):
                    dve.wait_ge(norm_hi, KT * m + k + 1)
                    nc.vector.tensor_tensor(lo[:, k, :], mod_tmp[:, k % 4, :], hi[:, k, :].bitcast(F32),
                                            ALU.subtract).then_inc(a_ready, 1)
                for k in range(KT):
                    modulate(k)
                    if k >= 2:
                        split(k - 2)
                split(KT - 2)
                split(KT - 1)

            def attention(n0, iters, keys, prob, bias, emit, sink_of):
                with dve.Fori(0, iters) as i:
                    for j in range(4):
                        n = n0 + 4 * i + j
                        p = j % 2
                        s3 = acc[p][:, 0:TT * keys].rearrange("p (t k) -> p t k", t=TT)
                        dve.wait_ge(scores, n + 1)
                        if bias:
                            bias(s3, 4 * i + j).then_inc(biased, 1)
                            dve.wait_ge(biased, n + 1 - BIAS_SKIP.get(n0, 0))
                        nc.vector.tensor_reduce(soft[:, p, 0:2], s3, AX.X, ALU.max).then_inc(head_max, 1)
                        dve.wait_ge(head_max, n + 1)
                        if sink_of:
                            nc.vector.tensor_scalar(soft[:, p, 2:4], soft[:, p, 0:2], -SCALE, sink_of(i, j),
                                                    ALU.mult, ALU.min).then_inc(neg_max, 1)
                        else:
                            nc.vector.tensor_scalar(soft[:, p, 2:4], soft[:, p, 0:2], -SCALE, None,
                                                    ALU.mult).then_inc(neg_max, 1)
                        dve.wait_ge(exp_done, n + 1)
                        if sink_of:
                            nc.vector.tensor_tensor(soft[:, p, 4:6], soft[:, p, 4:6], soft[:, p, 6:8], ALU.add).then_inc(sum_ready, 1)
                            dve.wait_ge(sum_ready, 4 * i + j + 1)
                        nc.vector.reciprocal(soft[:, p, 0:2], soft[:, p, 4:6]).then_inc(inv_ready, 1)
                        dve.wait_ge(inv_ready, n + 1)
                        for tt in range(TT):
                            nc.vector.tensor_scalar(prob[:, p, tt, :], prob[:, p, tt, :], soft[:, p, tt:tt + 1], None,
                                                    ALU.mult).then_inc(prob_ready, 1)
                        if emit:
                            emit(n, 4 * i + j, p)

            BIAS_SKIP = {HEAD2 + 8: HEADS}

            dve.sem_inc(split_done, 8)
            dve.sem_inc(acc_free, 2)
            dve.sem_inc(head_out, 2)
            mod_zero(mod_sum[:, 0, :])
            dve.wait_ge(ssq_ready, 2)
            mean_eps(0)
            normed_rows(X)
            split_lo(0, range(4))
            norm_split(0, col("g_mix_pre", 0, KT), None, a_hi, a_lo)
            dve.wait_ge(xn_ready, 2)
            link(nc.vector.memset(conv_in, 0.0))
            nc.vector.tensor_scalar(neg_sink[:], col("sink", 0, HEADS), -1.0, None, ALU.mult)
            dve.wait_ge(silu_ready, 1)
            with dve.Fori(0, 2) as i:
                b = BLOCK["u"] + 2 * i
                run_ahead(b, single("ev_gate", 4 * i))
                run_ahead(b + 1, single("ev_gate", 4 * i + 2))
                block_done(b + 1)
                dve.wait_ge(acc_free, 2 + ACC["u"] + 2 * i + 1)
                for f in range(FT):
                    e = nc.vector.scalar_tensor_tensor(
                        conv_in[:, bass.ds(4 * i + f, 1), PAD:HPAD].rearrange("p a t -> p (a t)"),
                        acc[1][:, T * f:T * (f + 1)], col("b_glu", 4 * i + f), sig[:, f, :], ALU.add, ALU.mult)
                e.then_inc(acc_free, 1)

            def conv_pair(pair, taps, n0):
                for t in taps:
                    for c in range(2):
                        ct = 2 * pair + c
                        dyn = not isinstance(pair, int)
                        src = (conv_in[:, bass.ds(ct, 1), t:t + T].rearrange("p a t -> p (a t)") if dyn
                               else conv_in[:, ct, t:t + T])
                        y = (conv_y[:, bass.ds(ct, 1), :].rearrange("p a t -> p (a t)") if dyn else conv_y[:, ct, :])
                        w = col("w_dw", TAPS * ct + t)
                        if t == 0:
                            e = nc.vector.tensor_scalar(y, src, w, col("b_dw", ct), ALU.mult, ALU.add)
                        else:
                            dve.wait_ge(conv_tap, n0 + 2 * t + c - 1)
                            e = nc.vector.scalar_tensor_tensor(y, src, w, y, ALU.mult, ALU.add)
                        e.then_inc(conv_tap, 1)

            CONV0 = 0
            dve.wait_ge(acc_free, 2 + ACC["qk"])
            with dve.Fori(0, 2) as i:
                for par in range(2):
                    run_ahead(BLOCK["qk"] + 2 * i + par,
                              lambda m: conv_pair(i, range(16 * par + 4 * m, min(16 * par + 4 * m + 4, TAPS)), CONV0 + 62 * i))
            for par in range(2):
                run_ahead(BLOCK["v"] + par,
                          lambda m: conv_pair(2, range(16 * par + 4 * m, min(16 * par + 4 * m + 4, TAPS)), CONV0 + 124))
            conv_pair(3, range(TAPS), CONV0 + 186)
            dve.wait_ge(conv_tap, CONV0 + 248)
            dve.wait_ge(ln_sum, 1)
            mean = aux[:, 0, 0:T]
            link(nc.vector.tensor_scalar(ln_rstd[:], mean, 1.0 / 1024, None, ALU.mult))
            nc.vector.tensor_tensor(conv_y, conv_y, ln_rstd[:].unsqueeze(1).to_broadcast([P, CONV_TILES, T]),
                                    ALU.subtract).then_inc(ln_act, 1)
            dve.wait_ge(ln_act, 1)
            dve.wait_ge(ln_sum, 2)
            nc.vector.tensor_scalar(ln_rstd[:], aux[:, 1, 0:T], 1.0 / 1024, LN_EPS, ALU.mult, ALU.add).then_inc(ln_act, 1)
            dve.wait_ge(conv_sq_ready, 2)
            link(nc.vector.reciprocal(ln_rstd[:], ln_rstd[:]))
            nc.vector.tensor_tensor(conv_y, conv_y, ln_rstd[:].unsqueeze(1).to_broadcast([P, CONV_TILES, T]),
                                    ALU.mult).then_inc(ln_act, 1)
            for k in range(CONV_TILES):
                dve.wait_ge(mix_hi, k + 1)
                nc.vector.tensor_tensor(b_lo[:, HEADS + k, :], conv_sq[:, k, :], b_hi[:, HEADS + k, :].bitcast(F32),
                                        ALU.subtract).then_inc(mix_ready, 1)
            dve.wait_ge(table_in, 16)

            def alibi(s3, h):
                return nc.vector.scalar_tensor_tensor(s3, dist_neg, col("slope", h), s3, ALU.mult, ALU.add)

            def emit1(n, h, p):
                dve.wait_ge(mix_hi, CONV_TILES + h + 1)
                nc.vector.tensor_tensor(b_lo[:, bass.ds(h, 1), :], head_o[:, p:p + 1, :],
                                        b_hi[:, bass.ds(h, 1), :].bitcast(F32), ALU.subtract).then_inc(mix_ready, 1)

            attention(HEAD1, 2, T, prob1, alibi, emit1, None)
            with dve.Fori(0, 2) as i:
                for par in range(2):
                    bi = 2 * i + par
                    run_ahead(BLOCK["out"] + bi, single("ev_gate", 8 + 2 * bi))

            def post_norm(n, ysq, xin, gin, gsem):
                dve.wait_ge(acc_free, ysq) if n != 3 else dve.wait_ge(y_ready, ysq)
                link(nc.vector.tensor_reduce(norm_s[:, 0:2], ssq_part[:], AX.X, ALU.add))
                mean_eps(n)
                if xin:
                    dve.wait_ge(x_in, xin)
                dve.wait_ge(gsem, gin)
                for tt in range(TT):
                    link(nc.vector.scalar_tensor_tensor(Y[:, tt, :], Y[:, tt, :], norm_s[:, 6 + tt:7 + tt], grow,
                                                        ALU.mult, ALU.mult))
                    nc.vector.tensor_tensor(X[:, tt, :], X[:, tt, :], Y[:, tt, :], ALU.add).then_inc(h_ready, 1)

            post_norm(1, 2 + ACC["ff"], 32, 16, grow_in)
            dve.wait_ge(ssq_ready, 4)
            mean_eps(2)
            normed_rows(X)
            norm_split(1, col("g_ffn_pre", 0, KT), None, a_hi, a_lo)
            mod_out(0, [(EV_GATE, col("ev_mod_b", 32, KT))])
            nc.vector.tensor_tensor(mod_cols[:, EV_GATE, :], mod_cols[:, EV_GATE, :], col("ev_post_g", 0, KT),
                                    ALU.mult)
            dve.wait_ge(tr_done, 16)
            nc.vector.memset(ff_sum, 0.0).then_inc(ff_zero, 1)
            for g0, unit, u, dsts in ((0, "ev_shift", 1, (EV_SHIFT, EV_SHIFT_C)), (2, "ev_scale", 2, (EV_SCALE, EV_SCALE_C))):
                mod_zero(mod_sum[:])
                with dve.Fori(0, 2) as g:
                    with dve.Fori(0, 2) as i:
                        for par in range(2):
                            bi = 2 * i + par
                            b = BLOCK["ff"] + 8 * (g + g0) + bi
                            m = 4 * (g + g0) + bi
                            run_ahead(b, both(unit, 8 * g + bi))
                            dve.wait_ge(acc_free, 2 + ACC["ff"] + 8 * (g + g0) + bi + 1)
                            nc.vector.tensor_tensor(hid, relu, relu, ALU.mult).then_inc(hid_sq, 1)
                            dve.wait_ge(hid_hi, m + 1)
                            nc.vector.tensor_tensor(b_lo[:, bass.ds(4 * bi, FT), :], hid,
                                                    b_hi[:, bass.ds(4 * bi, FT), :].bitcast(F32), ALU.subtract).then_inc(hid_ready, 1)
                    with dve.Fori(0, 2) as i:
                        for par in range(2):
                            bi = 2 * i + par
                            b = BLOCK["ff"] + 8 * (g + g0) + 4 + bi
                            run_ahead(b, both(unit, 8 * g + 4 + bi))
                            block_done(b)
                            dve.wait_ge(ff_zero, 1)
                            dve.wait_ge(acc_free, 2 + ACC["ff"] + 8 * (g + g0))
                            s = ff_sum[:, :, bass.ds(BW * bi, BW)]
                            nc.vector.tensor_tensor(s, s, acc[par][:, :].rearrange("p (t n) -> p t n", t=TT),
                                                    ALU.add).then_inc(acc_free, 1)
                part = 16 * (u - 1)
                mod_out(u, [(d, col("ev_mod_b", part, KT)) for d in dsts])
                if u == 2:
                    for d in dsts:
                        link(nc.vector.scalar_tensor_tensor(mod_cols[:, d, :], mod_cols[:, d, :], 1.0, col("ev_pre_g", 0, KT),
                                                            ALU.add, ALU.mult))
            mod_zero(mod_sum[:, 0, :])
            post_norm(3, 4 * FF_GROUPS + 4, 0, 32, grow_in)
            dve.wait_ge(ssq_ready, 6)
            mean_eps(4)
            normed_rows(X)
            norm_split(2, mod_cols[:, EV_SCALE, :], mod_cols[:, EV_SHIFT, :], a_hi, a_lo)
            dve.wait_ge(ssq_ready, 8)
            mean_eps(5)
            normed_rows(Y)
            norm_split(3, mod_cols[:, EV_SCALE_C, :], mod_cols[:, EV_SHIFT_C, :], b_hi, b_lo)
            dve.wait_ge(table_in, 32)
            dve.wait_ge(a_ready, 4 * KT)

            def head_norm(m, src, gain):
                dve.wait_ge(q_sq, m + 1)
                link(nc.vector.tensor_reduce(head_s[:, 0:8], rope_t[0].rearrange("p (h d) -> p h d", h=8), AX.X, ALU.add))
                nc.vector.tensor_scalar(head_s[:, 0:8], head_s[:, 0:8], 1.0 / HD, RMS_EPS, ALU.mult, ALU.add).then_inc(head_var, 1)
                dve.wait_ge(head_std, m + 1)
                link(nc.vector.reciprocal(head_s[:, 8:16], head_s[:, 8:16]))
                link(nc.vector.tensor_tensor(src, src, head_s[:, 8:16].unsqueeze(2).to_broadcast([P, 8, HD]), ALU.mult))
                link(nc.vector.tensor_tensor(src, src, qk_gain[:, gain, :].unsqueeze(1).to_broadcast([P, 8, HD]), ALU.mult))

            def rope(src, heads):
                n = TT * heads * HD
                t1 = rope_t[0][:, 0:n].rearrange("p (t h d) -> p t h d", t=TT, h=heads)
                t2 = rope_t[1][:, 0:n].rearrange("p (t h d) -> p t h d", t=TT, h=heads)
                half = HD // 2
                cos = rope_cos.unsqueeze(2).to_broadcast([P, TT, heads, HD])
                sin = rope_sin.unsqueeze(2).to_broadcast([P, TT, heads, HD])
                nc.vector.tensor_tensor(t1, src, cos, ALU.mult)
                nc.vector.tensor_tensor(t2[:, :, :, 0:half], src[:, :, :, half:HD], sin[:, :, :, 0:half], ALU.mult)
                link(nc.vector.tensor_tensor(t2[:, :, :, half:HD], src[:, :, :, 0:half], sin[:, :, :, half:HD], ALU.mult))
                nc.vector.tensor_tensor(src, t1, t2, ALU.add).then_inc(q_roped, 1)

            for n in range(4):
                run_ahead(BLOCK["evq"] + n, single("od_shift", 2 * n))
                dve.wait_ge(acc_free, 2 + ACC["evq"] + n + 1)
                if n < 2:
                    head_norm(n, q_sb[n % 2].rearrange("p (h d) -> p h d", h=8), 0)
                rope(q_sb[n % 2].rearrange("p (t h d) -> p t h d", t=TT, h=FT), FT)
            for m in range(2):
                n = 4 + m

                def four(mm, m=m):
                    for x in (0, 1):
                        k = 2 * mm + x
                        single("od_shift", 8 + 4 * m + 2 * (k // 4))(k % 4)
                run_ahead(BLOCK["evkv"] + m, four)
                dve.wait_ge(acc_free, 2 + ACC["evkv"] + 2 * (m + 1))
                k3 = q_sb[n % 2]
                if m == 0:
                    head_norm(2, k3.rearrange("p (h d) -> p h d", h=8), 1)
                rope(k3[:, 0:512].rearrange("p (t h d) -> p t h d", t=TT, h=2), 2)
            mod_out(3, [(OD_SHIFT, col("od_mod_b", 0, KT))])
            mod_zero(mod_sum[:, 0, :])

            def band_mask(s3, h):
                return nc.vector.tensor_tensor(s3[:, :, 0:T], s3[:, :, 0:T], band, ALU.add)

            attention(HEAD2, 2, 512, prob2, None, None, None)
            attention(HEAD2 + 8, 2, 512, prob2, band_mask, None,
                      lambda i, j: neg_sink[:, bass.ds(4 * i + j, 1)])
            with dve.Fori(0, 2) as i:
                for par in range(2):
                    bi = 2 * i + par
                    run_ahead(BLOCK["evz"] + bi, single("od_scale", 2 * bi))
                    dve.wait_ge(acc_free, 2 + ACC["evz"] + bi + 1)
                    nc.vector.tensor_tensor(gated, gated, q_T[:, bass.ds(4 * bi, FT), :], ALU.mult).then_inc(z_mul, 1)
                    dve.wait_ge(z_hi, bi + 1)
                    nc.vector.tensor_tensor(b_lo[:, bass.ds(4 * bi, FT), :], gated,
                                            b_hi[:, bass.ds(4 * bi, FT), :].bitcast(F32), ALU.subtract).then_inc(z_ready, 1)

            def gate_diagonals(src):
                for j in range(4):
                    nc.vector.tensor_tensor(grow[:, BW * j:BW * (j + 1)].rearrange("p (f n) -> p f n", f=FT),
                                            ident[:].unsqueeze(1).to_broadcast([P, FT, P]),
                                            mod_cols[:, src, FT * j:FT * (j + 1)].unsqueeze(2).to_broadcast([P, FT, P]),
                                            ALU.mult).then_inc(diag_ready, 1)

            dve.wait_ge(z_ready, 4)
            gate_diagonals(EV_GATE)
            with dve.Fori(0, 2) as i:
                for par in range(2):
                    bi = 2 * i + par
                    run_ahead(BLOCK["evo"] + bi, single("od_scale", 8 + 2 * bi))
            mod_out(4, [(OD_SCALE, col("od_mod_b", KT, KT))])
            link(nc.vector.scalar_tensor_tensor(mod_cols[:, OD_SCALE, :], mod_cols[:, OD_SCALE, :], 1.0, col("od_pre_g", 0, KT),
                                                ALU.add, ALU.mult))
            mod_zero(mod_sum[:, 0, :])
            post_norm(6, 2 + ACC["odu"], 64, 4, row_ready)
            dve.wait_ge(ssq_ready, 10)
            mean_eps(7)
            normed_rows(X)
            norm_split(4, mod_cols[:, OD_SCALE, :], mod_cols[:, OD_SHIFT, :], a_hi, a_lo)
            dve.wait_ge(table_in, 48)
            dve.wait_ge(a_ready, 5 * KT)
            nc.vector.memset(u_pad, 0.0).then_inc(u_zero, 1)
            for g in range(4):
                run_ahead(BLOCK["odu"] + g, single("od_gate", 2 * g))
                dve.wait_ge(acc_free, 2 + ACC["odu"] + g + 1)
                lo, hi = POOL_PAD - 8 + 1, POOL_PAD + T + 7
                link(nc.vector.tensor_tensor(win_a[:, :, lo:hi], u_pad[:, :, lo - 1:hi - 1], u_pad[:, :, lo:hi], ALU.add))
                cur, nxt, w = win_a, win_b, 2
                while w < POOL_SIZES[g]:
                    d = w // 2
                    lo, hi = lo + d, hi - d
                    link(nc.vector.tensor_tensor(nxt[:, :, lo:hi], cur[:, :, lo - d:hi - d], cur[:, :, lo + d:hi + d], ALU.add))
                    cur, nxt, w = nxt, cur, 2 * w
                s = cur[:, :, POOL_PAD:POOL_PAD + T]
                link(nc.vector.tensor_tensor(s, s, inv_cnt[:, g, :].unsqueeze(1).to_broadcast([P, FT, T]), ALU.mult))
                nc.vector.tensor_tensor(pooled, s, u_pad[:, :, POOL_PAD:POOL_PAD + T], ALU.subtract).then_inc(u_pooled, 1)
                dve.wait_ge(u_hi, g + 1)
                nc.vector.tensor_tensor(b_lo[:, FT * g:FT * (g + 1), :], pooled, b_hi[:, FT * g:FT * (g + 1), :].bitcast(F32),
                                        ALU.subtract).then_inc(u_ready, 1)
            with dve.Fori(0, 2) as i:
                for par in range(2):
                    bi = 2 * i + par
                    run_ahead(BLOCK["odg"] + bi, single("od_gate", 8 + 2 * bi))
            b = BLOCK["pool"]
            dve.wait_ge(acc_free, 2 + ACC["pool"])
            for g in range(4):
                split_lo(b + (g >= 2), range(4 + 2 * g, 6 + 2 * g) if g < 2 else range(2 * g - 4, 2 * g - 2))
                dve.wait_ge(step_done, 4 + 8 * b + 2 * (g + 1))
                if g:
                    dve.wait_ge(p_ready, g)
                for f in range(FT):
                    e = nc.vector.scalar_tensor_tensor(gated[:, f, :], acc[g % 2][:, T * f:T * (f + 1)],
                                                       col("pool_scale", FT * g + f), silu_g[:, FT * g + f, :], ALU.mult, ALU.mult)
                e.then_inc(acc_free, 1)
                dve.wait_ge(p_hi, g + 1)
                nc.vector.tensor_tensor(a_lo[:, FT * g:FT * (g + 1), :], gated, a_hi[:, FT * g:FT * (g + 1), :].bitcast(F32),
                                        ALU.subtract).then_inc(p_ready, 1)
            mod_out(5, [(OD_GATE, col("od_mod_b", 2 * KT, KT))])
            link(nc.vector.tensor_tensor(mod_cols[:, OD_GATE, :], mod_cols[:, OD_GATE, :], col("od_post_g", 0, KT), ALU.mult))
            dve.wait_ge(p_ready, 4)
            gate_diagonals(OD_GATE)
            for n in range(4):
                b = BLOCK["odo"] + n
                split_lo(b, range(4, 8))
                if b < LAST_BLOCK:
                    split_lo(b + 1, range(4))
            post_norm(8, 2 + ACC["odo"] + 4, 0, 8, row_ready)

        @block.tensor
        def _(pe):
            def step_feature(b, s, a2, hi, lo, first=None, kts=None):
                first = s == 0 if first is None else first
                for t in range(KPS):
                    k = KPS * s + t if kts is None else kts + t
                    for f in range(FT):
                        o = a2[:, T * f:T * (f + 1)]
                        wh = w_hi[:, s % SLOTS, t, P * f:P * (f + 1)]
                        wl = w_lo[:, s % SLOTS, t, P * f:P * (f + 1)]
                        nc.tensor.matmul(o, wh, hi[:, k, :], start=first and t == 0 and f % 2 == 0, stop=False, skip_group_check=True)
                        nc.tensor.matmul(o, wh, lo[:, k, :], start=False, stop=False, skip_group_check=True)
                        last = nc.tensor.matmul(o, wl, hi[:, k, :], start=False, stop=t == KPS - 1, skip_group_check=True)
                return last

            def step_tokens(b, s, a2, hi, lo):
                for t in range(KPS):
                    k = KPS * s + t
                    for tt in range(TT):
                        o = a2[:, BW * tt:BW * (tt + 1)]
                        ah = hi[:, k, P * tt:P * (tt + 1)]
                        nc.tensor.matmul(o, ah, w_hi[:, s % SLOTS, t, :], start=s == 0 and t == 0, stop=False)
                        nc.tensor.matmul(o, ah, w_lo[:, s % SLOTS, t, :], start=False, stop=False)
                        last = nc.tensor.matmul(o, lo[:, k, P * tt:P * (tt + 1)], w_hi[:, s % SLOTS, t, :],
                                                start=False, stop=s == STEPS - 1 and t == KPS - 1)
                return last

            def product(b, a, par, form, hi, lo, ready=None, per=1, base=0):
                pe.wait_ge(acc_free, a + 1)
                for s in range(STEPS):
                    if ready is not None:
                        pe.wait_ge(ready, base + (KPS * s + KPS - 1) // per + 1)
                    pe.wait_ge(split_done, 8 * b + s + 9)
                    form(b, s, acc[par][:, :], hi, lo).then_inc(step_done, 1)

            def transposes(m, xn):
                pe.wait_ge(xn_ready, xn)
                for j in range(KT // 2):
                    if m or j > 3:
                        pe.wait_ge(norm_tmp, KT * m + 2 * j - 6)
                    for k in range(2):
                        for tt in range(TT):
                            e = nc.tensor.transpose(aux[:, j % 4, T * k + P * tt:T * k + P * (tt + 1)],
                                                    Y[:, tt, P * (2 * j + k):P * (2 * j + k + 1)], ident[:])
                    e.then_inc(tr_done, 1)

            def sum_mod(unit, vectors, u):
                pe.wait_ge(mod_acc, MOD_END[unit])
                if u:
                    pe.wait_ge(mod_cols_ready, u)
                for v in range(vectors):
                    for f in range(KT):
                        e = nc.tensor.matmul(aux[:, 3, KT * v + f:KT * v + f + 1], mod_sum[:, v, P * f:P * (f + 1)], ones[:, 0:1],
                                             start=True, stop=True)
                e.then_inc(mod_summed, 1)

            def attention(n0, iters, keys, q_stage, v_stage, prob, prob_T, key_of, read_out):
                kt = keys // P
                with pe.Fori(0, iters) as i:
                    def score(j):
                        n = n0 + 4 * i + j
                        pe.wait_ge(staged, n + 1)
                        for tt in range(TT):
                            e = nc.tensor.matmul(acc[j % 2][:, keys * tt:keys * (tt + 1)], q_stage[:, j % 2, P * tt:P * (tt + 1)],
                                                 key_of(i, j), start=True, stop=True)
                        e.then_inc(scores, 1)

                    score(0)
                    for j in range(4):
                        n = n0 + 4 * i + j
                        p = j % 2
                        if j < 3:
                            score(j + 1)
                        pe.wait_ge(prob_ready, TT * (n + 1))
                        tr = aux[:, 0:kt // 2, :].rearrange("p a (k t) -> p (a k) t", t=T)
                        for k in range(kt):
                            for tt in range(TT):
                                e = nc.tensor.transpose(tr[:, k, P * tt:P * (tt + 1)], prob[:, p, tt, P * k:P * (k + 1)], ident[:])
                        e.then_inc(prob_tr, 1)
                        pe.wait_ge(prob_T_ready, n + 1)
                        pe.wait_ge(*read_out(n))
                        for k in range(kt):
                            e = nc.tensor.matmul(aux[:, 2 + p, 0:T], v_stage[:, p, k, :], prob_T[:, k, :],
                                                 start=k == 0, stop=k == kt - 1)
                        e.then_inc(pv_done, 1)

            pe.sem_inc(step_done, SLOTS)
            pe.sem_inc(pv_done, 2)
            pe.wait_ge(const_in, 64)
            pe.wait_ge(pad_ready, 1)
            transposes(0, 2)
            with pe.Fori(0, 2) as i:
                for par in range(2):
                    product(BLOCK["u"] + 2 * i + par, ACC["u"] + 2 * i + par, par, step_feature, a_hi, a_lo, a_ready)
            with pe.Fori(0, 2) as i:
                for par in range(2):
                    product(BLOCK["qk"] + 2 * i + par, ACC["qk"] + 2 * i + par, par, step_feature, a_hi, a_lo)
            for par in range(2):
                product(BLOCK["v"] + par, ACC["v"] + par, par, step_tokens, a_hi, a_lo)
            pe.wait_ge(conv_tap, 2 * CONV_TILES // 2 * TAPS)
            for k in range(CONV_TILES):
                e = nc.tensor.matmul(aux[:, 0, 0:T], ones[:], conv_y[:, k, :], start=k == 0, stop=k == CONV_TILES - 1)
            e.then_inc(ln_sum, 1)
            pe.wait_ge(conv_sq_ready, 1)
            for k in range(CONV_TILES):
                e = nc.tensor.matmul(aux[:, 1, 0:T], ones[:], conv_sq[:, k, :], start=k == 0, stop=k == CONV_TILES - 1)
            e.then_inc(ln_sum, 1)
            pe.wait_ge(acc_free, 2 + ACC["out"])
            pe.wait_ge(ln_act, 3)
            attention(HEAD1, 2, T, q_stage1, v_stage1, prob1, prob_T1,
                      lambda i, j: qk_T[:, bass.ds(HEADS + 4 * i + j, 1), :].rearrange("p a t -> p (a t)"),
                      lambda n: (mix_ready, CONV_TILES - 1 + n))
            pe.wait_ge(mix_ready, 16)
            with pe.Fori(0, 2) as i:
                for par in range(2):
                    product(BLOCK["out"] + 2 * i + par, ACC["out"] + 2 * i + par, par, step_tokens, b_hi, b_lo)
            transposes(1, 4)
            pe.wait_ge(norm_tmp, 2 * KT)
            sum_mod("ev_gate", 1, 0)
            for g0, unit in ((0, "ev_shift"), (2, "ev_scale")):
                with pe.Fori(0, 2) as g:
                    with pe.Fori(0, 2) as i:
                        for par in range(2):
                            bi = 8 * (g + g0) + 2 * i + par
                            product(BLOCK["ff"] + bi, ACC["ff"] + bi, par, step_feature, a_hi, a_lo, a_ready, 1, KT)
                    with pe.Fori(0, 2) as i:
                        for par in range(2):
                            bi = 8 * (g + g0) + 4 + 2 * i + par
                            product(BLOCK["ff"] + bi, ACC["ff"] + bi, par, step_tokens, b_hi, b_lo, hid_ready, FT, 4 * (g + g0))
                sum_mod(unit, 2, 1 + g0 // 2)
            pe.wait_ge(mod_cols_ready, 3)
            transposes(2, 6)
            transposes(3, 8)

            def q_transposes(n, tiles):
                pe.wait_ge(q_roped, n + 1)
                if n:
                    pe.wait_ge(q_T_ready, n)
                src = q_sb[n % 2]
                for x, (dst, s) in enumerate(tiles):
                    e = nc.tensor.transpose(aux[:, dst // 4, P * (dst % 4):P * (dst % 4 + 1)], src[:, P * s:P * (s + 1)], ident[:])
                e.then_inc(q_tr, 1)

            q_tiles = [(TT * h + tt, FT * tt + h) for h in range(FT) for tt in range(TT)]
            k_tiles = [(4 * h + tt, 2 * tt + h) for h in range(2) for tt in range(4)]
            for n in range(4):
                product(BLOCK["evq"] + n, ACC["evq"] + n, n % 2, step_tokens, a_hi, a_lo, a_ready, 1, 2 * KT)
                if n == 0:
                    pe.wait_ge(norm_tmp, 4 * KT)
                if n:
                    q_transposes(n - 1, q_tiles)
            for m in range(2):
                b = BLOCK["evkv"] + m
                pe.wait_ge(acc_free, ACC["evkv"] + 2 * m + 2)
                pe.wait_ge(a_ready, 4 * KT)
                for s in range(STEPS):
                    pe.wait_ge(split_done, 8 * b + s + 9)
                    step_tokens(b, s, acc[0][:, :], a_hi, a_lo)
                    step_tokens(b, s, acc[1][:, :], b_hi, b_lo).then_inc(step_done, 1)
                q_transposes(3 + m, q_tiles if m == 0 else k_tiles)
            sum_mod("od_shift", 1, 3)
            q_transposes(5, k_tiles)
            pe.wait_ge(q_T_ready, 6)
            pe.wait_ge(acc_free, 2 + ACC["evz"])
            pe.wait_ge(mod_cols_ready, 4)
            key2 = lambda first: lambda i, j: k_T[:, bass.ds(first + i, 1), :].rearrange("p a t -> p (a t)")
            attention(HEAD2, 2, 512, q_stage2, v_stage2, prob2, prob_T2, key2(0), lambda n: (head_out, n - HEAD2 + 1))
            attention(HEAD2 + 8, 2, 512, q_stage2, v_stage2, prob2, prob_T2, key2(2), lambda n: (head_out, n - HEAD2 + 1))
            with pe.Fori(0, 2) as i:
                for par in range(2):
                    product(BLOCK["evz"] + 2 * i + par, ACC["evz"] + 2 * i + par, par, step_feature, a_hi, a_lo)

            def gate_rows(g):
                for j in range(4):
                    pe.wait_ge(diag_ready, 4 * g + j + 1)
                    nc.tensor.matmul(aux[:, j, :], ones[:], grow[:, BW * j:BW * (j + 1)], start=True, stop=True).then_inc(row_sum, 1)

            pe.wait_ge(head_out, 2 + 16)
            gate_rows(0)
            pe.wait_ge(z_ready, 4)
            with pe.Fori(0, 2) as i:
                for par in range(2):
                    product(BLOCK["evo"] + 2 * i + par, ACC["evo"] + 2 * i + par, par, step_tokens, b_hi, b_lo)
            pe.wait_ge(row_ready, 4)
            sum_mod("od_scale", 1, 4)
            pe.wait_ge(mod_cols_ready, 5)
            transposes(4, 10)
            for g in range(4):
                product(BLOCK["odu"] + g, ACC["odu"] + g, g % 2, step_feature, a_hi, a_lo, a_ready, 1, 4 * KT)
            with pe.Fori(0, 2) as i:
                for par in range(2):
                    product(BLOCK["odg"] + 2 * i + par, ACC["odg"] + 2 * i + par, par, step_feature, a_hi, a_lo)
            b = BLOCK["pool"]
            for g in range(4):
                pe.wait_ge(acc_free, ACC["pool"] + g + 1)
                pe.wait_ge(u_ready, g + 1)
                for x in range(2):
                    s = 2 * g + x
                    pe.wait_ge(split_done, 8 * b + s + 9)
                    step_feature(b, s, acc[g % 2][:, :], b_hi, b_lo, first=x == 0).then_inc(step_done, 1)
            pe.wait_ge(norm_tmp, 5 * KT)
            sum_mod("od_gate", 1, 5)
            pe.wait_ge(mod_cols_ready, 6)
            gate_rows(1)
            for n in range(4):
                product(BLOCK["odo"] + n, ACC["odo"] + n, n % 2, step_tokens, a_hi, a_lo, p_ready, FT, 0)


def shape_constants():
    pos = np.arange(T)
    d = pos[:, None] - pos[None, :]
    dist = np.where(d >= 0, -d, -1e32).astype(np.float32)
    band = np.where(np.abs(d) <= WINDOW, 0.0, -1e30).astype(np.float32)
    freqs = HD // 4
    inv = (np.float32(10000.0) ** (-np.arange(freqs, dtype=np.float32) / np.float32(freqs))).astype(np.float32)
    row = (pos // GRID_W).astype(np.float32)
    column = (pos % GRID_W).astype(np.float32)
    ang = np.concatenate([row[:, None] * inv, column[:, None] * inv], axis=-1).astype(np.float32)
    cos = np.concatenate([np.cos(ang)] * 2, axis=-1).astype(np.float32)
    sin = np.concatenate([-np.sin(ang), np.sin(ang)], axis=-1).astype(np.float32)
    count = [np.clip(pos + w // 2, 0, T) - np.clip(pos - w // 2, 0, T) for w in POOL_SIZES]
    inv_count = np.stack([1.0 / c for c in count]).astype(np.float32).reshape(1, -1)
    tiles = lambda a: a.reshape(TT, P, -1).transpose(1, 0, 2).reshape(P, -1)
    return {
        "ident": np.eye(P, dtype=np.float32),
        "dist_neg": np.ascontiguousarray(tiles(dist)),
        "ev_table": np.ascontiguousarray(np.concatenate([tiles(cos), tiles(sin), tiles(band)], axis=1)),
        "od_table": np.ascontiguousarray(np.broadcast_to(inv_count, (P, inv_count.shape[1]))),
        "slope": np.broadcast_to((2.0 ** (-8.0 * np.arange(1, HEADS + 1) / HEADS) / SCALE).astype(np.float32), (P, HEADS)),
    }


def kernel(**inputs):
    import concourse.bacc as bacc
    from concourse.bass_utils import run_bass_kernel_spmd

    a = {n: np.asarray(v) for n, v in inputs.items()}
    consts = shape_constants()

    def column(v):
        return v.reshape(-1, P).T

    packed = {
        "g_mix_pre": column(a["g_mix_pre"]), "b_glu": column(a["b_glu"]), "b_dw": column(a["b_dw"]),
        "ln_g": column(a["ln_conv_g"]), "ln_b": column(a["ln_conv_b"]), "g_ffn_pre": column(a["g_ffn_pre"]),
        "c": column(a["c_2"]), "c_ctx": column(a["c_ctx_2"]), "ev_mod_b": column(a["ev_mod_b_2"]),
        "ev_pre_g": column(a["ev_pre_g_2"]), "ev_post_g": column(a["ev_post_g_2"]), "od_mod_b": column(a["od_mod_b_2"]),
        "od_pre_g": column(a["od_pre_g_2"]), "od_post_g": column(a["od_post_g_2"]), "pool_scale": column(a["od_pool_scale_2"]),
        "sink": np.broadcast_to(a["ev_sink_2"].reshape(1, HEADS), (P, HEADS)), "slope": consts.pop("slope"),
        "w_dw": a["w_dw"].reshape(TAPS, CONV_TILES, P).transpose(2, 1, 0).reshape(P, CONV_TILES * TAPS),
    }
    arrays = {
        "x": a["x"].reshape(T, D), "ctx": a["ctx_2"].reshape(T, D),
        "w_in": a["w_in"][0], "w_out": a["w_out"][0], "w_ff1": a["w_ff1"][0], "w_ff2": a["w_ff2"][0],
        "ev_mod_w": a["ev_mod_w_2"][0], "ev_w_in": a["ev_w_in_2"][0], "ev_w_out": a["ev_w_out_2"][0],
        "od_mod_w": a["od_mod_w_2"][0], "od_w_in": a["od_w_in_2"][0], "od_w_out": a["od_w_out_2"][0],
        "od_pool_w": a["od_pool_w_2"][0].reshape(D, BW),
        "g_mix_post": a["g_mix_post"].reshape(D), "g_ffn_post": a["g_ffn_post"].reshape(D),
        "q_norm": a["ev_q_norm_2"].reshape(HD), "k_norm": a["ev_k_norm_2"].reshape(HD),
        "cols": np.concatenate([packed[n] for n, _ in COLS], axis=1),
        **consts,
    }
    arrays = {f"in_{n}": np.ascontiguousarray(v) for n, v in arrays.items()}
    nc = bacc.Bacc("TRN2", target_bir_lowering=False, num_devices=1)
    io = {n[3:]: nc.dram_tensor(n, v.shape, mybir.dt.from_np(v.dtype), kind="ExternalInput").ap() for n, v in arrays.items()}
    out = nc.dram_tensor("out", (T, D), F32, kind="ExternalOutput").ap()
    build_program(nc, io, out)
    result = run_bass_kernel_spmd(nc, [arrays], core_ids=[0])
    return result.results[0]["out"].reshape(1, T, D)
```

```python
import math
from contextlib import ExitStack

import numpy as np

import concourse.bass as bass
import concourse.mybir as mybir

F32 = mybir.dt.float32
F32R = mybir.dt.float32r
ACT = mybir.ActivationFunctionType
ALU = mybir.AluOpType
AX = mybir.AxisListType

P = 128
T = 256
TT = T // P
D = 2048
KT = D // P
BW = 512
NBLK = D // BW
STEPS = 8
KPS = KT // STEPS
SLOTS = 4
FT = BW // P
HEADS = 8
HD = 128
CONV_TILES = 8
TAPS = 31
PAD = TAPS - 1
SCALE = HD ** -0.5
RMS_EPS = 1e-6
LN_EPS = 1e-5
POOL_PAD = 16
POOL_SIZES = (2, 4, 8, 16)
WINDOW = 128
GRID_W = 64
FF_GROUPS = 4
MH = D // 2

PRODUCTS = [("u", 4, 4), ("qk", 4, 4), ("v", 2, 2), ("out", 4, 4), ("ff", 8 * FF_GROUPS, 8 * FF_GROUPS),
            ("evq", 4, 4), ("evkv", 2, 4), ("evz", 4, 4), ("evo", 4, 4),
            ("odu", 4, 4), ("odg", 4, 4), ("pool", 1, 4), ("odo", 4, 4)]
BLOCK, ACC = {}, {}
_b = _a = 0
for _name, _nb, _na in PRODUCTS:
    BLOCK[_name], ACC[_name] = _b, _a
    _b, _a = _b + _nb, _a + _na
LAST_BLOCK = _b - 1

MOD_UNITS = [("ev_gate", 1), ("ev_shift", 2), ("ev_scale", 2), ("od_shift", 1), ("od_scale", 1), ("od_gate", 1)]
MOD_STEP0, MOD_LOAD0, MOD_END = {}, {}, {}
_n = _l = 0
for _name, _v in MOD_UNITS:
    MOD_STEP0[_name] = _n + 4
    MOD_LOAD0[_name] = _l
    _n += 4 + 2 * KT * _v
    _l += 2 * KT
    MOD_END[_name] = _n

COLS = [("g_mix_pre", 16), ("b_glu", 16), ("b_dw", 8), ("ln_g", 8), ("ln_b", 8), ("g_ffn_pre", 16),
        ("c", 16), ("c_ctx", 16), ("ev_mod_b", 48), ("ev_pre_g", 16), ("ev_post_g", 16),
        ("od_mod_b", 48), ("od_pre_g", 16), ("od_post_g", 16), ("pool_scale", 16), ("sink", 8),
        ("slope", 8), ("w_dw", CONV_TILES * TAPS)]
COL = {}
_c = 0
for _name, _n in COLS:
    COL[_name] = _c
    _c += _n
NCOLS = _c

R0, R1, R2, R3, SCRATCH = 0, 4096, 8192, 10240, 11264
HPAD = T + PAD
UPAD = T + 2 * POOL_PAD


def build_program(nc, io, out):
    weights = {n: io[n].rearrange("(t p) n -> p t n", p=P)
               for n in ("w_in", "w_out", "w_ff1", "w_ff2", "ev_w_in", "ev_w_out", "od_w_in", "od_w_out", "od_pool_w")}
    mod_w = {"ev": io["ev_mod_w"].rearrange("(t p) n -> p t n", p=P),
             "od": io["od_mod_w"].rearrange("(t p) n -> p t n", p=P)}
    tok = lambda ap: ap.rearrange("(t p) n -> p t n", p=P)

    with ExitStack() as ctx:
        def sb(name, shape, dt=F32):
            return ctx.enter_context(nc.sbuf_tensor(name, shape, dt))

        def sem(name):
            return ctx.enter_context(nc.semaphore(name))

        raw = sb("raw", [P, 4, 4, BW])
        w_hi = sb("w_hi", [P, SLOTS, KPS, BW], F32R)
        w_lo = sb("w_lo", [P, SLOTS, KPS, BW], F32R)
        mod_raw = sb("mod_raw", [P, 2, MH])
        mod_sum = sb("mod_sum", [P, 2, D])
        a_hi = sb("a_hi", [P, KT, T], F32R)
        a_lo = sb("a_lo", [P, KT, T], F32R)
        b_hi = sb("b_hi", [P, KT, T], F32R)
        b_lo = sb("b_lo", [P, KT, T], F32R)
        scratch = sb("scratch", [P, SCRATCH])
        cols = sb("cols", [P, NCOLS])
        ident = sb("ident", [P, P])
        ones = sb("ones", [P, P])
        qk_gain = sb("qk_gain", [P, 2, HD])
        table = sb("table", [P, 1024])
        silu_c = sb("silu_c", [P, 2, KT])
        neg_sink = sb("neg_sink", [P, HEADS])
        mod_cols = sb("mod_cols", [P, 8, KT])
        ssq_part = sb("ssq_part", [P, TT, NBLK])
        norm_s = sb("norm_s", [P, 8])
        head_s = sb("head_s", [P, 16])
        soft = sb("soft", [P, 2, 8])
        ln_rstd = sb("ln_rstd", [P, T])
        EV_GATE, EV_SHIFT, EV_SHIFT_C, EV_SCALE, EV_SCALE_C, OD_SHIFT, OD_SCALE, OD_GATE = range(8)

        acc = [ctx.enter_context(nc.psum_tensor(f"acc{i}", [P, 1024], F32)) for i in range(2)]
        aux = ctx.enter_context(nc.psum_tensor("aux", [P, 4, 512], F32))
        h_dram = nc.dram_tensor("h_spill", (T, D), F32, kind="Internal").ap()

        def view(off, *shape):
            n = math.prod(shape)
            v = scratch[:, off:off + n]
            if len(shape) == 2:
                v = v.rearrange("p (a b) -> p a b", a=shape[0])
            elif len(shape) == 3:
                v = v.rearrange("p (a b c) -> p a b c", a=shape[0], b=shape[1])
            return v

        Y = view(R0, TT, D)
        X = view(R1, TT, D)
        grow = view(R2, D)
        junk = view(R3, 512).bitcast(mybir.dt.bfloat16).rearrange("p (t n) -> p t n", t=TT)
        qk_T = view(R0, 2 * HEADS, T)
        conv_in = view(R1, CONV_TILES, HPAD)
        v_tok1 = view(R1 + CONV_TILES * HPAD, TT, HEADS * HD)
        o = R1 + CONV_TILES * HPAD + TT * HEADS * HD
        sig = view(o, FT, T)
        prob1 = view(o, 2, TT, T)
        prob_T1 = view(o + 4 * T, TT, T)
        q_stage1 = view(o + 6 * T, 2, T)
        v_stage1 = view(o + 8 * T, 2, TT, HD)
        head_o = table[:, 512:1024].rearrange("p (b t) -> p b t", b=2)
        conv_y = mod_sum[:, 1, :].rearrange("p (c t) -> p c t", c=CONV_TILES)
        conv_sq = view(R1, CONV_TILES, T)
        ff_sum = Y
        relu = view(R2, FT, T)
        hid = view(R2 + FT * T, FT, T)
        q_T = view(R0, 16, T)
        k_T = view(R1, 4, 512)
        v_tok2 = view(R1 + 2048, 4, 512)
        q_sb = [view(R2 + 1024 * i, 1024) for i in range(2)]
        ctx_junk = mod_sum[:, 1, :].bitcast(mybir.dt.bfloat16).rearrange("p (t n) -> p t n", t=TT)
        rope_t = [mod_sum[:, 1, 1024 * i:1024 * (i + 1)] for i in range(2)]
        prob2 = mod_sum[:, 1, :].rearrange("p (b t k) -> p b t k", b=2, t=TT)
        prob_T2 = view(R2, 4, T)
        q_stage2 = view(R2 + 1024, 2, T)
        v_stage2 = view(R2 + 1536, 4, HD)
        z_gate = view(R2 + 2048, FT, T)
        score2 = [aux[:, 0:2, :].rearrange("p a n -> p (a n)"), acc[1][:, :]]
        gated = view(R2, FT, T)
        mod_tmp = view(R2, 4, T)
        silu_g = view(R0, KT, T)
        u_pad = view(R2, FT, UPAD)
        win_a = view(R2 + FT * UPAD, FT, UPAD)
        win_b = mod_sum[:, 1, 0:FT * UPAD].rearrange("p (c t) -> p c t", c=FT)
        pooled = view(R0, FT, T)

        def col(name, i, n=1):
            c = COL[name]
            return cols[:, bass.ds(c + i, n)] if not isinstance(i, int) else cols[:, c + i:c + i + n]

        dist_neg = table[:, 0:512].rearrange("p (t k) -> p t k", t=TT)
        rope_cos = table[:, 0:256].rearrange("p (t d) -> p t d", t=TT)
        rope_sin = table[:, 256:512].rearrange("p (t d) -> p t d", t=TT)
        band = table[:, 512:1024].rearrange("p (t k) -> p t k", t=TT)
        inv_cnt = table[:, :].rearrange("p (g t) -> p g t", g=4)

        raw_in = [sem(f"raw_in{q}") for q in range(4)]
        hi_ready = sem("hi_ready")
        split_done = sem("split_done")
        step_done = sem("step_done")
        acc_free = sem("acc_free")
        mod_in = [sem(f"mod_in{i}") for i in range(2)]
        mod_acc = sem("mod_acc")
        mod_summed = sem("mod_summed")
        mod_cols_ready = sem("mod_cols_ready")
        const_in = sem("const_in")
        x_in = sem("x_in")
        grow_in = sem("grow_in")
        table_in = sem("table_in")
        h_out = sem("h_out")
        silu_ready = sem("silu_ready")
        dve_self = sem("dve_self")
        ssq_ready = sem("ssq_ready")
        var_ready = sem("var_ready")
        std_ready = sem("std_ready")
        h_ready = sem("h_ready")
        xn_ready = sem("xn_ready")
        tr_done = sem("tr_done")
        norm_hi = sem("norm_hi")
        norm_tmp = sem("norm_tmp")
        a_ready = sem("a_ready")
        pad_ready = sem("pad_ready")
        conv_tap = sem("conv_tap")
        conv_sq_ready = sem("conv_sq_ready")
        ln_sum = sem("ln_sum")
        ln_act = sem("ln_act")
        mix_hi = sem("mix_hi")
        mix_ready = sem("mix_ready")
        staged = sem("staged")
        q_staged = sem("q_staged")
        v_staged = sem("v_staged")
        scores = sem("scores")
        biased = sem("biased")
        head_max = sem("head_max")
        neg_max = sem("neg_max")
        exp_done = sem("exp_done")
        sum_ready = sem("sum_ready")
        inv_ready = sem("inv_ready")
        prob_ready = sem("prob_ready")
        prob_tr = sem("prob_tr")
        prob_T_ready = sem("prob_T_ready")
        pv_done = sem("pv_done")
        head_copied = sem("head_copied")
        head_out = sem("head_out")
        y_ready = sem("y_ready")
        hid_sq = sem("hid_sq")
        hid_hi = sem("hid_hi")
        hid_ready = sem("hid_ready")
        ff_zero = sem("ff_zero")
        q_sq = sem("q_sq")
        head_var = sem("head_var")
        head_std = sem("head_std")
        q_roped = sem("q_roped")
        q_tr = sem("q_tr")
        q_T_ready = sem("q_T_ready")
        z_mul = sem("z_mul")
        z_hi = sem("z_hi")
        z_ready = sem("z_ready")
        u_zero = sem("u_zero")
        u_pooled = sem("u_pooled")
        u_hi = sem("u_hi")
        u_ready = sem("u_ready")
        p_hi = sem("p_hi")
        p_ready = sem("p_ready")
        diag_ready = sem("diag_ready")
        row_sum = sem("row_sum")
        row_ready = sem("row_ready")
        out_done = sem("out_done")

        def span(i, n):
            return slice(i, i + n) if isinstance(i, int) else bass.ds(i, n)

        block = ctx.enter_context(nc.Block())

        HEAD1, HEAD2 = 0, HEADS

        @block.sync
        def _(sp):
            def load_block(b, w, row_tile, column):
                for q in range(4):
                    sp.wait_ge(split_done, 8 * b + 2 * q + 2)
                    sp.dma_start(raw[:, q], w[:, row_tile(4 * q), column]).then_inc(raw_in[q], 16)

            def rows(first=0):
                return lambda k: slice(first + k, first + k + 4)

            sp.dma_start(X, tok(io["x"])).then_inc(x_in, 16)
            sp.dma_start(ident[:], io["ident"]).then_inc(const_in, 16)
            sp.dma_start(cols[:], io["cols"]).then_inc(const_in, 16)
            sp.dma_start(qk_gain[:, 0, :], io["q_norm"].partition_broadcast(P)).then_inc(const_in, 16)
            sp.dma_start(qk_gain[:, 1, :], io["k_norm"].partition_broadcast(P)).then_inc(const_in, 16)
            sp.dma_start(table[:, 0:512], io["dist_neg"]).then_inc(table_in, 16)

            W = weights["w_in"]
            with sp.Fori(0, 2) as i:
                for par, c0 in ((0, 4096), (1, 3072)):
                    load_block(BLOCK["u"] + 2 * i + par, W, rows(), bass.ds(c0 + BW * i, BW))
            with sp.Fori(0, 4) as i:
                load_block(BLOCK["qk"] + i, W, rows(), bass.ds(BW * i, BW))
            with sp.Fori(0, 2) as i:
                load_block(BLOCK["v"] + i, W, rows(), bass.ds(D + BW * i, BW))
            W = weights["w_out"]

            load_block(BLOCK["out"], W, rows(), slice(0, BW))
            sp.wait_ge(mix_ready, 16)
            sp.dma_start(X, tok(io["x"])).then_inc(x_in, 16)
            sp.dma_start(grow, io["g_mix_post"].partition_broadcast(P)).then_inc(grow_in, 16)
            with sp.Fori(1, 4) as i:
                load_block(BLOCK["out"] + i, W, rows(), bass.ds(BW * i, BW))
            with sp.Fori(0, FF_GROUPS) as g:
                for half, W in ((0, weights["w_ff1"]), (1, weights["w_ff2"])):
                    with sp.Fori(0, 4) as i:
                        b = BLOCK["ff"] + 8 * g + 4 * half + i
                        if half == 0:
                            load_block(b, W, rows(), bass.ds(D * g + BW * i, BW))
                        else:
                            load_block(b, W, lambda k: bass.ds(KT * g + k, 4), bass.ds(BW * i, BW))
            sp.wait_ge(hid_ready, 4 * FF_GROUPS)
            sp.dma_start(grow, io["g_ffn_post"].partition_broadcast(P)).then_inc(grow_in, 16)
            sp.dma_start(table[:], io["ev_table"]).then_inc(table_in, 16)
            W = weights["ev_w_in"]
            load_block(BLOCK["evq"], W, rows(), slice(0, BW))
            sp.wait_ge(h_ready, 4)
            sp.dma_start(tok(h_dram), X).then_inc(h_out, 16)
            sp.wait_ge(tr_done, 24)
            sp.dma_start(Y, tok(io["ctx"])).then_inc(x_in, 16)
            with sp.Fori(1, 4) as i:
                load_block(BLOCK["evq"] + i, W, rows(), bass.ds(BW * i, BW))
            with sp.Fori(0, 2) as i:
                load_block(BLOCK["evkv"] + i, W, rows(), bass.ds(D + BW * i, BW))
            with sp.Fori(0, 4) as i:
                load_block(BLOCK["evz"] + i, W, rows(), bass.ds(D + 1024 + BW * i, BW))
            W = weights["ev_w_out"]
            load_block(BLOCK["evo"], W, rows(), slice(0, BW))
            sp.wait_ge(h_out, 16)
            sp.wait_ge(head_out, 2 + 16)
            sp.dma_start(X, tok(h_dram)).then_inc(x_in, 16)
            sp.dma_start(table[:], io["od_table"]).then_inc(table_in, 16)
            with sp.Fori(1, 4) as i:
                load_block(BLOCK["evo"] + i, W, rows(), bass.ds(BW * i, BW))
            W = weights["od_w_in"]
            with sp.Fori(0, 8) as i:
                load_block(BLOCK["odu"] + i, W, rows(), bass.ds(BW * i, BW))
            load_block(BLOCK["pool"], weights["od_pool_w"], rows(), slice(0, BW))
            with sp.Fori(0, 4) as i:
                load_block(BLOCK["odo"] + i, weights["od_w_out"], rows(), bass.ds(BW * i, BW))
            for tt in range(TT):
                sp.wait_ge(h_ready, 7 + tt)
                sp.dma_start(out[tt * P:(tt + 1) * P, :], X[:, tt, :]).then_inc(out_done, 16)
            sp.wait_ge(out_done, 32)

        @block.gpsimd
        def _(pool):
            nc.gpsimd.memset(ones[:], 1.0).then_inc(pad_ready, 1)

            def load_mod(unit, layer, part, first, last):
                vectors = dict(MOD_UNITS)[unit]
                with pool.Fori(first, last) as kt:
                    for half in range(2):
                        pool.wait_ge(mod_acc, MOD_STEP0[unit] + vectors * (2 * kt + half) - (2 if vectors == 2 else 1))
                        nc.gpsimd.dma_start(mod_raw[:, half, :],
                                            mod_w[layer][:, bass.ds(kt, 1), part * D + half * MH:part * D + (half + 1) * MH]
                                            ).then_inc(mod_in[half], 16)

            def stage(n, q_src, q_stage, v_src, v_stage, par):
                pool.wait_ge(pv_done, n + 1)
                nc.gpsimd.tensor_copy(q_stage[:, par, :], q_src)
                nc.gpsimd.tensor_copy(v_stage[:, par], v_src).then_inc(staged, 1)

            load_mod("ev_gate", "ev", 2, 0, 8)
            pool.wait_ge(acc_free, 2 + ACC["out"])
            with pool.Fori(0, 2) as i:
                for j in range(4):
                    h = 4 * i + j
                    stage(HEAD1 + h, qk_T[:, bass.ds(h, 1), :].rearrange("p a t -> p (a t)"), q_stage1,
                          v_tok1[:, :, bass.ds(h * HD, HD)], v_stage1, j % 2)
            load_mod("ev_gate", "ev", 2, 8, KT)
            load_mod("ev_shift", "ev", 0, 0, KT)
            load_mod("ev_scale", "ev", 1, 0, KT)
            load_mod("od_shift", "od", 0, 0, KT)
            def stage_q(h, par):
                if not isinstance(h, int) or h >= 2:
                    pool.wait_ge(scores, HEAD2 + h - 1)
                nc.gpsimd.tensor_copy(q_stage2[:, par, :], q_T[:, span(h, 1), :].rearrange("p a t -> p (a t)")).then_inc(q_staged, 1)

            def load_scale(kt, half, load):
                pool.wait_ge(mod_acc, MOD_STEP0["od_scale"] + load - 1)
                nc.gpsimd.dma_start(mod_raw[:, half, :],
                                    mod_w["od"][:, span(kt, 1), D + half * MH:D + (half + 1) * MH]).then_inc(mod_in[half], 16)

            def head_slots(i, slots):
                for j in slots:
                    stage_q(4 * i + j + 1, (j + 1) % 2)
                    if j == 0:
                        pool.wait_ge(pv_done, HEAD2 + 4 * i + 2)
                        nc.gpsimd.tensor_copy(v_stage2, v_tok2[:, :, span(i * HD, HD)]).then_inc(v_staged, 1)
                    load_scale(2 * i + (j + 1) // 2, (j + 1) % 2, 4 * i + j + 1)

            load_scale(0, 0, 0)
            pool.wait_ge(q_T_ready, 6)
            stage_q(0, 0)
            with pool.Fori(0, 3) as i:
                head_slots(i, range(4))
            head_slots(3, range(3))
            load_scale(8, 0, 16)
            load_scale(8, 1, 17)
            load_mod("od_scale", "od", 1, 9, KT)
            load_mod("od_gate", "od", 2, 0, KT)

        @block.scalar
        def _(act):
            def split_hi(b, steps):
                for s in steps:
                    act.wait_ge(step_done, 8 * b + s + 1)
                    if s % 2 == 0:
                        act.wait_ge(raw_in[s // 2], 16 * (b + 1))
                    nc.scalar.activation(w_hi[:, s % SLOTS], raw[:, s // 2, KPS * (s % 2):KPS * (s % 2) + KPS, :],
                                         ACT.Copy).then_inc(hi_ready, 1)

            def run_ahead(b):
                split_hi(b, range(4, 8))
                split_hi(b + 1, range(4))

            def block_done(b):
                act.wait_ge(step_done, 4 + 8 * (b + 1))

            def sums_of_squares(src, product):
                for tt in range(TT):
                    nc.scalar.activation(product(tt), src(tt), ACT.Square, accum_out=norm_s[:, tt:tt + 1]).then_inc(ssq_ready, 1)

            def root(n):
                act.wait_ge(var_ready, n + 1)
                nc.scalar.activation(norm_s[:, 4:6], norm_s[:, 2:4], ACT.Sqrt).then_inc(std_ready, 1)

            def norm_round(m, dst):
                for k in range(KT):
                    act.wait_ge(norm_tmp, KT * m + k + 1)
                    nc.scalar.activation(dst[:, k, :], mod_tmp[:, k % 4, :], ACT.Copy).then_inc(norm_hi, 1)

            def squares_out(i, par, src):
                for tt in range(TT):
                    c = ssq_part[:, tt, bass.ds(i, 1)] if not isinstance(i, int) else ssq_part[:, tt, i:i + 1]
                    last = nc.scalar.activation(junk[:, tt, :], src(tt), ACT.Square, accum_out=c)
                return last

            def row_block(name, i, par):
                b = BLOCK[name] + i
                block_done(b)
                act.wait_ge(acc_free, 2 + ACC[name] + i)
                dst = Y[:, :, bass.ds(BW * i, BW)] if not isinstance(i, int) else Y[:, :, BW * i:BW * (i + 1)]
                nc.scalar.activation(dst, acc[par][:, :].rearrange("p (t n) -> p t n", t=TT), ACT.Copy).then_inc(y_ready, 1)
                squares_out(i, par, lambda tt: acc[par][:, BW * tt:BW * (tt + 1)]).then_inc(acc_free, 1)

            def attention(n0, iters, keys, prob, prob_T, emit, sink_of):
                kt = keys // P
                with act.Fori(0, iters) as i:
                    for j in range(4):
                        n = n0 + 4 * i + j
                        p = j % 2
                        act.wait_ge(neg_max, n + 1)
                        for tt in range(TT):
                            e = nc.scalar.activation(prob[:, p, tt, :], acc[p][:, keys * tt:keys * (tt + 1)], ACT.Exp,
                                                     bias=soft[:, p, 2 + tt:3 + tt], scale=SCALE,
                                                     accum_out=soft[:, p, 4 + tt:5 + tt])
                        if sink_of:
                            e = nc.scalar.activation(soft[:, p, 6:8], soft[:, p, 2:4], ACT.Exp, bias=sink_of(i, j))
                        e.then_inc(exp_done, 1)
                        act.wait_ge(prob_tr, n + 1)
                        nc.scalar.activation(prob_T, aux[:, 0:kt // 2, :].rearrange("p a (k t) -> p (a k) t", t=T),
                                             ACT.Copy).then_inc(prob_T_ready, 1)
                        emit(n, 4 * i + j, p)

            act.wait_ge(const_in, 64)
            nc.scalar.activation(silu_c[:].rearrange("p a k -> p (a k)"), col("c", 0, 2 * KT), ACT.Silu).then_inc(silu_ready, 1)
            act.wait_ge(x_in, 16)
            sums_of_squares(lambda tt: X[:, tt, :], lambda tt: Y[:, tt, :])
            split_hi(0, range(4))
            root(0)
            norm_round(0, a_hi)
            with act.Fori(0, 2) as i:
                b = BLOCK["u"] + 2 * i
                run_ahead(b)
                block_done(b)
                act.wait_ge(acc_free, 2 + 2 * i)
                for f in range(FT):
                    e = nc.scalar.activation(sig[:, f, :], acc[0][:, T * f:T * (f + 1)], ACT.Sigmoid,
                                             bias=col("b_glu", 8 + 4 * i + f))
                e.then_inc(acc_free, 1)
                run_ahead(b + 1)
            with act.Fori(0, 2) as i:
                for par in range(2):
                    b = BLOCK["qk"] + 2 * i + par
                    run_ahead(b)
                    block_done(b)
                    nc.scalar.activation(qk_T[:, bass.ds(8 * i + 4 * par, FT), :],
                                         acc[par][:, :].rearrange("p (f t) -> p f t", f=FT), ACT.Copy).then_inc(acc_free, 1)
            for par in range(2):
                b = BLOCK["v"] + par
                run_ahead(b)
                block_done(b)
                nc.scalar.activation(v_tok1[:, :, BW * par:BW * (par + 1)],
                                     acc[par][:, :].rearrange("p (t n) -> p t n", t=TT), ACT.Copy).then_inc(acc_free, 1)
            act.wait_ge(ln_act, 1)
            nc.scalar.activation(conv_sq, conv_y, ACT.Square).then_inc(conv_sq_ready, 1)
            act.wait_ge(ln_act, 2)
            nc.scalar.activation(ln_rstd[:], ln_rstd[:], ACT.Sqrt).then_inc(conv_sq_ready, 1)
            act.wait_ge(ln_act, 3)
            for k in range(CONV_TILES):
                nc.scalar.activation(conv_sq[:, k, :], conv_y[:, k, :], ACT.Silu, bias=col("ln_b", k),
                                     scale=col("ln_g", k)).then_inc(conv_sq_ready, 1)
            for k in range(CONV_TILES):
                act.wait_ge(conv_sq_ready, 3 + k)
                nc.scalar.activation(b_hi[:, HEADS + k, :], conv_sq[:, k, :], ACT.Copy).then_inc(mix_hi, 1)

            def emit1(n, h, p):
                act.wait_ge(pv_done, n + 3)
                nc.scalar.activation(head_o[:, p, :], aux[:, 2 + p, 0:T], ACT.Copy).then_inc(head_copied, 1)
                act.wait_ge(head_copied, n + 1)
                nc.scalar.activation(b_hi[:, bass.ds(h, 1), :], head_o[:, p:p + 1, :], ACT.Copy).then_inc(mix_hi, 1)

            attention(HEAD1, 2, T, prob1, prob_T1, emit1, None)
            with act.Fori(0, 2) as i:
                for par in range(2):
                    run_ahead(BLOCK["out"] + 2 * i + par)
                    row_block("out", 2 * i + par, par)

            def post_then_norm(post, pre):
                root(post)
                for tt in range(TT):
                    act.wait_ge(h_ready, 2 * ((post + 1) // 2) - 1 + tt)
                    nc.scalar.activation(Y[:, tt, :], X[:, tt, :], ACT.Square,
                                         accum_out=norm_s[:, tt:tt + 1]).then_inc(ssq_ready, 1)
                root(pre)

            post_then_norm(1, 2)
            norm_round(1, a_hi)
            for g0 in (0, 2):
                with act.Fori(0, 2) as g:
                    with act.Fori(0, 2) as i:
                        for par in range(2):
                            bi = 2 * i + par
                            b = BLOCK["ff"] + 8 * (g + g0) + bi
                            m = 4 * (g + g0) + bi
                            run_ahead(b)
                            block_done(b)
                            nc.scalar.activation(relu, acc[par][:, :].rearrange("p (f t) -> p f t", f=FT),
                                                 ACT.Relu).then_inc(acc_free, 1)
                            act.wait_ge(hid_sq, m + 1)
                            nc.scalar.activation(b_hi[:, bass.ds(4 * bi, FT), :], hid, ACT.Copy).then_inc(hid_hi, 1)
                    with act.Fori(0, 2) as i:
                        for par in range(2):
                            bi = 2 * i + par
                            b = BLOCK["ff"] + 8 * (g + g0) + 4 + bi
                            run_ahead(b)
                            act.wait_ge(acc_free, 2 + ACC["ff"] + 8 * (g + g0) + 4 + bi + 1)
                            act.wait_ge(y_ready, NBLK + 4 * (g + g0) + bi)
                            squares_out(bi, par, lambda tt: ff_sum[:, tt, bass.ds(BW * bi, BW)]).then_inc(y_ready, 1)
            post_then_norm(3, 4)
            norm_round(2, a_hi)
            act.wait_ge(x_in, 48)
            for tt in range(TT):
                nc.scalar.activation(ctx_junk[:, tt, :], Y[:, tt, :], ACT.Square,
                                     accum_out=norm_s[:, tt:tt + 1]).then_inc(ssq_ready, 1)
            root(5)
            norm_round(3, b_hi)

            def q_block(b, par, n, heads_normed):
                block_done(b)
                nc.scalar.activation(q_sb[n % 2], acc[par][:, :], ACT.Copy).then_inc(acc_free, 1)

            def head_norm(n, src, m):
                act.wait_ge(acc_free, 2 + ACC["evq"] + (m + 1 if m < 2 else 6))
                if m:
                    act.wait_ge(q_roped, 1 if m == 1 else 4)
                nc.scalar.activation(rope_t[0], src, ACT.Square).then_inc(q_sq, 1)
                act.wait_ge(head_var, m + 1)
                nc.scalar.activation(head_s[:, 8:16], head_s[:, 0:8], ACT.Sqrt).then_inc(head_std, 1)

            def q_out(n):
                act.wait_ge(q_tr, n + 1)
                dst = (q_T[:, FT * n:FT * (n + 1), :] if n < 4 else k_T[:, 2 * (n - 4):2 * (n - 4) + 2, :])
                nc.scalar.activation(dst, aux[:, 0:2, :] if n >= 4 else
                                     aux[:, 0:2, :].rearrange("p a (h t) -> p (a h) t", t=T), ACT.Copy).then_inc(q_T_ready, 1)

            for n in range(4):
                b = BLOCK["evq"] + n
                run_ahead(b)
                q_block(b, n % 2, n, n < 2)
                if n < 2:
                    head_norm(n, q_sb[n % 2], n)
                if n >= 1:
                    q_out(n - 1)
            for m in range(2):
                n = 4 + m
                b = BLOCK["evkv"] + m
                run_ahead(b)
                block_done(b)
                kv = q_sb[n % 2].rearrange("p (t n) -> p t n", t=4)
                for side in range(2):
                    a4 = acc[side][:, :].rearrange("p (t n) -> p t n", t=TT)
                    nc.scalar.activation(kv[:, 2 * side:2 * side + 2, :], a4[:, :, 0:256], ACT.Copy)
                    nc.scalar.activation(v_tok2[:, 2 * side:2 * side + 2, 256 * m:256 * (m + 1)], a4[:, :, 256:512],
                                         ACT.Copy).then_inc(acc_free, 1)
                if m == 0:
                    head_norm(n, q_sb[n % 2], 2)
                q_out(n - 1)
            q_out(5)

            Z = BLOCK["evz"]

            def prob_copy(h, half):
                act.wait_ge(prob_tr, HEADS + 2 * h + half + 1)
                nc.scalar.activation(prob_T2[:, 2 * half:2 * half + 2, :], aux[:, 2, :].rearrange("p (k t) -> p k t", t=T),
                                     ACT.Copy).then_inc(prob_T_ready, 1)

            def head_read(h):
                act.wait_ge(pv_done, HEAD2 + h + 3)
                nc.scalar.activation(q_T[:, span(h, 1), :], aux[:, 3, 0:T].rearrange("p (a t) -> p a t", a=1),
                                     ACT.Copy).then_inc(head_out, 1)

            def z_silu(i):
                block_done(Z + i)
                if not isinstance(i, int) or i > 0:
                    act.wait_ge(z_mul, i)
                nc.scalar.activation(z_gate, acc[0][:, :].rearrange("p (f t) -> p f t", f=FT), ACT.Silu).then_inc(acc_free, 1)

            def z_round(i):
                act.wait_ge(z_mul, i + 1)
                nc.scalar.activation(b_hi[:, span(4 * i, FT), :], q_T[:, span(4 * i, FT), :], ACT.Copy).then_inc(z_hi, 1)

            def head_slots(i, windowed, first=False):
                for j in range(4):
                    h = 4 * i + j
                    p = j % 2
                    ahead = Z + i + (j >= 2), (2 * j + 4) % STEPS
                    if j == 0 and not first:
                        z_silu(i - 1)
                    if not first or j >= 2:
                        head_read(h - 2)
                    if not first or j >= 1:
                        prob_copy(h - 1, 0)
                    act.wait_ge(neg_max, HEAD2 + h + 1)
                    for tt in range(TT):
                        e = nc.scalar.activation(prob2[:, p, tt, :], score2[p][:, 512 * tt:512 * (tt + 1)], ACT.Exp,
                                                 bias=soft[:, p, 2 + tt:3 + tt], scale=SCALE,
                                                 accum_out=soft[:, p, 4 + tt:5 + tt])
                    if windowed:
                        e = nc.scalar.activation(soft[:, p, 6:8], soft[:, p, 2:4], ACT.Exp, bias=col("sink", h - 8))
                    e.then_inc(exp_done, 1)
                    split_hi(ahead[0], [ahead[1]])
                    if not first or j >= 1:
                        prob_copy(h - 1, 1)
                    if j == 2 and not first:
                        z_round(i - 1)
                    split_hi(ahead[0], [ahead[1] + 1])

            head_slots(0, False, True)
            head_slots(1, False)
            with act.Fori(2, 4) as i:
                head_slots(i, True)
            z_silu(3)
            head_read(14)
            prob_copy(15, 0)
            prob_copy(15, 1)
            head_read(15)
            z_round(3)

            def gate_row(g):
                for j in range(4):
                    act.wait_ge(row_sum, 4 * g + j + 1)
                    nc.scalar.activation(grow[:, BW * j:BW * (j + 1)], aux[:, j, :], ACT.Copy).then_inc(row_ready, 1)

            for n in range(4):
                run_ahead(BLOCK["evo"] + n)
                row_block("evo", n, n % 2)
                if n == 1:
                    gate_row(0)
            root(6)
            for tt in range(TT):
                act.wait_ge(h_ready, 5 + tt)
                nc.scalar.activation(Y[:, tt, :], X[:, tt, :], ACT.Square,
                                     accum_out=norm_s[:, tt:tt + 1]).then_inc(ssq_ready, 1)
            root(7)
            norm_round(4, a_hi)
            for g in range(4):
                b = BLOCK["odu"] + g
                run_ahead(b)
                block_done(b)
                act.wait_ge(u_zero, 1)
                if g:
                    act.wait_ge(u_pooled, g)
                nc.scalar.activation(u_pad[:, :, POOL_PAD:POOL_PAD + T],
                                     acc[g % 2][:, :].rearrange("p (f t) -> p f t", f=FT), ACT.Copy).then_inc(acc_free, 1)
                act.wait_ge(u_pooled, g + 1)
                nc.scalar.activation(b_hi[:, FT * g:FT * (g + 1), :], pooled, ACT.Copy).then_inc(u_hi, 1)
            with act.Fori(0, 2) as i:
                for par in range(2):
                    bi = 2 * i + par
                    b = BLOCK["odg"] + bi
                    run_ahead(b)
                    block_done(b)
                    nc.scalar.activation(silu_g[:, bass.ds(4 * bi, FT), :], acc[par][:, :].rearrange("p (f t) -> p f t", f=FT),
                                         ACT.Silu).then_inc(acc_free, 1)
            b = BLOCK["pool"]
            for g in range(4):
                split_hi(b + (g >= 2), range(4 + 2 * g, 6 + 2 * g) if g < 2 else range(2 * g - 4, 2 * g - 2))
                act.wait_ge(acc_free, 2 + ACC["pool"] + g + 1)
                nc.scalar.activation(a_hi[:, FT * g:FT * (g + 1), :], gated, ACT.Copy).then_inc(p_hi, 1)
            gate_row(1)
            for n in range(4):
                b = BLOCK["odo"] + n
                split_hi(b, range(4, 8))
                if b < LAST_BLOCK:
                    split_hi(b + 1, range(4))
                row_block("odo", n, n % 2)
            root(8)

        @block.vector
        def _(dve):
            chain = [0]

            def link(ins):
                chain[0] += 1
                ins.then_inc(dve_self, 1)
                dve.wait_ge(dve_self, chain[0])

            def split_lo(b, steps):
                for s in steps:
                    dve.wait_ge(hi_ready, 8 * b + s + 1)
                    nc.vector.tensor_tensor(w_lo[:, s % SLOTS], raw[:, s // 2, KPS * (s % 2):KPS * (s % 2) + KPS, :],
                                            w_hi[:, s % SLOTS].bitcast(F32), ALU.subtract).then_inc(split_done, 1)

            def run_ahead(b, between=None):
                for m in range(4):
                    split_lo(b + (m >= 2), (4, 5) if m == 0 else (6, 7) if m == 1 else (0, 1) if m == 2 else (2, 3))
                    if between:
                        between(m)

            def block_done(b):
                dve.wait_ge(step_done, 4 + 8 * (b + 1))

            def mod_step(unit, layer_vecs, kt, half, v, n, back, load):
                dve.wait_ge(mod_in[half], 16 * (load + 1))
                dve.wait_ge(mod_acc, n + 1 - back)
                c = silu_c[:, layer_vecs[v], bass.ds(kt, 1)] if not isinstance(kt, int) else silu_c[:, layer_vecs[v], kt:kt + 1]
                s = mod_sum[:, v, MH * half:MH * (half + 1)]
                nc.vector.scalar_tensor_tensor(s, mod_raw[:, half, :], c, s, ALU.mult, ALU.add).then_inc(mod_acc, 1)

            def single(unit, kt0):
                base = MOD_LOAD0[unit] // 2

                def go(m):
                    kt = kt0 + m // 2
                    mod_step(unit, (0,), kt, m % 2, 0, MOD_STEP0[unit] + 2 * kt + m % 2, 2, base + kt)
                return go

            def both(unit, kt):
                base = MOD_LOAD0[unit] // 2

                def go(m):
                    mod_step(unit, (0, 1), kt, m // 2, m % 2, MOD_STEP0[unit] + 4 * kt + m, 4, base + kt)
                return go

            def mod_zero(what):
                nc.vector.memset(what, 0.0).then_inc(mod_acc, 4)

            def mod_out(u, biases):
                dve.wait_ge(mod_summed, u + 1)
                for v, (dst, bias) in enumerate(biases):
                    e = nc.vector.tensor_tensor(mod_cols[:, dst, :], aux[:, 3, KT * v:KT * (v + 1)], bias, ALU.add)
                e.then_inc(mod_cols_ready, 1)
                dve.wait_ge(mod_cols_ready, u + 1)

            def mean_eps(n):
                nc.vector.tensor_scalar(norm_s[:, 2:4], norm_s[:, 0:2], 1.0 / D, RMS_EPS, ALU.mult, ALU.add).then_inc(var_ready, 1)
                dve.wait_ge(std_ready, n + 1)
                link(nc.vector.reciprocal(norm_s[:, 6:8], norm_s[:, 4:6]))

            def normed_rows(src):
                for tt in range(TT):
                    nc.vector.tensor_scalar(Y[:, tt, :], src[:, tt, :], norm_s[:, 6 + tt:7 + tt], None,
                                            ALU.mult).then_inc(xn_ready, 1)

            def norm_split(m, scale, shift, hi, lo):
                def modulate(k):
                    if k % 2 == 0:
                        dve.wait_ge(tr_done, KT // 2 * m + k // 2 + 1)
                    if m or k > 3:
                        dve.wait_ge(a_ready, KT * m + k - 3)
                    ps = aux[:, (k // 2) % 4, T * (k % 2):T * (k % 2) + T]
                    if shift is None:
                        e = nc.vector.tensor_scalar(mod_tmp[:, k % 4, :], ps, scale[:, k:k + 1], None, ALU.mult)
                    else:
                        e = nc.vector.tensor_scalar(mod_tmp[:, k % 4, :], ps, scale[:, k:k + 1], shift[:, k:k + 1],
                                                    ALU.mult, ALU.add)
                    e.then_inc(norm_tmp, 1)

                def split(k):
                    dve.wait_ge(norm_hi, KT * m + k + 1)
                    nc.vector.tensor_tensor(lo[:, k, :], mod_tmp[:, k % 4, :], hi[:, k, :].bitcast(F32),
                                            ALU.subtract).then_inc(a_ready, 1)
                for k in range(KT):
                    modulate(k)
                    if k >= 2:
                        split(k - 2)
                split(KT - 2)
                split(KT - 1)

            def attention(n0, iters, keys, prob, bias, emit, sink_of):
                with dve.Fori(0, iters) as i:
                    for j in range(4):
                        n = n0 + 4 * i + j
                        p = j % 2
                        s3 = acc[p][:, 0:TT * keys].rearrange("p (t k) -> p t k", t=TT)
                        dve.wait_ge(scores, n + 1)
                        if bias:
                            bias(s3, 4 * i + j).then_inc(biased, 1)
                            dve.wait_ge(biased, n + 1 - BIAS_SKIP.get(n0, 0))
                        nc.vector.tensor_reduce(soft[:, p, 0:2], s3, AX.X, ALU.max).then_inc(head_max, 1)
                        dve.wait_ge(head_max, n + 1)
                        if sink_of:
                            nc.vector.tensor_scalar(soft[:, p, 2:4], soft[:, p, 0:2], -SCALE, sink_of(i, j),
                                                    ALU.mult, ALU.min).then_inc(neg_max, 1)
                        else:
                            nc.vector.tensor_scalar(soft[:, p, 2:4], soft[:, p, 0:2], -SCALE, None,
                                                    ALU.mult).then_inc(neg_max, 1)
                        dve.wait_ge(exp_done, n + 1)
                        if sink_of:
                            nc.vector.tensor_tensor(soft[:, p, 4:6], soft[:, p, 4:6], soft[:, p, 6:8], ALU.add).then_inc(sum_ready, 1)
                            dve.wait_ge(sum_ready, 4 * i + j + 1)
                        nc.vector.reciprocal(soft[:, p, 0:2], soft[:, p, 4:6]).then_inc(inv_ready, 1)
                        dve.wait_ge(inv_ready, n + 1)
                        for tt in range(TT):
                            nc.vector.tensor_scalar(prob[:, p, tt, :], prob[:, p, tt, :], soft[:, p, tt:tt + 1], None,
                                                    ALU.mult).then_inc(prob_ready, 1)
                        if emit:
                            emit(n, 4 * i + j, p)

            BIAS_SKIP = {HEAD2 + 8: HEADS}

            dve.sem_inc(split_done, 8)
            dve.sem_inc(acc_free, 2)
            dve.sem_inc(head_out, 2)
            mod_zero(mod_sum[:, 0, :])
            dve.wait_ge(ssq_ready, 2)
            mean_eps(0)
            normed_rows(X)
            split_lo(0, range(4))
            norm_split(0, col("g_mix_pre", 0, KT), None, a_hi, a_lo)
            dve.wait_ge(xn_ready, 2)
            link(nc.vector.memset(conv_in, 0.0))
            nc.vector.tensor_scalar(neg_sink[:], col("sink", 0, HEADS), -1.0, None, ALU.mult)
            dve.wait_ge(silu_ready, 1)
            with dve.Fori(0, 2) as i:
                b = BLOCK["u"] + 2 * i
                run_ahead(b, single("ev_gate", 4 * i))
                run_ahead(b + 1, single("ev_gate", 4 * i + 2))
                block_done(b + 1)
                dve.wait_ge(acc_free, 2 + ACC["u"] + 2 * i + 1)
                for f in range(FT):
                    e = nc.vector.scalar_tensor_tensor(
                        conv_in[:, bass.ds(4 * i + f, 1), PAD:HPAD].rearrange("p a t -> p (a t)"),
                        acc[1][:, T * f:T * (f + 1)], col("b_glu", 4 * i + f), sig[:, f, :], ALU.add, ALU.mult)
                e.then_inc(acc_free, 1)

            def conv_pair(pair, taps, n0):
                for t in taps:
                    for c in range(2):
                        ct = 2 * pair + c
                        dyn = not isinstance(pair, int)
                        src = (conv_in[:, bass.ds(ct, 1), t:t + T].rearrange("p a t -> p (a t)") if dyn
                               else conv_in[:, ct, t:t + T])
                        y = (conv_y[:, bass.ds(ct, 1), :].rearrange("p a t -> p (a t)") if dyn else conv_y[:, ct, :])
                        w = col("w_dw", TAPS * ct + t)
                        if t == 0:
                            e = nc.vector.tensor_scalar(y, src, w, col("b_dw", ct), ALU.mult, ALU.add)
                        else:
                            dve.wait_ge(conv_tap, n0 + 2 * t + c - 1)
                            e = nc.vector.scalar_tensor_tensor(y, src, w, y, ALU.mult, ALU.add)
                        e.then_inc(conv_tap, 1)

            CONV0 = 0
            dve.wait_ge(acc_free, 2 + ACC["qk"])
            with dve.Fori(0, 2) as i:
                for par in range(2):
                    run_ahead(BLOCK["qk"] + 2 * i + par,
                              lambda m: conv_pair(i, range(16 * par + 4 * m, min(16 * par + 4 * m + 4, TAPS)), CONV0 + 62 * i))
            for par in range(2):
                run_ahead(BLOCK["v"] + par,
                          lambda m: conv_pair(2, range(16 * par + 4 * m, min(16 * par + 4 * m + 4, TAPS)), CONV0 + 124))
            conv_pair(3, range(TAPS), CONV0 + 186)
            dve.wait_ge(conv_tap, CONV0 + 248)
            dve.wait_ge(ln_sum, 1)
            mean = aux[:, 0, 0:T]
            link(nc.vector.tensor_scalar(ln_rstd[:], mean, 1.0 / 1024, None, ALU.mult))
            nc.vector.tensor_tensor(conv_y, conv_y, ln_rstd[:].unsqueeze(1).to_broadcast([P, CONV_TILES, T]),
                                    ALU.subtract).then_inc(ln_act, 1)
            dve.wait_ge(ln_act, 1)
            dve.wait_ge(ln_sum, 2)
            nc.vector.tensor_scalar(ln_rstd[:], aux[:, 1, 0:T], 1.0 / 1024, LN_EPS, ALU.mult, ALU.add).then_inc(ln_act, 1)
            dve.wait_ge(conv_sq_ready, 2)
            link(nc.vector.reciprocal(ln_rstd[:], ln_rstd[:]))
            nc.vector.tensor_tensor(conv_y, conv_y, ln_rstd[:].unsqueeze(1).to_broadcast([P, CONV_TILES, T]),
                                    ALU.mult).then_inc(ln_act, 1)
            for k in range(CONV_TILES):
                dve.wait_ge(mix_hi, k + 1)
                nc.vector.tensor_tensor(b_lo[:, HEADS + k, :], conv_sq[:, k, :], b_hi[:, HEADS + k, :].bitcast(F32),
                                        ALU.subtract).then_inc(mix_ready, 1)
            dve.wait_ge(table_in, 16)

            def alibi(s3, h):
                return nc.vector.scalar_tensor_tensor(s3, dist_neg, col("slope", h), s3, ALU.mult, ALU.add)

            def emit1(n, h, p):
                dve.wait_ge(mix_hi, CONV_TILES + h + 1)
                nc.vector.tensor_tensor(b_lo[:, bass.ds(h, 1), :], head_o[:, p:p + 1, :],
                                        b_hi[:, bass.ds(h, 1), :].bitcast(F32), ALU.subtract).then_inc(mix_ready, 1)

            attention(HEAD1, 2, T, prob1, alibi, emit1, None)
            with dve.Fori(0, 2) as i:
                for par in range(2):
                    bi = 2 * i + par
                    run_ahead(BLOCK["out"] + bi, single("ev_gate", 8 + 2 * bi))

            def post_norm(n, ysq, xin, gin, gsem):
                dve.wait_ge(acc_free, ysq) if n != 3 else dve.wait_ge(y_ready, ysq)
                link(nc.vector.tensor_reduce(norm_s[:, 0:2], ssq_part[:], AX.X, ALU.add))
                mean_eps(n)
                if xin:
                    dve.wait_ge(x_in, xin)
                dve.wait_ge(gsem, gin)
                for tt in range(TT):
                    link(nc.vector.scalar_tensor_tensor(Y[:, tt, :], Y[:, tt, :], norm_s[:, 6 + tt:7 + tt], grow,
                                                        ALU.mult, ALU.mult))
                    nc.vector.tensor_tensor(X[:, tt, :], X[:, tt, :], Y[:, tt, :], ALU.add).then_inc(h_ready, 1)

            post_norm(1, 2 + ACC["ff"], 32, 16, grow_in)
            dve.wait_ge(ssq_ready, 4)
            mean_eps(2)
            normed_rows(X)
            norm_split(1, col("g_ffn_pre", 0, KT), None, a_hi, a_lo)
            mod_out(0, [(EV_GATE, col("ev_mod_b", 32, KT))])
            nc.vector.tensor_tensor(mod_cols[:, EV_GATE, :], mod_cols[:, EV_GATE, :], col("ev_post_g", 0, KT),
                                    ALU.mult)
            dve.wait_ge(tr_done, 16)
            nc.vector.memset(ff_sum, 0.0).then_inc(ff_zero, 1)
            for g0, unit, u, dsts in ((0, "ev_shift", 1, (EV_SHIFT, EV_SHIFT_C)), (2, "ev_scale", 2, (EV_SCALE, EV_SCALE_C))):
                mod_zero(mod_sum[:])
                with dve.Fori(0, 2) as g:
                    with dve.Fori(0, 2) as i:
                        for par in range(2):
                            bi = 2 * i + par
                            b = BLOCK["ff"] + 8 * (g + g0) + bi
                            m = 4 * (g + g0) + bi
                            run_ahead(b, both(unit, 8 * g + bi))
                            dve.wait_ge(acc_free, 2 + ACC["ff"] + 8 * (g + g0) + bi + 1)
                            nc.vector.tensor_tensor(hid, relu, relu, ALU.mult).then_inc(hid_sq, 1)
                            dve.wait_ge(hid_hi, m + 1)
                            nc.vector.tensor_tensor(b_lo[:, bass.ds(4 * bi, FT), :], hid,
                                                    b_hi[:, bass.ds(4 * bi, FT), :].bitcast(F32), ALU.subtract).then_inc(hid_ready, 1)
                    with dve.Fori(0, 2) as i:
                        for par in range(2):
                            bi = 2 * i + par
                            b = BLOCK["ff"] + 8 * (g + g0) + 4 + bi
                            run_ahead(b, both(unit, 8 * g + 4 + bi))
                            block_done(b)
                            dve.wait_ge(ff_zero, 1)
                            dve.wait_ge(acc_free, 2 + ACC["ff"] + 8 * (g + g0))
                            s = ff_sum[:, :, bass.ds(BW * bi, BW)]
                            nc.vector.tensor_tensor(s, s, acc[par][:, :].rearrange("p (t n) -> p t n", t=TT),
                                                    ALU.add).then_inc(acc_free, 1)
                part = 16 * (u - 1)
                mod_out(u, [(d, col("ev_mod_b", part, KT)) for d in dsts])
                if u == 2:
                    for d in dsts:
                        link(nc.vector.scalar_tensor_tensor(mod_cols[:, d, :], mod_cols[:, d, :], 1.0, col("ev_pre_g", 0, KT),
                                                            ALU.add, ALU.mult))
            mod_zero(mod_sum[:, 0, :])
            post_norm(3, 4 * FF_GROUPS + 4, 0, 32, grow_in)
            dve.wait_ge(ssq_ready, 6)
            mean_eps(4)
            normed_rows(X)
            norm_split(2, mod_cols[:, EV_SCALE, :], mod_cols[:, EV_SHIFT, :], a_hi, a_lo)
            dve.wait_ge(ssq_ready, 8)
            mean_eps(5)
            normed_rows(Y)
            norm_split(3, mod_cols[:, EV_SCALE_C, :], mod_cols[:, EV_SHIFT_C, :], b_hi, b_lo)
            dve.wait_ge(table_in, 32)
            dve.wait_ge(a_ready, 4 * KT)

            def head_norm(m, src, gain):
                dve.wait_ge(q_sq, m + 1)
                link(nc.vector.tensor_reduce(head_s[:, 0:8], rope_t[0].rearrange("p (h d) -> p h d", h=8), AX.X, ALU.add))
                nc.vector.tensor_scalar(head_s[:, 0:8], head_s[:, 0:8], 1.0 / HD, RMS_EPS, ALU.mult, ALU.add).then_inc(head_var, 1)
                dve.wait_ge(head_std, m + 1)
                link(nc.vector.reciprocal(head_s[:, 8:16], head_s[:, 8:16]))
                link(nc.vector.tensor_tensor(src, src, head_s[:, 8:16].unsqueeze(2).to_broadcast([P, 8, HD]), ALU.mult))
                link(nc.vector.tensor_tensor(src, src, qk_gain[:, gain, :].unsqueeze(1).to_broadcast([P, 8, HD]), ALU.mult))

            def rope(src, heads):
                n = TT * heads * HD
                t1 = rope_t[0][:, 0:n].rearrange("p (t h d) -> p t h d", t=TT, h=heads)
                t2 = rope_t[1][:, 0:n].rearrange("p (t h d) -> p t h d", t=TT, h=heads)
                half = HD // 2
                cos = rope_cos.unsqueeze(2).to_broadcast([P, TT, heads, HD])
                sin = rope_sin.unsqueeze(2).to_broadcast([P, TT, heads, HD])
                nc.vector.tensor_tensor(t1, src, cos, ALU.mult)
                nc.vector.tensor_tensor(t2[:, :, :, 0:half], src[:, :, :, half:HD], sin[:, :, :, 0:half], ALU.mult)
                link(nc.vector.tensor_tensor(t2[:, :, :, half:HD], src[:, :, :, 0:half], sin[:, :, :, half:HD], ALU.mult))
                nc.vector.tensor_tensor(src, t1, t2, ALU.add).then_inc(q_roped, 1)

            for n in range(4):
                run_ahead(BLOCK["evq"] + n, single("od_shift", 2 * n))
                dve.wait_ge(acc_free, 2 + ACC["evq"] + n + 1)
                if n < 2:
                    head_norm(n, q_sb[n % 2].rearrange("p (h d) -> p h d", h=8), 0)
                rope(q_sb[n % 2].rearrange("p (t h d) -> p t h d", t=TT, h=FT), FT)
            for m in range(2):
                n = 4 + m

                def four(mm, m=m):
                    for x in (0, 1):
                        k = 2 * mm + x
                        single("od_shift", 8 + 4 * m + 2 * (k // 4))(k % 4)
                run_ahead(BLOCK["evkv"] + m, four)
                dve.wait_ge(acc_free, 2 + ACC["evkv"] + 2 * (m + 1))
                k3 = q_sb[n % 2]
                if m == 0:
                    head_norm(2, k3.rearrange("p (h d) -> p h d", h=8), 1)
                rope(k3[:, 0:512].rearrange("p (t h d) -> p t h d", t=TT, h=2), 2)
            mod_out(3, [(OD_SHIFT, col("od_mod_b", 0, KT))])
            mod_zero(mod_sum[:, 0, :])

            Z = BLOCK["evz"]

            def z_gating(i):
                dve.wait_ge(head_out, 2 + 4 * (i + 1))
                dve.wait_ge(acc_free, 2 + ACC["evz"] + i + 1)
                heads = q_T[:, span(4 * i, FT), :]
                nc.vector.tensor_tensor(heads, heads, z_gate, ALU.mult).then_inc(z_mul, 1)

            def z_split(i):
                dve.wait_ge(z_hi, i + 1)
                nc.vector.tensor_tensor(b_lo[:, span(4 * i, FT), :], q_T[:, span(4 * i, FT), :],
                                        b_hi[:, span(4 * i, FT), :].bitcast(F32), ALU.subtract).then_inc(z_ready, 1)

            def head_slots(i, windowed, first=False):
                scale_step = single("od_scale", 2 * i)
                for j in range(4):
                    h = 4 * i + j
                    p = j % 2
                    ahead = Z + i + (j >= 2), (2 * j + 4) % STEPS
                    s3 = score2[p].rearrange("p (t k) -> p t k", t=TT)
                    dve.wait_ge(scores, HEAD2 + h + 1)
                    if windowed:
                        nc.vector.tensor_tensor(s3[:, :, 0:T], s3[:, :, 0:T], band, ALU.add).then_inc(biased, 1)
                        dve.wait_ge(biased, h + 1)
                    nc.vector.tensor_reduce(soft[:, p, 0:2], s3, AX.X, ALU.max).then_inc(head_max, 1)
                    dve.wait_ge(head_max, HEAD2 + h + 1)
                    if windowed:
                        nc.vector.tensor_scalar(soft[:, p, 2:4], soft[:, p, 0:2], -SCALE, neg_sink[:, span(h - 8, 1)],
                                                ALU.mult, ALU.min).then_inc(neg_max, 1)
                    else:
                        nc.vector.tensor_scalar(soft[:, p, 2:4], soft[:, p, 0:2], -SCALE, None, ALU.mult).then_inc(neg_max, 1)
                    if j == 1 and not first:
                        z_gating(i - 1)
                    dve.wait_ge(exp_done, HEAD2 + h + 1)
                    if windowed:
                        nc.vector.tensor_tensor(soft[:, p, 4:6], soft[:, p, 4:6], soft[:, p, 6:8], ALU.add).then_inc(sum_ready, 1)
                        dve.wait_ge(sum_ready, h - 7)
                    nc.vector.reciprocal(soft[:, p, 0:2], soft[:, p, 4:6]).then_inc(inv_ready, 1)
                    dve.wait_ge(inv_ready, HEAD2 + h + 1)
                    for tt in range(TT):
                        nc.vector.tensor_scalar(prob2[:, p, tt, :], prob2[:, p, tt, :], soft[:, p, tt:tt + 1], None,
                                                ALU.mult).then_inc(prob_ready, 1)
                    split_lo(ahead[0], [ahead[1]])
                    scale_step(j)
                    if j == 3 and not first:
                        z_split(i - 1)
                    split_lo(ahead[0], [ahead[1] + 1])

            head_slots(0, False, True)
            head_slots(1, False)
            with dve.Fori(2, 4) as i:
                head_slots(i, True)
            z_gating(3)
            z_split(3)

            def gate_diagonals(src):
                for j in range(4):
                    nc.vector.tensor_tensor(grow[:, BW * j:BW * (j + 1)].rearrange("p (f n) -> p f n", f=FT),
                                            ident[:].unsqueeze(1).to_broadcast([P, FT, P]),
                                            mod_cols[:, src, FT * j:FT * (j + 1)].unsqueeze(2).to_broadcast([P, FT, P]),
                                            ALU.mult).then_inc(diag_ready, 1)

            for n in range(4):
                run_ahead(BLOCK["evo"] + n, single("od_scale", 8 + 2 * n))
                if n == 1:
                    dve.wait_ge(z_ready, 4)
                    gate_diagonals(EV_GATE)
            mod_out(4, [(OD_SCALE, col("od_mod_b", KT, KT))])
            link(nc.vector.scalar_tensor_tensor(mod_cols[:, OD_SCALE, :], mod_cols[:, OD_SCALE, :], 1.0, col("od_pre_g", 0, KT),
                                                ALU.add, ALU.mult))
            mod_zero(mod_sum[:, 0, :])
            post_norm(6, 2 + ACC["odu"], 64, 4, row_ready)
            dve.wait_ge(ssq_ready, 10)
            mean_eps(7)
            normed_rows(X)
            norm_split(4, mod_cols[:, OD_SCALE, :], mod_cols[:, OD_SHIFT, :], a_hi, a_lo)
            dve.wait_ge(table_in, 48)
            dve.wait_ge(a_ready, 5 * KT)
            nc.vector.memset(u_pad, 0.0).then_inc(u_zero, 1)
            for g in range(4):
                run_ahead(BLOCK["odu"] + g, single("od_gate", 2 * g))
                dve.wait_ge(acc_free, 2 + ACC["odu"] + g + 1)
                lo, hi = POOL_PAD - 8 + 1, POOL_PAD + T + 7
                link(nc.vector.tensor_tensor(win_a[:, :, lo:hi], u_pad[:, :, lo - 1:hi - 1], u_pad[:, :, lo:hi], ALU.add))
                cur, nxt, w = win_a, win_b, 2
                while w < POOL_SIZES[g]:
                    d = w // 2
                    lo, hi = lo + d, hi - d
                    link(nc.vector.tensor_tensor(nxt[:, :, lo:hi], cur[:, :, lo - d:hi - d], cur[:, :, lo + d:hi + d], ALU.add))
                    cur, nxt, w = nxt, cur, 2 * w
                s = cur[:, :, POOL_PAD:POOL_PAD + T]
                link(nc.vector.tensor_tensor(s, s, inv_cnt[:, g, :].unsqueeze(1).to_broadcast([P, FT, T]), ALU.mult))
                nc.vector.tensor_tensor(pooled, s, u_pad[:, :, POOL_PAD:POOL_PAD + T], ALU.subtract).then_inc(u_pooled, 1)
                dve.wait_ge(u_hi, g + 1)
                nc.vector.tensor_tensor(b_lo[:, FT * g:FT * (g + 1), :], pooled, b_hi[:, FT * g:FT * (g + 1), :].bitcast(F32),
                                        ALU.subtract).then_inc(u_ready, 1)
            with dve.Fori(0, 2) as i:
                for par in range(2):
                    bi = 2 * i + par
                    run_ahead(BLOCK["odg"] + bi, single("od_gate", 8 + 2 * bi))
            b = BLOCK["pool"]
            dve.wait_ge(acc_free, 2 + ACC["pool"])
            for g in range(4):
                split_lo(b + (g >= 2), range(4 + 2 * g, 6 + 2 * g) if g < 2 else range(2 * g - 4, 2 * g - 2))
                dve.wait_ge(step_done, 4 + 8 * b + 2 * (g + 1))
                if g:
                    dve.wait_ge(p_ready, g)
                for f in range(FT):
                    e = nc.vector.scalar_tensor_tensor(gated[:, f, :], acc[g % 2][:, T * f:T * (f + 1)],
                                                       col("pool_scale", FT * g + f), silu_g[:, FT * g + f, :], ALU.mult, ALU.mult)
                e.then_inc(acc_free, 1)
                dve.wait_ge(p_hi, g + 1)
                nc.vector.tensor_tensor(a_lo[:, FT * g:FT * (g + 1), :], gated, a_hi[:, FT * g:FT * (g + 1), :].bitcast(F32),
                                        ALU.subtract).then_inc(p_ready, 1)
            mod_out(5, [(OD_GATE, col("od_mod_b", 2 * KT, KT))])
            link(nc.vector.tensor_tensor(mod_cols[:, OD_GATE, :], mod_cols[:, OD_GATE, :], col("od_post_g", 0, KT), ALU.mult))
            dve.wait_ge(p_ready, 4)
            gate_diagonals(OD_GATE)
            for n in range(4):
                b = BLOCK["odo"] + n
                split_lo(b, range(4, 8))
                if b < LAST_BLOCK:
                    split_lo(b + 1, range(4))
            post_norm(8, 2 + ACC["odo"] + 4, 0, 8, row_ready)

        @block.tensor
        def _(pe):
            def step_feature(b, s, a2, hi, lo, first=None, kts=None):
                first = s == 0 if first is None else first
                for t in range(KPS):
                    k = KPS * s + t if kts is None else kts + t
                    for f in range(FT):
                        o = a2[:, T * f:T * (f + 1)]
                        wh = w_hi[:, s % SLOTS, t, P * f:P * (f + 1)]
                        wl = w_lo[:, s % SLOTS, t, P * f:P * (f + 1)]
                        nc.tensor.matmul(o, wh, hi[:, k, :], start=first and t == 0 and f % 2 == 0, stop=False, skip_group_check=True)
                        nc.tensor.matmul(o, wh, lo[:, k, :], start=False, stop=False, skip_group_check=True)
                        last = nc.tensor.matmul(o, wl, hi[:, k, :], start=False, stop=t == KPS - 1, skip_group_check=True)
                return last

            def step_tokens(b, s, a2, hi, lo):
                for t in range(KPS):
                    k = KPS * s + t
                    for tt in range(TT):
                        o = a2[:, BW * tt:BW * (tt + 1)]
                        ah = hi[:, k, P * tt:P * (tt + 1)]
                        nc.tensor.matmul(o, ah, w_hi[:, s % SLOTS, t, :], start=s == 0 and t == 0, stop=False)
                        nc.tensor.matmul(o, ah, w_lo[:, s % SLOTS, t, :], start=False, stop=False)
                        last = nc.tensor.matmul(o, lo[:, k, P * tt:P * (tt + 1)], w_hi[:, s % SLOTS, t, :],
                                                start=False, stop=s == STEPS - 1 and t == KPS - 1)
                return last

            def product(b, a, par, form, hi, lo, ready=None, per=1, base=0):
                pe.wait_ge(acc_free, a + 1)
                for s in range(STEPS):
                    if ready is not None:
                        pe.wait_ge(ready, base + (KPS * s + KPS - 1) // per + 1)
                    pe.wait_ge(split_done, 8 * b + s + 9)
                    form(b, s, acc[par][:, :], hi, lo).then_inc(step_done, 1)

            def transposes(m, xn):
                pe.wait_ge(xn_ready, xn)
                for j in range(KT // 2):
                    if m or j > 3:
                        pe.wait_ge(norm_tmp, KT * m + 2 * j - 6)
                    for k in range(2):
                        for tt in range(TT):
                            e = nc.tensor.transpose(aux[:, j % 4, T * k + P * tt:T * k + P * (tt + 1)],
                                                    Y[:, tt, P * (2 * j + k):P * (2 * j + k + 1)], ident[:])
                    e.then_inc(tr_done, 1)

            def sum_mod(unit, vectors, u):
                pe.wait_ge(mod_acc, MOD_END[unit])
                if u:
                    pe.wait_ge(mod_cols_ready, u)
                for v in range(vectors):
                    for f in range(KT):
                        e = nc.tensor.matmul(aux[:, 3, KT * v + f:KT * v + f + 1], mod_sum[:, v, P * f:P * (f + 1)], ones[:, 0:1],
                                             start=True, stop=True)
                e.then_inc(mod_summed, 1)

            def attention(n0, iters, keys, q_stage, v_stage, prob, prob_T, key_of, read_out):
                kt = keys // P
                with pe.Fori(0, iters) as i:
                    def score(j):
                        n = n0 + 4 * i + j
                        pe.wait_ge(staged, n + 1)
                        for tt in range(TT):
                            e = nc.tensor.matmul(acc[j % 2][:, keys * tt:keys * (tt + 1)], q_stage[:, j % 2, P * tt:P * (tt + 1)],
                                                 key_of(i, j), start=True, stop=True)
                        e.then_inc(scores, 1)

                    score(0)
                    for j in range(4):
                        n = n0 + 4 * i + j
                        p = j % 2
                        if j < 3:
                            score(j + 1)
                        pe.wait_ge(prob_ready, TT * (n + 1))
                        tr = aux[:, 0:kt // 2, :].rearrange("p a (k t) -> p (a k) t", t=T)
                        for k in range(kt):
                            for tt in range(TT):
                                e = nc.tensor.transpose(tr[:, k, P * tt:P * (tt + 1)], prob[:, p, tt, P * k:P * (k + 1)], ident[:])
                        e.then_inc(prob_tr, 1)
                        pe.wait_ge(prob_T_ready, n + 1)
                        pe.wait_ge(*read_out(n))
                        for k in range(kt):
                            e = nc.tensor.matmul(aux[:, 2 + p, 0:T], v_stage[:, p, k, :], prob_T[:, k, :],
                                                 start=k == 0, stop=k == kt - 1)
                        e.then_inc(pv_done, 1)

            pe.sem_inc(step_done, SLOTS)
            pe.sem_inc(pv_done, 2)
            pe.wait_ge(const_in, 64)
            pe.wait_ge(pad_ready, 1)
            transposes(0, 2)
            with pe.Fori(0, 2) as i:
                for par in range(2):
                    product(BLOCK["u"] + 2 * i + par, ACC["u"] + 2 * i + par, par, step_feature, a_hi, a_lo, a_ready)
            with pe.Fori(0, 2) as i:
                for par in range(2):
                    product(BLOCK["qk"] + 2 * i + par, ACC["qk"] + 2 * i + par, par, step_feature, a_hi, a_lo)
            for par in range(2):
                product(BLOCK["v"] + par, ACC["v"] + par, par, step_tokens, a_hi, a_lo)
            pe.wait_ge(conv_tap, 2 * CONV_TILES // 2 * TAPS)
            for k in range(CONV_TILES):
                e = nc.tensor.matmul(aux[:, 0, 0:T], ones[:], conv_y[:, k, :], start=k == 0, stop=k == CONV_TILES - 1)
            e.then_inc(ln_sum, 1)
            pe.wait_ge(conv_sq_ready, 1)
            for k in range(CONV_TILES):
                e = nc.tensor.matmul(aux[:, 1, 0:T], ones[:], conv_sq[:, k, :], start=k == 0, stop=k == CONV_TILES - 1)
            e.then_inc(ln_sum, 1)
            pe.wait_ge(acc_free, 2 + ACC["out"])
            pe.wait_ge(ln_act, 3)
            attention(HEAD1, 2, T, q_stage1, v_stage1, prob1, prob_T1,
                      lambda i, j: qk_T[:, bass.ds(HEADS + 4 * i + j, 1), :].rearrange("p a t -> p (a t)"),
                      lambda n: (mix_ready, CONV_TILES - 1 + n))
            pe.wait_ge(mix_ready, 16)
            with pe.Fori(0, 2) as i:
                for par in range(2):
                    product(BLOCK["out"] + 2 * i + par, ACC["out"] + 2 * i + par, par, step_tokens, b_hi, b_lo)
            transposes(1, 4)
            pe.wait_ge(norm_tmp, 2 * KT)
            sum_mod("ev_gate", 1, 0)
            for g0, unit in ((0, "ev_shift"), (2, "ev_scale")):
                with pe.Fori(0, 2) as g:
                    with pe.Fori(0, 2) as i:
                        for par in range(2):
                            bi = 8 * (g + g0) + 2 * i + par
                            product(BLOCK["ff"] + bi, ACC["ff"] + bi, par, step_feature, a_hi, a_lo, a_ready, 1, KT)
                    with pe.Fori(0, 2) as i:
                        for par in range(2):
                            bi = 8 * (g + g0) + 4 + 2 * i + par
                            product(BLOCK["ff"] + bi, ACC["ff"] + bi, par, step_tokens, b_hi, b_lo, hid_ready, FT, 4 * (g + g0))
                sum_mod(unit, 2, 1 + g0 // 2)
            pe.wait_ge(mod_cols_ready, 3)
            transposes(2, 6)
            transposes(3, 8)

            def q_transposes(n, tiles):
                pe.wait_ge(q_roped, n + 1)
                if n:
                    pe.wait_ge(q_T_ready, n)
                src = q_sb[n % 2]
                for x, (dst, s) in enumerate(tiles):
                    e = nc.tensor.transpose(aux[:, dst // 4, P * (dst % 4):P * (dst % 4 + 1)], src[:, P * s:P * (s + 1)], ident[:])
                e.then_inc(q_tr, 1)

            q_tiles = [(TT * h + tt, FT * tt + h) for h in range(FT) for tt in range(TT)]
            k_tiles = [(4 * h + tt, 2 * tt + h) for h in range(2) for tt in range(4)]
            for n in range(4):
                product(BLOCK["evq"] + n, ACC["evq"] + n, n % 2, step_tokens, a_hi, a_lo, a_ready, 1, 2 * KT)
                if n == 0:
                    pe.wait_ge(norm_tmp, 4 * KT)
                if n:
                    q_transposes(n - 1, q_tiles)
            for m in range(2):
                b = BLOCK["evkv"] + m
                pe.wait_ge(acc_free, ACC["evkv"] + 2 * m + 2)
                pe.wait_ge(a_ready, 4 * KT)
                for s in range(STEPS):
                    pe.wait_ge(split_done, 8 * b + s + 9)
                    step_tokens(b, s, acc[0][:, :], a_hi, a_lo)
                    step_tokens(b, s, acc[1][:, :], b_hi, b_lo).then_inc(step_done, 1)
                q_transposes(3 + m, q_tiles if m == 0 else k_tiles)
            sum_mod("od_shift", 1, 3)
            q_transposes(5, k_tiles)
            pe.wait_ge(q_T_ready, 6)
            pe.wait_ge(acc_free, 2 + ACC["evz"])
            pe.wait_ge(mod_cols_ready, 4)
            Z = BLOCK["evz"]

            def prob_transposes(h, j, half):
                p = j % 2
                pe.wait_ge(prob_ready, TT * (HEAD2 + h + 1))
                if half or not isinstance(h, int) or h > 0:
                    pe.wait_ge(prob_T_ready, HEADS + 2 * h + half)
                for k in range(2):
                    for tt in range(TT):
                        e = nc.tensor.transpose(aux[:, 2, T * k + P * tt:T * k + P * (tt + 1)],
                                                prob2[:, p, tt, P * (2 * half + k):P * (2 * half + k + 1)], ident[:])
                e.then_inc(prob_tr, 1)

            def weigh_v(h, i):
                pe.wait_ge(v_staged, i + 1)
                pe.wait_ge(prob_T_ready, HEADS + 2 * h + 2)
                pe.wait_ge(head_out, 2 + h)
                for k in range(4):
                    e = nc.tensor.matmul(aux[:, 3, 0:T], v_stage2[:, k, :], prob_T2[:, k, :], start=k == 0, stop=k == 3)
                e.then_inc(pv_done, 1)

            def z_step(i, s):
                pe.wait_ge(split_done, 8 * (Z + i) + s + 9)
                step_feature(Z + i, s, acc[0][:, :], a_hi, a_lo).then_inc(step_done, 1)

            def head_slots(i, first=False):
                for j in range(4):
                    h = 4 * i + j
                    before = not first or j >= 1
                    pe.wait_ge(q_staged, h + 1)
                    for tt in range(TT):
                        e = nc.tensor.matmul(score2[j % 2][:, 512 * tt:512 * (tt + 1)], q_stage2[:, j % 2, P * tt:P * (tt + 1)],
                                             k_T[:, span(i, 1), :].rearrange("p a t -> p (a t)"), start=True, stop=True)
                    e.then_inc(scores, 1)
                    if before:
                        prob_transposes(h - 1, j + 1, 0)
                    if j == 0 and not first:
                        pe.wait_ge(acc_free, 2 + ACC["evz"] + i)
                    z_step(i, 2 * j)
                    if before:
                        prob_transposes(h - 1, j + 1, 1)
                    z_step(i, 2 * j + 1)
                    if before:
                        weigh_v(h - 1, i - 1 if j == 0 else i)

            head_slots(0, True)
            with pe.Fori(1, 4) as i:
                head_slots(i)
            prob_transposes(15, 3, 0)
            prob_transposes(15, 3, 1)
            weigh_v(15, 3)

            def gate_rows(g):
                for j in range(4):
                    pe.wait_ge(diag_ready, 4 * g + j + 1)
                    nc.tensor.matmul(aux[:, j, :], ones[:], grow[:, BW * j:BW * (j + 1)], start=True, stop=True).then_inc(row_sum, 1)

            pe.wait_ge(acc_free, 2 + ACC["evo"])
            for n in range(4):
                product(BLOCK["evo"] + n, ACC["evo"] + n, n % 2, step_tokens, b_hi, b_lo, z_ready, FT, 0)
                if n == 1:
                    pe.wait_ge(head_out, 2 + 16)
                    gate_rows(0)
            pe.wait_ge(row_ready, 4)
            sum_mod("od_scale", 1, 4)
            pe.wait_ge(mod_cols_ready, 5)
            transposes(4, 10)
            for g in range(4):
                product(BLOCK["odu"] + g, ACC["odu"] + g, g % 2, step_feature, a_hi, a_lo, a_ready, 1, 4 * KT)
            with pe.Fori(0, 2) as i:
                for par in range(2):
                    product(BLOCK["odg"] + 2 * i + par, ACC["odg"] + 2 * i + par, par, step_feature, a_hi, a_lo)
            b = BLOCK["pool"]
            for g in range(4):
                pe.wait_ge(acc_free, ACC["pool"] + g + 1)
                pe.wait_ge(u_ready, g + 1)
                for x in range(2):
                    s = 2 * g + x
                    pe.wait_ge(split_done, 8 * b + s + 9)
                    step_feature(b, s, acc[g % 2][:, :], b_hi, b_lo, first=x == 0).then_inc(step_done, 1)
            pe.wait_ge(norm_tmp, 5 * KT)
            sum_mod("od_gate", 1, 5)
            pe.wait_ge(mod_cols_ready, 6)
            gate_rows(1)
            for n in range(4):
                product(BLOCK["odo"] + n, ACC["odo"] + n, n % 2, step_tokens, a_hi, a_lo, p_ready, FT, 0)


def shape_constants():
    pos = np.arange(T)
    d = pos[:, None] - pos[None, :]
    dist = np.where(d >= 0, -d, -1e32).astype(np.float32)
    band = np.where(np.abs(d) <= WINDOW, 0.0, -1e30).astype(np.float32)
    freqs = HD // 4
    inv = (np.float32(10000.0) ** (-np.arange(freqs, dtype=np.float32) / np.float32(freqs))).astype(np.float32)
    row = (pos // GRID_W).astype(np.float32)
    column = (pos % GRID_W).astype(np.float32)
    ang = np.concatenate([row[:, None] * inv, column[:, None] * inv], axis=-1).astype(np.float32)
    cos = np.concatenate([np.cos(ang)] * 2, axis=-1).astype(np.float32)
    sin = np.concatenate([-np.sin(ang), np.sin(ang)], axis=-1).astype(np.float32)
    count = [np.clip(pos + w // 2, 0, T) - np.clip(pos - w // 2, 0, T) for w in POOL_SIZES]
    inv_count = np.stack([1.0 / c for c in count]).astype(np.float32).reshape(1, -1)
    tiles = lambda a: a.reshape(TT, P, -1).transpose(1, 0, 2).reshape(P, -1)
    return {
        "ident": np.eye(P, dtype=np.float32),
        "dist_neg": np.ascontiguousarray(tiles(dist)),
        "ev_table": np.ascontiguousarray(np.concatenate([tiles(cos), tiles(sin), tiles(band)], axis=1)),
        "od_table": np.ascontiguousarray(np.broadcast_to(inv_count, (P, inv_count.shape[1]))),
        "slope": np.broadcast_to((2.0 ** (-8.0 * np.arange(1, HEADS + 1) / HEADS) / SCALE).astype(np.float32), (P, HEADS)),
    }


def kernel(**inputs):
    import concourse.bacc as bacc
    from concourse.bass_utils import run_bass_kernel_spmd

    a = {n: np.asarray(v) for n, v in inputs.items()}
    consts = shape_constants()

    def column(v):
        return v.reshape(-1, P).T

    packed = {
        "g_mix_pre": column(a["g_mix_pre"]), "b_glu": column(a["b_glu"]), "b_dw": column(a["b_dw"]),
        "ln_g": column(a["ln_conv_g"]), "ln_b": column(a["ln_conv_b"]), "g_ffn_pre": column(a["g_ffn_pre"]),
        "c": column(a["c_2"]), "c_ctx": column(a["c_ctx_2"]), "ev_mod_b": column(a["ev_mod_b_2"]),
        "ev_pre_g": column(a["ev_pre_g_2"]), "ev_post_g": column(a["ev_post_g_2"]), "od_mod_b": column(a["od_mod_b_2"]),
        "od_pre_g": column(a["od_pre_g_2"]), "od_post_g": column(a["od_post_g_2"]), "pool_scale": column(a["od_pool_scale_2"]),
        "sink": np.broadcast_to(a["ev_sink_2"].reshape(1, HEADS), (P, HEADS)), "slope": consts.pop("slope"),
        "w_dw": a["w_dw"].reshape(TAPS, CONV_TILES, P).transpose(2, 1, 0).reshape(P, CONV_TILES * TAPS),
    }
    arrays = {
        "x": a["x"].reshape(T, D), "ctx": a["ctx_2"].reshape(T, D),
        "w_in": a["w_in"][0], "w_out": a["w_out"][0], "w_ff1": a["w_ff1"][0], "w_ff2": a["w_ff2"][0],
        "ev_mod_w": a["ev_mod_w_2"][0], "ev_w_in": a["ev_w_in_2"][0], "ev_w_out": a["ev_w_out_2"][0],
        "od_mod_w": a["od_mod_w_2"][0], "od_w_in": a["od_w_in_2"][0], "od_w_out": a["od_w_out_2"][0],
        "od_pool_w": a["od_pool_w_2"][0].reshape(D, BW),
        "g_mix_post": a["g_mix_post"].reshape(D), "g_ffn_post": a["g_ffn_post"].reshape(D),
        "q_norm": a["ev_q_norm_2"].reshape(HD), "k_norm": a["ev_k_norm_2"].reshape(HD),
        "cols": np.concatenate([packed[n] for n, _ in COLS], axis=1),
        **consts,
    }
    arrays = {f"in_{n}": np.ascontiguousarray(v) for n, v in arrays.items()}
    nc = bacc.Bacc("TRN2", target_bir_lowering=False, num_devices=1)
    io = {n[3:]: nc.dram_tensor(n, v.shape, mybir.dt.from_np(v.dtype), kind="ExternalInput").ap() for n, v in arrays.items()}
    out = nc.dram_tensor("out", (T, D), F32, kind="ExternalOutput").ap()
    build_program(nc, io, out)
    result = run_bass_kernel_spmd(nc, [arrays], core_ids=[0])
    return result.results[0]["out"].reshape(1, T, D)
```

```python
import math
from contextlib import ExitStack

import numpy as np

import concourse.bass as bass
import concourse.mybir as mybir

F32 = mybir.dt.float32
F32R = mybir.dt.float32r
ACT = mybir.ActivationFunctionType
ALU = mybir.AluOpType
AX = mybir.AxisListType

P = 128
T = 256
TT = T // P
D = 2048
KT = D // P
BW = 512
NBLK = D // BW
STEPS = 8
KPS = KT // STEPS
SLOTS = 4
FT = BW // P
HEADS = 8
HD = 128
CONV_TILES = 8
TAPS = 31
PAD = TAPS - 1
SCALE = HD ** -0.5
RMS_EPS = 1e-6
LN_EPS = 1e-5
POOL_PAD = 16
POOL_SIZES = (2, 4, 8, 16)
WINDOW = 128
GRID_W = 64
FF_GROUPS = 4
MH = D // 2

PRODUCTS = [("u", 4, 4), ("qkv", 6, 6), ("out", 4, 4), ("ff", 8 * FF_GROUPS, 8 * FF_GROUPS),
            ("evq", 4, 4), ("evkv", 2, 4), ("evz", 4, 4), ("evo", 4, 4),
            ("odu", 4, 4), ("odg", 4, 4), ("pool", 1, 4), ("odo", 4, 4)]
BLOCK, ACC = {}, {}
_b = _a = 0
for _name, _nb, _na in PRODUCTS:
    BLOCK[_name], ACC[_name] = _b, _a
    _b, _a = _b + _nb, _a + _na
LAST_BLOCK = _b - 1

MOD_UNITS = [("ev_gate", 1), ("ev_shift", 2), ("ev_scale", 2), ("od_shift", 1), ("od_scale", 1), ("od_gate", 1)]
MOD_STEP0, MOD_LOAD0, MOD_END = {}, {}, {}
_n = _l = 0
for _name, _v in MOD_UNITS:
    MOD_STEP0[_name] = _n + 4
    MOD_LOAD0[_name] = _l
    _n += 4 + 2 * KT * _v
    _l += 2 * KT
    MOD_END[_name] = _n

COLS = [("g_mix_pre", 16), ("b_glu", 16), ("b_dw", 8), ("ln_g", 8), ("ln_b", 8), ("g_ffn_pre", 16),
        ("c", 16), ("c_ctx", 16), ("ev_mod_b", 48), ("ev_pre_g", 16), ("ev_post_g", 16),
        ("od_mod_b", 48), ("od_pre_g", 16), ("od_post_g", 16), ("pool_scale", 16), ("sink", 8),
        ("slope", 8), ("w_dw", CONV_TILES * TAPS)]
COL = {}
_c = 0
for _name, _n in COLS:
    COL[_name] = _c
    _c += _n
NCOLS = _c

R0, R1, R2, R3, SCRATCH = 0, 4096, 8192, 10240, 11264
HPAD = T + PAD
UPAD = T + 2 * POOL_PAD


def build_program(nc, io, out):
    weights = {n: io[n].rearrange("(t p) n -> p t n", p=P)
               for n in ("w_in", "w_out", "w_ff1", "w_ff2", "ev_w_in", "ev_w_out", "od_w_in", "od_w_out", "od_pool_w")}
    mod_w = {"ev": io["ev_mod_w"].rearrange("(t p) n -> p t n", p=P),
             "od": io["od_mod_w"].rearrange("(t p) n -> p t n", p=P)}
    tok = lambda ap: ap.rearrange("(t p) n -> p t n", p=P)

    with ExitStack() as ctx:
        def sb(name, shape, dt=F32):
            return ctx.enter_context(nc.sbuf_tensor(name, shape, dt))

        def sem(name):
            return ctx.enter_context(nc.semaphore(name))

        raw = sb("raw", [P, 4, 4, BW])
        w_hi = sb("w_hi", [P, SLOTS, KPS, BW], F32R)
        w_lo = sb("w_lo", [P, SLOTS, KPS, BW], F32R)
        mod_raw = sb("mod_raw", [P, 2, MH])
        mod_sum = sb("mod_sum", [P, 2, D])
        a_hi = sb("a_hi", [P, KT, T], F32R)
        a_lo = sb("a_lo", [P, KT, T], F32R)
        b_hi = sb("b_hi", [P, KT, T], F32R)
        b_lo = sb("b_lo", [P, KT, T], F32R)
        scratch = sb("scratch", [P, SCRATCH])
        cols = sb("cols", [P, NCOLS])
        ident = sb("ident", [P, P])
        ones = sb("ones", [P, P])
        qk_gain = sb("qk_gain", [P, 2, HD])
        table = sb("table", [P, 1024])
        silu_c = sb("silu_c", [P, 2, KT])
        neg_sink = sb("neg_sink", [P, HEADS])
        mod_cols = sb("mod_cols", [P, 8, KT])
        root_one = sb("root_one", [P, 1])
        ssq_part = sb("ssq_part", [P, TT, NBLK])
        norm_s = sb("norm_s", [P, 8])
        head_s = sb("head_s", [P, 16])
        soft = sb("soft", [P, 2, 8])
        ln_rstd = sb("ln_rstd", [P, T])
        EV_GATE, EV_SHIFT, EV_SHIFT_C, EV_SCALE, EV_SCALE_C, OD_SHIFT, OD_SCALE, OD_GATE = range(8)

        acc = [ctx.enter_context(nc.psum_tensor(f"acc{i}", [P, 1024], F32)) for i in range(2)]
        aux = ctx.enter_context(nc.psum_tensor("aux", [P, 4, 512], F32))
        h_dram = nc.dram_tensor("h_spill", (T, D), F32, kind="Internal").ap()

        def view(off, *shape):
            n = math.prod(shape)
            v = scratch[:, off:off + n]
            if len(shape) == 2:
                v = v.rearrange("p (a b) -> p a b", a=shape[0])
            elif len(shape) == 3:
                v = v.rearrange("p (a b c) -> p a b c", a=shape[0], b=shape[1])
            return v

        Y = view(R0, TT, D)
        X = view(R1, TT, D)
        grow = view(R2, D)
        junk = view(R3, 512).bitcast(mybir.dt.bfloat16).rearrange("p (t n) -> p t n", t=TT)
        qk_T = view(R0, 2 * HEADS, T)
        conv_in = view(R1, CONV_TILES, HPAD)
        v_tok1 = view(R1 + CONV_TILES * HPAD, TT, HEADS * HD)
        o = R1 + CONV_TILES * HPAD + TT * HEADS * HD
        sig = view(o, FT, T)
        prob1 = view(o, 2, TT, T)
        token_diag = ln_rstd[:].rearrange("p (t n) -> p t n", t=TT)
        score1 = [aux[:, i, :] for i in range(2)]
        prob_T1 = view(o + 4 * T, TT, T)
        q_stage1 = view(o + 6 * T, 2, T)
        v_stage1 = view(o + 8 * T, 2, TT, HD)
        head_o = table[:, 512:1024].rearrange("p (b t) -> p b t", b=2)
        conv_y = mod_sum[:, 1, :].rearrange("p (c t) -> p c t", c=CONV_TILES)
        conv_sq = view(R1, CONV_TILES, T)
        ff_sum = Y
        relu = view(R2, FT, T)
        hid = view(R2 + FT * T, FT, T)
        q_T = view(R0, 16, T)
        k_T = view(R1, 4, 512)
        v_tok2 = view(R1 + 2048, 4, 512)
        q_sb = [view(R2 + 1024 * i, 1024) for i in range(2)]
        ctx_junk = mod_sum[:, 1, :].bitcast(mybir.dt.bfloat16).rearrange("p (t n) -> p t n", t=TT)
        rope_t = [mod_sum[:, 1, 1024 * i:1024 * (i + 1)] for i in range(2)]
        prob2 = mod_sum[:, 1, :].rearrange("p (b t k) -> p b t k", b=2, t=TT)
        prob_T2 = view(R2, 4, T)
        q_stage2 = view(R2 + 1024, 2, T)
        v_stage2 = view(R2 + 1536, 4, HD)
        z_gate = view(R2 + 2048, FT, T)
        score2 = [aux[:, 0:2, :].rearrange("p a n -> p (a n)"), acc[1][:, :]]
        gated = view(R2, FT, T)
        mod_tmp = view(R2 + 2048, 4, T)
        silu_g = view(R0, KT, T)
        u_pad = view(R2, FT, UPAD)
        win_a = view(R2 + FT * UPAD, FT, UPAD)
        win_b = mod_sum[:, 1, 0:FT * UPAD].rearrange("p (c t) -> p c t", c=FT)
        pooled = view(R0, FT, T)

        def col(name, i, n=1):
            c = COL[name]
            return cols[:, bass.ds(c + i, n)] if not isinstance(i, int) else cols[:, c + i:c + i + n]

        dist_neg = table[:, 0:512].rearrange("p (t k) -> p t k", t=TT)
        rope_cos = table[:, 0:256].rearrange("p (t d) -> p t d", t=TT)
        rope_sin = table[:, 256:512].rearrange("p (t d) -> p t d", t=TT)
        band = table[:, 512:1024].rearrange("p (t k) -> p t k", t=TT)
        inv_cnt = table[:, :].rearrange("p (g t) -> p g t", g=4)

        raw_in = [sem(f"raw_in{q}") for q in range(4)]
        hi_ready = sem("hi_ready")
        split_done = sem("split_done")
        step_done = sem("step_done")
        acc_free = sem("acc_free")
        mod_in = [sem(f"mod_in{i}") for i in range(2)]
        mod_acc = sem("mod_acc")
        mod_summed = sem("mod_summed")
        mod_cols_ready = sem("mod_cols_ready")
        const_in = sem("const_in")
        x_first = [sem(f"x_first{i}") for i in range(TT)]
        x_in = sem("x_in")
        grow_in = sem("grow_in")
        table_in = sem("table_in")
        h_out = sem("h_out")
        silu_ready = sem("silu_ready")
        dve_self = sem("dve_self")
        ssq_ready = sem("ssq_ready")
        var_ready = sem("var_ready")
        std_ready = sem("std_ready")
        h_ready = sem("h_ready")
        scale_ready = sem("scale_ready")
        tr_done = sem("tr_done")
        norm_hi = sem("norm_hi")
        norm_tmp = sem("norm_tmp")
        a_ready = sem("a_ready")
        ones_ready = sem("ones_ready")
        conv_tap = sem("conv_tap")
        conv_sq_ready = sem("conv_sq_ready")
        ln_sum = sem("ln_sum")
        ln_act = sem("ln_act")
        conv_hi = sem("conv_hi")
        conv_ready = sem("conv_ready")
        heads_hi = sem("heads_hi")
        heads_ready = sem("heads_ready")
        q_staged = sem("q_staged")
        v_staged = sem("v_staged")
        scores = sem("scores")
        biased = sem("biased")
        head_max = sem("head_max")
        neg_max = sem("neg_max")
        exp_done = sem("exp_done")
        sum_ready = sem("sum_ready")
        inv_ready = sem("inv_ready")
        prob_ready = sem("prob_ready")
        prob_tr = sem("prob_tr")
        prob_T_ready = sem("prob_T_ready")
        pv_done = sem("pv_done")
        head_copied = sem("head_copied")
        head_out = sem("head_out")
        y_squared = sem("y_squared")
        ff_squared = sem("ff_squared")
        hid_sq = sem("hid_sq")
        hid_hi = sem("hid_hi")
        hid_ready = sem("hid_ready")
        ff_zero = sem("ff_zero")
        q_sq = sem("q_sq")
        head_var = sem("head_var")
        head_std = sem("head_std")
        q_roped = sem("q_roped")
        q_tr = sem("q_tr")
        q_T_ready = sem("q_T_ready")
        z_mul = sem("z_mul")
        z_hi = sem("z_hi")
        z_ready = sem("z_ready")
        u_zero = sem("u_zero")
        u_pooled = sem("u_pooled")
        u_hi = sem("u_hi")
        u_ready = sem("u_ready")
        p_hi = sem("p_hi")
        p_ready = sem("p_ready")
        diag_ready = sem("diag_ready")
        row_sum = sem("row_sum")
        row_ready = sem("row_ready")
        out_done = sem("out_done")

        def span(i, n):
            return slice(i, i + n) if isinstance(i, int) else bass.ds(i, n)

        def norm_bank(m, k):
            j = k // 2
            return aux[:, 2 + j % 2 if m == 3 and j > 3 else j % 4, T * (k % 2):T * (k % 2) + T]

        block = ctx.enter_context(nc.Block())

        HEAD1, HEAD2 = 0, HEADS

        @block.sync
        def _(sp):
            def load_block(b, w, row_tile, column):
                for q in range(4):
                    sp.wait_ge(split_done, 8 * b + 2 * q + 2)
                    sp.dma_start(raw[:, q], w[:, row_tile(4 * q), column]).then_inc(raw_in[q], 16)

            def rows(first=0):
                return lambda k: slice(first + k, first + k + 4)

            for tt in range(TT):
                sp.dma_start(X[:, tt, :], io["x"][tt * P:(tt + 1) * P, :]).then_inc(x_first[tt], 16)
            sp.dma_start(ident[:], io["ident"]).then_inc(const_in, 16)
            sp.dma_start(cols[:], io["cols"]).then_inc(const_in, 16)
            sp.dma_start(qk_gain[:, 0, :], io["q_norm"].partition_broadcast(P)).then_inc(const_in, 16)
            sp.dma_start(qk_gain[:, 1, :], io["k_norm"].partition_broadcast(P)).then_inc(const_in, 16)
            sp.dma_start(table[:, 0:512], io["dist_neg"]).then_inc(table_in, 16)

            W = weights["w_in"]
            with sp.Fori(0, 2) as i:
                for par, c0 in ((0, 4096), (1, 3072)):
                    load_block(BLOCK["u"] + 2 * i + par, W, rows(), bass.ds(c0 + BW * i, BW))
            with sp.Fori(0, 2) as half:
                for part in range(3):
                    load_block(BLOCK["qkv"] + 3 * half + part, W, rows(), bass.ds(BW * half + 1024 * part, BW))
            W = weights["w_out"]
            load_block(BLOCK["out"], W, rows(), slice(0, BW))
            sp.wait_ge(heads_ready, 8)
            sp.dma_start(grow, io["g_mix_post"].partition_broadcast(P)).then_inc(grow_in, 16)
            load_block(BLOCK["out"] + 1, W, rows(), slice(BW, 2 * BW))
            sp.wait_ge(conv_ready, 8)
            sp.dma_start(X, tok(io["x"])).then_inc(x_in, 16)
            with sp.Fori(2, 4) as i:
                load_block(BLOCK["out"] + i, W, rows(), bass.ds(BW * i, BW))
            def ff_block(g, half, i):
                b = BLOCK["ff"] + 8 * g + 4 * half + i
                if half == 0:
                    load_block(b, weights["w_ff1"], rows(), span(D * g + BW * i, BW))
                else:
                    load_block(b, weights["w_ff2"], lambda k: span(KT * g + k, 4), span(BW * i, BW))

            with sp.Fori(0, FF_GROUPS - 1) as g:
                for half in range(2):
                    with sp.Fori(0, 4) as i:
                        ff_block(g, half, i)
            g = FF_GROUPS - 1
            with sp.Fori(0, 4) as i:
                ff_block(g, 0, i)
            ff_block(g, 1, 0)
            sp.wait_ge(hid_ready, 4 * FF_GROUPS)
            sp.dma_start(grow, io["g_ffn_post"].partition_broadcast(P)).then_inc(grow_in, 16)
            sp.dma_start(table[:], io["ev_table"]).then_inc(table_in, 16)
            with sp.Fori(1, 4) as i:
                ff_block(g, 1, i)
            W = weights["ev_w_in"]
            load_block(BLOCK["evq"], W, rows(), slice(0, BW))
            sp.wait_ge(h_ready, 8)
            sp.dma_start(tok(h_dram), X).then_inc(h_out, 16)
            sp.wait_ge(ssq_ready, 10)
            sp.dma_start(Y, tok(io["ctx"])).then_inc(x_in, 16)
            with sp.Fori(1, 4) as i:
                load_block(BLOCK["evq"] + i, W, rows(), bass.ds(BW * i, BW))
            with sp.Fori(0, 2) as i:
                load_block(BLOCK["evkv"] + i, W, rows(), bass.ds(D + BW * i, BW))
            with sp.Fori(0, 4) as i:
                load_block(BLOCK["evz"] + i, W, rows(), bass.ds(D + 1024 + BW * i, BW))
            W = weights["ev_w_out"]
            load_block(BLOCK["evo"], W, rows(), slice(0, BW))
            sp.wait_ge(h_out, 16)
            sp.wait_ge(head_out, 2 + 16)
            sp.dma_start(X, tok(h_dram)).then_inc(x_in, 16)
            sp.dma_start(table[:], io["od_table"]).then_inc(table_in, 16)
            with sp.Fori(1, 4) as i:
                load_block(BLOCK["evo"] + i, W, rows(), bass.ds(BW * i, BW))
            W = weights["od_w_in"]
            with sp.Fori(0, 8) as i:
                load_block(BLOCK["odu"] + i, W, rows(), bass.ds(BW * i, BW))
            load_block(BLOCK["pool"], weights["od_pool_w"], rows(), slice(0, BW))
            with sp.Fori(0, 4) as i:
                load_block(BLOCK["odo"] + i, weights["od_w_out"], rows(), bass.ds(BW * i, BW))
            for n in range(2 * TT):
                tt, half = n // 2, slice(D // 2 * (n % 2), D // 2 * (n % 2 + 1))
                sp.wait_ge(h_ready, 13 + n)
                sp.dma_start(out[tt * P:(tt + 1) * P, half], X[:, tt, half]).then_inc(out_done, 16)
            sp.wait_ge(out_done, 16 * 2 * TT)

        @block.gpsimd
        def _(pool):
            nc.gpsimd.memset(ones[:], 1.0).then_inc(ones_ready, 1)

            def load_mod(unit, layer, part, first, last):
                vectors = dict(MOD_UNITS)[unit]
                def loads(kt):
                    for half in range(2):
                        pool.wait_ge(mod_acc, MOD_STEP0[unit] + vectors * (2 * kt + half) - (2 if vectors == 2 else 1))
                        nc.gpsimd.dma_start(mod_raw[:, half, :],
                                            mod_w[layer][:, span(kt, 1), part * D + half * MH:part * D + (half + 1) * MH]
                                            ).then_inc(mod_in[half], 16)

                if last == first + 1:
                    loads(first)
                else:
                    with pool.Fori(first, last) as kt:
                        loads(kt)

            def clear_sums(unit, what):
                if unit:
                    pool.wait_ge(mod_summed, unit)
                nc.gpsimd.memset(what, 0.0).then_inc(mod_acc, 4)

            clear_sums(0, mod_sum[:, 0, :])
            load_mod("ev_gate", "ev", 2, 0, 7)
            def stage_q1(h):
                if h >= 2:
                    pool.wait_ge(scores, h - 1)
                nc.gpsimd.tensor_copy(q_stage1[:, h % 2, :], qk_T[:, h, :]).then_inc(q_staged, 1)

            pool.wait_ge(acc_free, 2 + ACC["qkv"] + 3)
            stage_q1(0)
            for h in range(HEADS):
                if h == HEADS // 2 - 1:
                    pool.wait_ge(acc_free, 2 + ACC["qkv"] + 6)
                if h < HEADS - 1:
                    stage_q1(h + 1)
                pool.wait_ge(pv_done, h + 1)
                nc.gpsimd.tensor_copy(v_stage1[:, h % 2], v_tok1[:, :, h * HD:(h + 1) * HD]).then_inc(v_staged, 1)
                if h in (1, 3):
                    load_mod("ev_gate", "ev", 2, 7 + h // 2, 8 + h // 2)
            load_mod("ev_gate", "ev", 2, 9, KT)
            pool.wait_ge(conv_ready, 8)
            clear_sums(1, mod_sum[:])
            pool.wait_ge(ssq_ready, 6)
            nc.gpsimd.memset(ff_sum, 0.0).then_inc(ff_zero, 1)
            load_mod("ev_shift", "ev", 0, 0, KT)
            clear_sums(2, mod_sum[:])
            load_mod("ev_scale", "ev", 1, 0, KT)
            clear_sums(3, mod_sum[:, 0, :])
            load_mod("od_shift", "od", 0, 0, KT)
            clear_sums(4, mod_sum[:, 0, :])
            def stage_q(h, par):
                if not isinstance(h, int) or h >= 2:
                    pool.wait_ge(scores, HEAD2 + h - 1)
                nc.gpsimd.tensor_copy(q_stage2[:, par, :], q_T[:, span(h, 1), :].rearrange("p a t -> p (a t)")).then_inc(q_staged, 1)

            def load_scale(kt):
                for half in range(2):
                    pool.wait_ge(mod_acc, MOD_STEP0["od_scale"] + 2 * kt + half - 1)
                    nc.gpsimd.dma_start(mod_raw[:, half, :],
                                        mod_w["od"][:, span(kt, 1), D + half * MH:D + (half + 1) * MH]).then_inc(mod_in[half], 16)

            def head_slots(i, slots):
                for j in slots:
                    stage_q(4 * i + j + 1, (j + 1) % 2)
                    if j == 0:
                        pool.wait_ge(pv_done, HEAD2 + 4 * i + 2)
                        nc.gpsimd.tensor_copy(v_stage2, v_tok2[:, :, span(i * HD, HD)]).then_inc(v_staged, 1)
                    load_scale(4 * i + j + 1)

            load_scale(0)
            pool.wait_ge(q_T_ready, 6)
            stage_q(0, 0)
            with pool.Fori(0, 3) as i:
                head_slots(i, range(4))
            head_slots(3, range(3))
            clear_sums(5, mod_sum[:, 0, :])
            load_mod("od_gate", "od", 2, 0, KT)

        @block.scalar
        def _(act):
            def split_hi(b, steps):
                for s in steps:
                    act.wait_ge(step_done, 8 * b + s + 1)
                    if s % 2 == 0:
                        act.wait_ge(raw_in[s // 2], 16 * (b + 1))
                    nc.scalar.activation(w_hi[:, s % SLOTS], raw[:, s // 2, KPS * (s % 2):KPS * (s % 2) + KPS, :],
                                         ACT.Copy).then_inc(hi_ready, 1)

            def run_ahead(b):
                split_hi(b, range(4, 8))
                split_hi(b + 1, range(4))

            def most_ahead(b):
                split_hi(b, range(4, 8))
                split_hi(b + 1, range(2))

            def block_done(b):
                act.wait_ge(step_done, 4 + 8 * (b + 1))

            def sums_of_squares(src, product, tiles=range(TT)):
                for tt in tiles:
                    nc.scalar.activation(product[:, tt, :], src[:, tt, :], ACT.Square, accum_out=norm_s[:, tt:tt + 1]).then_inc(ssq_ready, 1)

            def load_root():
                nc.scalar.activation(root_one[:], ones[:, 0:1], ACT.Sqrt)

            def root(n):
                act.wait_ge(var_ready, n + 1)
                nc.scalar.activation(norm_s[:, 4:6], norm_s[:, 2:4], ACT.Sqrt).then_inc(std_ready, 1)

            def norm_scaled(m, scale, hi):
                for k in range(KT):
                    if k % 2 == 0:
                        act.wait_ge(tr_done, KT // 2 * m + k // 2 + 1)
                    nc.scalar.activation(hi[:, k, :], norm_bank(m, k), ACT.Copy, scale=scale[:, k:k + 1]).then_inc(norm_hi, 1)

            def norm_modulated(m, scale, shift, hi, tiles=range(KT)):
                def rounded(k):
                    act.wait_ge(norm_tmp, KT * (m - 2) + k + 1)
                    nc.scalar.activation(hi[:, k, :], mod_tmp[:, k % 4, :], ACT.Copy).then_inc(norm_hi, 1)

                for k in tiles:
                    if k % 2 == 0:
                        act.wait_ge(tr_done, KT // 2 * m + k // 2 + 1)
                    if m > 2 or k > 3:
                        act.wait_ge(a_ready, KT * m + k - 3)
                    nc.scalar.activation(mod_tmp[:, k % 4, :], norm_bank(m, k), ACT.Identity, bias=shift[:, k:k + 1],
                                         scale=scale[:, k:k + 1]).then_inc(norm_tmp, 1)
                    if k > tiles[0]:
                        rounded(k - 1)
                rounded(tiles[-1])

            def row_block(name, i, par):
                block_done(BLOCK[name] + i)
                act.wait_ge(acc_free, 2 + ACC[name] + i)
                for tt in range(TT):
                    nc.scalar.activation(junk[:, tt, :], acc[par][:, BW * tt:BW * (tt + 1)], ACT.Square,
                                         accum_out=ssq_part[:, tt, span(i, 1)]).then_inc(y_squared, 1)

            def residual_squares(post):
                for n in range(2 * TT):
                    tt, half = n // 2, slice(D // 2 * (n % 2), D // 2 * (n % 2 + 1))
                    act.wait_ge(h_ready, 4 * {1: 0, 3: 1, 6: 2}[post] + n + 1)
                    nc.scalar.activation(Y[:, tt, half], X[:, tt, half], ACT.Square,
                                         accum_out=ssq_part[:, tt, n % 2:n % 2 + 1]).then_inc(ssq_ready, 1)

            for tt in range(TT):
                act.wait_ge(x_first[tt], 16)
                sums_of_squares(X, Y, [tt])
            root(0)
            split_hi(0, (0, 1))
            act.wait_ge(const_in, 64)
            norm_scaled(0, col("g_mix_pre", 0, KT), a_hi)
            split_hi(0, (2, 3))
            nc.scalar.activation(silu_c[:].rearrange("p a k -> p (a k)"), col("c", 0, 2 * KT), ACT.Silu).then_inc(silu_ready, 1)
            with act.Fori(0, 2) as i:
                b = BLOCK["u"] + 2 * i
                run_ahead(b)
                block_done(b)
                act.wait_ge(acc_free, 2 + 2 * i)
                for f in range(FT):
                    e = nc.scalar.activation(sig[:, f, :], acc[0][:, T * f:T * (f + 1)], ACT.Sigmoid,
                                             bias=col("b_glu", 8 + 4 * i + f))
                e.then_inc(acc_free, 1)
                run_ahead(b + 1)
            QKV = BLOCK["qkv"]

            def qkv_read(n):
                half, part = n // 3, n % 3
                block_done(QKV + n)
                a2 = acc[n % 2][:, :]
                if part < 2:
                    e = nc.scalar.activation(qk_T[:, HEADS * part + FT * half:HEADS * part + FT * (half + 1), :],
                                             a2.rearrange("p (f t) -> p f t", f=FT), ACT.Copy)
                else:
                    e = nc.scalar.activation(v_tok1[:, :, BW * half:BW * (half + 1)], a2.rearrange("p (t n) -> p t n", t=TT), ACT.Copy)
                e.then_inc(acc_free, 1)

            for n in range(3):
                run_ahead(QKV + n)
                qkv_read(n)

            def ahead1(m, ks):
                for k in ks:
                    f = 6 * m + k + SLOTS
                    split_hi(QKV + 3 + f // STEPS, [f % STEPS])

            def head_slot1(m):
                p = m % 2
                if m >= 1:
                    act.wait_ge(prob_tr, m)
                    nc.scalar.activation(prob_T1, aux[:, 2, :].rearrange("p (k t) -> p k t", t=T), ACT.Copy).then_inc(prob_T_ready, 1)
                if m < 4:
                    ahead1(m, [0])
                if m < HEADS:
                    act.wait_ge(neg_max, m + 1)
                    for tt in range(TT):
                        e = nc.scalar.activation(prob1[:, p, tt, :], score1[p][:, T * tt:T * (tt + 1)], ACT.Exp,
                                                 bias=soft[:, p, 2 + tt:3 + tt], scale=SCALE, accum_out=soft[:, p, 4 + tt:5 + tt])
                    e.then_inc(exp_done, 1)
                    act.wait_ge(inv_ready, m + 1)
                    for tt in range(TT):
                        nc.scalar.activation(prob1[:, p, tt, :], prob1[:, p, tt, :], ACT.Copy,
                                             scale=soft[:, p, tt:tt + 1]).then_inc(prob_ready, 1)
                if m < 4:
                    ahead1(m, [1, 2, 3])
                if m >= 1:
                    act.wait_ge(pv_done, m + 2)
                    if m >= 3:
                        act.wait_ge(heads_ready, m - 2)
                    nc.scalar.activation(head_o[:, 1 - p, :], aux[:, 3, 0:T], ACT.Copy).then_inc(head_copied, 1)
                    act.wait_ge(head_copied, m)
                    nc.scalar.activation(b_hi[:, m - 1, :], head_o[:, 1 - p, :], ACT.Copy).then_inc(heads_hi, 1)
                if m < 4:
                    ahead1(m, [4, 5])
                if 1 <= m < 4:
                    qkv_read(2 + m)

            for m in range(HEADS):
                if m == HEADS - 1:
                    act.wait_ge(ln_act, 1)
                    nc.scalar.activation(conv_sq, conv_y, ACT.Square).then_inc(conv_sq_ready, 1)
                head_slot1(m)
            head_slot1(HEADS)
            act.wait_ge(ln_act, 2)
            nc.scalar.activation(ln_rstd[:], ln_rstd[:], ACT.Sqrt).then_inc(conv_sq_ready, 1)
            act.wait_ge(ln_act, 3)
            b = BLOCK["out"]
            split_hi(b, (4, 5))
            for k in range(CONV_TILES + 1):
                if k < CONV_TILES:
                    nc.scalar.activation(conv_sq[:, k, :], conv_y[:, k, :], ACT.Silu, bias=col("ln_b", k),
                                         scale=col("ln_g", k)).then_inc(conv_sq_ready, 1)
                if k:
                    act.wait_ge(conv_sq_ready, 2 + k)
                    nc.scalar.activation(b_hi[:, HEADS + k - 1, :], conv_sq[:, k - 1, :], ACT.Copy).then_inc(conv_hi, 1)
                if k in (2, 5):
                    split_hi(b, (6,) if k == 2 else (7,))
            load_root()
            split_hi(b + 1, range(4))
            row_block("out", 0, 0)
            for n in range(1, 4):
                if n < 3:
                    run_ahead(b + n)
                else:
                    most_ahead(b + n)
                row_block("out", n, n % 2)
            root(1)
            split_hi(b + 4, (2, 3))
            residual_squares(1)
            root(2)
            norm_scaled(1, col("g_ffn_pre", 0, KT), a_hi)
            def ff_hidden(g):
                with act.Fori(0, 2) as i:
                    for par in range(2):
                        bi = 2 * i + par
                        b = BLOCK["ff"] + 8 * g + bi
                        run_ahead(b)
                        block_done(b)
                        nc.scalar.activation(relu, acc[par][:, :].rearrange("p (f t) -> p f t", f=FT),
                                             ACT.Relu).then_inc(acc_free, 1)
                        act.wait_ge(hid_sq, 4 * g + bi + 1)
                        nc.scalar.activation(b_hi[:, bass.ds(4 * bi, FT), :], hid, ACT.Copy).then_inc(hid_hi, 1)

            def ff_squares(g, bi):
                act.wait_ge(acc_free, 2 + ACC["ff"] + 8 * g + 4 + bi + 1)
                act.wait_ge(ff_squared, 4 * g + bi + 1)
                for tt in range(TT):
                    e = nc.scalar.activation(junk[:, tt, :], ff_sum[:, tt, span(BW * bi, BW)], ACT.Square,
                                             accum_out=ssq_part[:, tt, span(bi, 1)])
                e.then_inc(ff_squared, 1)

            act.sem_inc(ff_squared, 1)
            with act.Fori(0, FF_GROUPS - 1) as g:
                ff_hidden(g)
                with act.Fori(0, 2) as i:
                    for par in range(2):
                        run_ahead(BLOCK["ff"] + 8 * g + 4 + 2 * i + par)
                        ff_squares(g, 2 * i + par)
            g = FF_GROUPS - 1
            ff_hidden(g)
            for n in range(NBLK):
                b = BLOCK["ff"] + 8 * g + 4 + n
                if n < NBLK - 1:
                    run_ahead(b)
                else:
                    most_ahead(b)
                ff_squares(g, n)
            root(3)
            split_hi(b + 1, (2, 3))
            residual_squares(3)
            root(4)
            norm_modulated(2, mod_cols[:, EV_SCALE, :], mod_cols[:, EV_SHIFT, :], a_hi)
            def q_block(b, par, n):
                block_done(b)
                nc.scalar.activation(q_sb[n % 2], acc[par][:, :], ACT.Copy).then_inc(acc_free, 1)

            def head_norm(n, src, m):
                act.wait_ge(acc_free, 2 + ACC["evq"] + (m + 1 if m < 2 else 6))
                if m:
                    act.wait_ge(q_roped, 1 if m == 1 else 4)
                nc.scalar.activation(rope_t[0], src, ACT.Square).then_inc(q_sq, 1)
                act.wait_ge(head_var, m + 1)
                nc.scalar.activation(head_s[:, 8:16], head_s[:, 0:8], ACT.Sqrt).then_inc(head_std, 1)

            def q_out(n):
                act.wait_ge(q_tr, n + 1)
                dst = (q_T[:, FT * n:FT * (n + 1), :] if n < 4 else k_T[:, 2 * (n - 4):2 * (n - 4) + 2, :])
                nc.scalar.activation(dst, aux[:, 0:2, :] if n >= 4 else
                                     aux[:, 0:2, :].rearrange("p a (h t) -> p (a h) t", t=T), ACT.Copy).then_inc(q_T_ready, 1)

            ctx_tiles = [range(4), range(4, 8), range(8, KT), ()]
            for n in range(4):
                b = BLOCK["evq"] + n
                if n == 0:
                    for tt in range(TT):
                        split_hi(b, (4 + 2 * tt, 5 + 2 * tt))
                        act.wait_ge(x_in, 32)
                        sums_of_squares(Y, ctx_junk, [tt])
                    split_hi(b + 1, range(2))
                    root(5)
                    split_hi(b + 1, range(2, 4))
                else:
                    run_ahead(b)
                q_block(b, n % 2, n)
                if ctx_tiles[n]:
                    norm_modulated(3, mod_cols[:, EV_SCALE_C, :], mod_cols[:, EV_SHIFT_C, :], b_hi, ctx_tiles[n])
                if n < 2:
                    head_norm(n, q_sb[n % 2], n)
                if n >= 1:
                    q_out(n - 1)
            for m in range(2):
                n = 4 + m
                b = BLOCK["evkv"] + m
                run_ahead(b)
                block_done(b)
                kv = q_sb[n % 2].rearrange("p (t n) -> p t n", t=4)
                for side in range(2):
                    a4 = acc[side][:, :].rearrange("p (t n) -> p t n", t=TT)
                    nc.scalar.activation(kv[:, 2 * side:2 * side + 2, :], a4[:, :, 0:256], ACT.Copy)
                    nc.scalar.activation(v_tok2[:, 2 * side:2 * side + 2, 256 * m:256 * (m + 1)], a4[:, :, 256:512],
                                         ACT.Copy).then_inc(acc_free, 1)
                if m == 0:
                    head_norm(n, q_sb[n % 2], 2)
                q_out(n - 1)
            q_out(5)

            Z = BLOCK["evz"]

            def prob_copy(h, half):
                act.wait_ge(prob_tr, HEADS + 2 * h + half + 1)
                nc.scalar.activation(prob_T2[:, 2 * half:2 * half + 2, :], aux[:, 2, :].rearrange("p (k t) -> p k t", t=T),
                                     ACT.Copy).then_inc(prob_T_ready, 1)

            def head_read(h):
                act.wait_ge(pv_done, HEAD2 + h + 3)
                nc.scalar.activation(q_T[:, span(h, 1), :], aux[:, 3, 0:T].rearrange("p (a t) -> p a t", a=1),
                                     ACT.Copy).then_inc(head_out, 1)

            def z_silu(i):
                block_done(Z + i)
                if not isinstance(i, int) or i > 0:
                    act.wait_ge(z_mul, i)
                nc.scalar.activation(z_gate, acc[0][:, :].rearrange("p (f t) -> p f t", f=FT), ACT.Silu).then_inc(acc_free, 1)

            def z_round(i):
                act.wait_ge(z_mul, i + 1)
                nc.scalar.activation(b_hi[:, span(4 * i, FT), :], q_T[:, span(4 * i, FT), :], ACT.Copy).then_inc(z_hi, 1)

            def head_slots(i, windowed, first=False):
                for j in range(4):
                    h = 4 * i + j
                    p = j % 2
                    ahead = Z + i + (j >= 2), (2 * j + 4) % STEPS
                    if j == 0 and not first:
                        z_silu(i - 1)
                    if not first or j >= 2:
                        head_read(h - 2)
                    if not first or j >= 1:
                        prob_copy(h - 1, 0)
                    act.wait_ge(neg_max, HEAD2 + h + 1)
                    for tt in range(TT):
                        e = nc.scalar.activation(prob2[:, p, tt, :], score2[p][:, 512 * tt:512 * (tt + 1)], ACT.Exp,
                                                 bias=soft[:, p, 2 + tt:3 + tt], scale=SCALE,
                                                 accum_out=soft[:, p, 4 + tt:5 + tt])
                    if windowed:
                        e = nc.scalar.activation(soft[:, p, 6:8], soft[:, p, 2:4], ACT.Exp, bias=col("sink", h - 8))
                    e.then_inc(exp_done, 1)
                    split_hi(ahead[0], [ahead[1]])
                    if not first or j >= 1:
                        prob_copy(h - 1, 1)
                    if j == 2 and not first:
                        z_round(i - 1)
                    split_hi(ahead[0], [ahead[1] + 1])

            head_slots(0, False, True)
            head_slots(1, False)
            with act.Fori(2, 4) as i:
                head_slots(i, True)
            z_silu(3)
            head_read(14)
            prob_copy(15, 0)
            prob_copy(15, 1)
            head_read(15)
            z_round(3)

            def gate_row(g):
                for j in range(4):
                    act.wait_ge(row_sum, 4 * g + j + 1)
                    nc.scalar.activation(grow[:, BW * j:BW * (j + 1)], aux[:, j, :], ACT.Copy).then_inc(row_ready, 1)

            load_root()
            for n in range(4):
                b = BLOCK["evo"] + n
                if n < 3:
                    run_ahead(b)
                else:
                    most_ahead(b)
                row_block("evo", n, n % 2)
                if n == 0:
                    gate_row(0)
            root(6)
            split_hi(b + 1, (2, 3))
            residual_squares(6)
            root(7)
            norm_modulated(4, mod_cols[:, OD_SCALE, :], mod_cols[:, OD_SHIFT, :], a_hi)
            def u_round(g):
                act.wait_ge(u_pooled, g + 1)
                nc.scalar.activation(b_hi[:, FT * g:FT * (g + 1), :], pooled, ACT.Copy).then_inc(u_hi, 1)

            act.wait_ge(u_zero, 1)
            for g in range(4):
                b = BLOCK["odu"] + g
                split_hi(b, range(4, 8))
                split_hi(b + 1, (0, 1))
                if g:
                    u_round(g - 1)
                split_hi(b + 1, (2, 3))
                block_done(b)
                nc.scalar.activation(u_pad[:, :, POOL_PAD:POOL_PAD + T],
                                     acc[g % 2][:, :].rearrange("p (f t) -> p f t", f=FT), ACT.Copy).then_inc(acc_free, 1)
            for n in range(4):
                b = BLOCK["odg"] + n
                split_hi(b, range(4, 8))
                split_hi(b + 1, (0, 1))
                if n == 0:
                    u_round(3)
                split_hi(b + 1, (2, 3))
                block_done(b)
                if n == 0:
                    act.wait_ge(u_ready, 4)
                nc.scalar.activation(silu_g[:, FT * n:FT * (n + 1), :], acc[n % 2][:, :].rearrange("p (f t) -> p f t", f=FT),
                                     ACT.Silu).then_inc(acc_free, 1)
            b = BLOCK["pool"]
            for g in range(4):
                split_hi(b + (g >= 2), range(4 + 2 * g, 6 + 2 * g) if g < 2 else range(2 * g - 4, 2 * g - 2))
                act.wait_ge(acc_free, 2 + ACC["pool"] + g + 1)
                nc.scalar.activation(a_hi[:, FT * g:FT * (g + 1), :], gated, ACT.Copy).then_inc(p_hi, 1)
            load_root()
            for n in range(4):
                b = BLOCK["odo"] + n
                split_hi(b, range(4, 8))
                if b < LAST_BLOCK:
                    split_hi(b + 1, range(4))
                row_block("odo", n, n % 2)
                if n == 0:
                    gate_row(1)
            root(8)

        @block.vector
        def _(dve):
            chain = [0]

            def link(ins):
                chain[0] += 1
                ins.then_inc(dve_self, 1)
                dve.wait_ge(dve_self, chain[0])

            def split_lo(b, steps):
                for s in steps:
                    dve.wait_ge(hi_ready, 8 * b + s + 1)
                    nc.vector.tensor_tensor(w_lo[:, s % SLOTS], raw[:, s // 2, KPS * (s % 2):KPS * (s % 2) + KPS, :],
                                            w_hi[:, s % SLOTS].bitcast(F32), ALU.subtract).then_inc(split_done, 1)

            def run_ahead(b, between=None):
                for m in range(4):
                    split_lo(b + (m >= 2), (4, 5) if m == 0 else (6, 7) if m == 1 else (0, 1) if m == 2 else (2, 3))
                    if between:
                        between(m)

            def most_ahead(b, between=None):
                for m in range(3):
                    split_lo(b + (m >= 2), (4, 5) if m == 0 else (6, 7) if m == 1 else (0, 1))
                    if between:
                        between(m)

            def block_done(b):
                dve.wait_ge(step_done, 4 + 8 * (b + 1))

            def mod_step(unit, layer_vecs, kt, half, v, n, back, load):
                dve.wait_ge(mod_in[half], 16 * (load + 1))
                dve.wait_ge(mod_acc, n + 1 - back)
                c = silu_c[:, layer_vecs[v], bass.ds(kt, 1)] if not isinstance(kt, int) else silu_c[:, layer_vecs[v], kt:kt + 1]
                s = mod_sum[:, v, MH * half:MH * (half + 1)]
                nc.vector.scalar_tensor_tensor(s, mod_raw[:, half, :], c, s, ALU.mult, ALU.add).then_inc(mod_acc, 1)

            def single(unit, kt0):
                return lambda m: halves(unit, 2 * kt0 + (0, 2, 3, 4)[m], (2, 1, 1, 0)[m])

            def halves(unit, h0, n):
                for h in range(n):
                    kt = (h0 + h) // 2
                    mod_step(unit, (0,), kt, (h0 + h) % 2, 0, MOD_STEP0[unit] + h0 + h, 2, MOD_LOAD0[unit] // 2 + kt)

            def one_tile(unit, kt):
                base = MOD_LOAD0[unit] // 2

                def go(m):
                    if m % 2 == 0:
                        mod_step(unit, (0,), kt, m // 2, 0, MOD_STEP0[unit] + 2 * kt + m // 2, 2, base + kt)
                return go

            def three(unit, kt0):
                return lambda m: halves(unit, 2 * kt0 + (0, 2, 3, 5)[m], (2, 1, 2, 1)[m])

            def both(unit, kt):
                base = MOD_LOAD0[unit] // 2

                def go(m):
                    for x in ((0, 1), (2,), (3,), ())[m]:
                        mod_step(unit, (0, 1), kt, x // 2, x % 2, MOD_STEP0[unit] + 4 * kt + x, 4, base + kt)
                return go

            def mod_out(u, biases):
                dve.wait_ge(mod_summed, u + 1)
                for v, (dst, bias) in enumerate(biases):
                    e = nc.vector.tensor_tensor(mod_cols[:, dst, :], aux[:, 3, KT * v:KT * (v + 1)], bias, ALU.add)
                e.then_inc(mod_cols_ready, 1)
                dve.wait_ge(mod_cols_ready, u + 1)

            def mean_eps(n, meanwhile=None):
                nc.vector.tensor_scalar(norm_s[:, 2:4], norm_s[:, 0:2], 1.0 / D, RMS_EPS, ALU.mult, ALU.add).then_inc(var_ready, 1)
                if meanwhile:
                    meanwhile()
                dve.wait_ge(std_ready, n + 1)
                link(nc.vector.reciprocal(norm_s[:, 6:8], norm_s[:, 4:6]))

            def token_diagonals():
                for tt in range(TT):
                    nc.vector.tensor_scalar(token_diag[:, tt, :], ident[:], norm_s[:, 6 + tt:7 + tt], None,
                                            ALU.mult).then_inc(scale_ready, 1)

            def norm_scaled(m, scale, hi, lo):
                for k in range(KT):
                    if k % 2 == 0:
                        dve.wait_ge(norm_hi, KT * m + k + 2)
                    nc.vector.scalar_tensor_tensor(lo[:, k, :], norm_bank(m, k), scale[:, k:k + 1],
                                                   hi[:, k, :].bitcast(F32), ALU.mult, ALU.subtract).then_inc(a_ready, 1)

            def norm_modulated(m, hi, lo, tiles=range(KT)):
                for k in tiles:
                    dve.wait_ge(norm_hi, KT * m + k + 1)
                    nc.vector.tensor_tensor(lo[:, k, :], mod_tmp[:, k % 4, :], hi[:, k, :].bitcast(F32), ALU.subtract).then_inc(a_ready, 1)

            dve.sem_inc(split_done, 8)
            dve.sem_inc(acc_free, 2)
            dve.sem_inc(head_out, 2)
            dve.wait_ge(const_in, 64)
            dve.wait_ge(ssq_ready, 2)
            mean_eps(0)
            token_diagonals()
            split_lo(0, (0, 1))
            norm_scaled(0, col("g_mix_pre", 0, KT), a_hi, a_lo)
            split_lo(0, (2, 3))
            link(nc.vector.memset(conv_in, 0.0))
            nc.vector.tensor_scalar(neg_sink[:], col("sink", 0, HEADS), -1.0, None, ALU.mult)
            dve.wait_ge(silu_ready, 1)
            tap_now = [0]

            def conv_taps(n):
                for o in range(tap_now[0], min(tap_now[0] + n, CONV_TILES * TAPS)):
                    pair, t, c = o // (2 * TAPS), o % (2 * TAPS) // 2, o % 2
                    ct = 2 * pair + c
                    src, y, w = conv_in[:, ct, t:t + T], conv_y[:, ct, :], col("w_dw", TAPS * ct + t)
                    if t == 0:
                        e = nc.vector.tensor_scalar(y, src, w, col("b_dw", ct), ALU.mult, ALU.add)
                    else:
                        dve.wait_ge(conv_tap, o - 1)
                        e = nc.vector.scalar_tensor_tensor(y, src, w, y, ALU.mult, ALU.add)
                    e.then_inc(conv_tap, 1)
                tap_now[0] += n

            for i in range(2):
                b = BLOCK["u"] + 2 * i
                run_ahead(b, three("ev_gate", 0) if i == 0 else lambda m: conv_taps(7))
                run_ahead(b + 1, three("ev_gate", 3) if i == 0 else lambda m: conv_taps(7))
                block_done(b + 1)
                dve.wait_ge(acc_free, 2 + ACC["u"] + 2 * i + 1)
                for f in range(FT):
                    e = nc.vector.scalar_tensor_tensor(conv_in[:, FT * i + f, PAD:HPAD], acc[1][:, T * f:T * (f + 1)],
                                                       col("b_glu", FT * i + f), sig[:, f, :], ALU.add, ALU.mult)
                e.then_inc(acc_free, 1)
                dve.wait_ge(acc_free, 2 + ACC["u"] + 2 * i + 2)
            QKV = BLOCK["qkv"]
            for n in range(3):
                run_ahead(QKV + n, lambda m: conv_taps(7))
            dve.wait_ge(table_in, 16)

            def ahead1(m, k):
                f = 6 * m + k + SLOTS
                split_lo(QKV + 3 + f // STEPS, [f % STEPS])

            def head_slot1(m):
                p = m % 2
                s3 = score1[p].rearrange("p (t k) -> p t k", t=TT)
                if m < HEADS:
                    dve.wait_ge(scores, m + 1)
                    nc.vector.scalar_tensor_tensor(s3, dist_neg, col("slope", m), s3, ALU.mult, ALU.add).then_inc(biased, 1)
                    dve.wait_ge(biased, m + 1)
                    nc.vector.tensor_reduce(soft[:, p, 0:2], s3, AX.X, ALU.max).then_inc(head_max, 1)
                    dve.wait_ge(head_max, m + 1)
                    nc.vector.tensor_scalar(soft[:, p, 2:4], soft[:, p, 0:2], -SCALE, None, ALU.mult).then_inc(neg_max, 1)
                if m < 4:
                    ahead1(m, 0)
                    conv_taps(3)
                if m < HEADS:
                    dve.wait_ge(exp_done, m + 1)
                    nc.vector.reciprocal(soft[:, p, 0:2], soft[:, p, 4:6]).then_inc(inv_ready, 1)
                for k in range(1, 6) if m < 4 else ():
                    ahead1(m, k)
                    conv_taps(4)
                    if k == 3:
                        halves("ev_gate", 12 + m, 1)
                if 4 <= m < 6:
                    conv_taps((CONV_TILES * TAPS - tap_now[0]) // (6 - m))
                if m >= 1:
                    dve.wait_ge(heads_hi, m)
                    nc.vector.tensor_tensor(b_lo[:, m - 1, :], head_o[:, 1 - p, :], b_hi[:, m - 1, :].bitcast(F32),
                                            ALU.subtract).then_inc(heads_ready, 1)

            for m in range(HEADS - 1):
                head_slot1(m)
            halves("ev_gate", 16, 2)
            dve.wait_ge(conv_tap, CONV_TILES * TAPS)
            dve.wait_ge(ln_sum, 1)
            link(nc.vector.tensor_scalar(ln_rstd[:], acc[0][:, 0:T], 1.0 / 1024, None, ALU.mult))
            nc.vector.tensor_tensor(conv_y, conv_y, ln_rstd[:].unsqueeze(1).to_broadcast([P, CONV_TILES, T]),
                                    ALU.subtract).then_inc(ln_act, 1)
            head_slot1(HEADS - 1)
            dve.wait_ge(ln_act, 1)
            dve.wait_ge(ln_sum, 2)
            nc.vector.tensor_scalar(ln_rstd[:], acc[1][:, 0:T], 1.0 / 1024, LN_EPS, ALU.mult, ALU.add).then_inc(ln_act, 1)
            head_slot1(HEADS)
            halves("ev_gate", 18, 2)
            dve.wait_ge(conv_sq_ready, 2)
            link(nc.vector.reciprocal(ln_rstd[:], ln_rstd[:]))
            nc.vector.tensor_tensor(conv_y, conv_y, ln_rstd[:].unsqueeze(1).to_broadcast([P, CONV_TILES, T]),
                                    ALU.mult).then_inc(ln_act, 1)
            b = BLOCK["out"]
            split_lo(b, (4,))
            for k in range(CONV_TILES):
                dve.wait_ge(conv_hi, k + 1)
                nc.vector.tensor_tensor(b_lo[:, HEADS + k, :], conv_sq[:, k, :], b_hi[:, HEADS + k, :].bitcast(F32),
                                        ALU.subtract).then_inc(conv_ready, 1)
                if k in (1, 3, 5):
                    split_lo(b, (5 + k // 2,))

            def gained(name, before, i, par):
                for tt in range(TT):
                    dve.wait_ge(y_squared, 2 * (NBLK * before + i) + tt + 1)
                    e = nc.vector.tensor_tensor(Y[:, tt, span(BW * i, BW)], acc[par][:, BW * tt:BW * (tt + 1)],
                                                grow[:, span(BW * i, BW)], ALU.mult)
                e.then_inc(acc_free, 1)

            split_lo(b + 1, (0, 1))
            halves("ev_gate", 20, 1)
            split_lo(b + 1, (2, 3))
            halves("ev_gate", 21, 1)
            dve.wait_ge(grow_in, 16)
            gained("out", 0, 0, 0)
            for n in range(1, 4):
                (run_ahead if n < 3 else most_ahead)(
                    b + n, (None, single("ev_gate", 11), single("ev_gate", 13), one_tile("ev_gate", 15))[n])
                gained("out", 0, n, n % 2)

            def add_to_residual():
                for tt in range(TT):
                    for half in (slice(0, D // 2), slice(D // 2, D)):
                        nc.vector.scalar_tensor_tensor(X[:, tt, half], Y[:, tt, half], norm_s[:, 6 + tt:7 + tt], X[:, tt, half],
                                                       ALU.mult, ALU.add).then_inc(h_ready, 1)

            def post_norm(n, meanwhile=None):
                link(nc.vector.tensor_reduce(norm_s[:, 0:2], ssq_part[:], AX.X, ALU.add))
                mean_eps(n, meanwhile)
                add_to_residual()

            def residual_norm(n, squares, next_block):
                dve.wait_ge(ssq_ready, squares)
                link(nc.vector.tensor_reduce(norm_s[:, 0:2], ssq_part[:, :, 0:2], AX.X, ALU.add))
                mean_eps(n)
                token_diagonals()
                split_lo(next_block, (2, 3))

            dve.wait_ge(x_in, 16)
            dve.wait_ge(acc_free, 2 + ACC["ff"])
            post_norm(1)
            mod_out(0, [(EV_GATE, col("ev_mod_b", 32, KT))])
            nc.vector.tensor_tensor(mod_cols[:, EV_GATE, :], mod_cols[:, EV_GATE, :], col("ev_post_g", 0, KT),
                                    ALU.mult)
            residual_norm(2, 6, BLOCK["ff"])
            norm_scaled(1, col("g_ffn_pre", 0, KT), a_hi, a_lo)
            def ff_hidden(g, unit, kt0):
                with dve.Fori(0, 2) as i:
                    for par in range(2):
                        bi = 2 * i + par
                        run_ahead(BLOCK["ff"] + 8 * g + bi, both(unit, kt0 + bi))
                        dve.wait_ge(acc_free, 2 + ACC["ff"] + 8 * g + bi + 1)
                        nc.vector.tensor_tensor(hid, relu, relu, ALU.mult).then_inc(hid_sq, 1)
                        dve.wait_ge(hid_hi, 4 * g + bi + 1)
                        nc.vector.tensor_tensor(b_lo[:, bass.ds(4 * bi, FT), :], hid,
                                                b_hi[:, bass.ds(4 * bi, FT), :].bitcast(F32), ALU.subtract).then_inc(hid_ready, 1)

            def ff_add(g, bi, par):
                block_done(BLOCK["ff"] + 8 * g + 4 + bi)
                dve.wait_ge(ff_zero, 1)
                dve.wait_ge(acc_free, 2 + ACC["ff"] + 8 * g)
                s = ff_sum[:, :, span(BW * bi, BW)]
                nc.vector.tensor_tensor(s, s, acc[par][:, :].rearrange("p (t n) -> p t n", t=TT), ALU.add).then_inc(acc_free, 1)

            def ff_outer(g, unit, kt0):
                with dve.Fori(0, 2) as i:
                    for par in range(2):
                        run_ahead(BLOCK["ff"] + 8 * g + 4 + 2 * i + par, both(unit, kt0 + 2 * i + par))
                        ff_add(g, 2 * i + par, par)

            def ff_gained(n):
                dve.wait_ge(ff_squared, NBLK * (FF_GROUPS - 1) + n + 2)
                c = slice(BW * n, BW * (n + 1))
                return nc.vector.tensor_tensor(ff_sum[:, :, c], ff_sum[:, :, c],
                                               grow[:, c].unsqueeze(1).to_broadcast([P, TT, BW]), ALU.mult)

            with dve.Fori(0, 2) as g:
                ff_hidden(g, "ev_shift", 8 * g)
                ff_outer(g, "ev_shift", 8 * g + 4)
            mod_out(1, [(EV_SHIFT, col("ev_mod_b", 0, KT)), (EV_SHIFT_C, col("ev_mod_b", 0, KT))])
            ff_hidden(2, "ev_scale", 0)
            ff_outer(2, "ev_scale", 4)
            ff_hidden(3, "ev_scale", 8)
            for n in range(NBLK):
                (run_ahead if n < NBLK - 1 else most_ahead)(BLOCK["ff"] + 28 + n, both("ev_scale", 12 + n))
                ff_add(3, n, n % 2)
                if n == 1:
                    dve.wait_ge(grow_in, 32)
                if n:
                    ff_gained(n - 1)
            dve.wait_ge(ff_squared, NBLK * FF_GROUPS + 1)
            post_norm(3, lambda: link(ff_gained(NBLK - 1)))
            scales = (EV_SCALE, EV_SCALE_C)
            mod_out(2, [(d, col("ev_mod_b", KT, KT)) for d in scales])
            for d in scales:
                link(nc.vector.scalar_tensor_tensor(mod_cols[:, d, :], mod_cols[:, d, :], 1.0, col("ev_pre_g", 0, KT),
                                                    ALU.add, ALU.mult))
            residual_norm(4, 10, BLOCK["evq"])
            norm_modulated(2, a_hi, a_lo)
            dve.wait_ge(table_in, 32)

            def head_norm(m, src, gain):
                dve.wait_ge(q_sq, m + 1)
                link(nc.vector.tensor_reduce(head_s[:, 0:8], rope_t[0].rearrange("p (h d) -> p h d", h=8), AX.X, ALU.add))
                nc.vector.tensor_scalar(head_s[:, 0:8], head_s[:, 0:8], 1.0 / HD, RMS_EPS, ALU.mult, ALU.add).then_inc(head_var, 1)
                dve.wait_ge(head_std, m + 1)
                link(nc.vector.reciprocal(head_s[:, 8:16], head_s[:, 8:16]))
                link(nc.vector.tensor_tensor(src, src, head_s[:, 8:16].unsqueeze(2).to_broadcast([P, 8, HD]), ALU.mult))
                link(nc.vector.tensor_tensor(src, src, qk_gain[:, gain, :].unsqueeze(1).to_broadcast([P, 8, HD]), ALU.mult))

            def rope(src, heads):
                n = TT * heads * HD
                t1 = rope_t[0][:, 0:n].rearrange("p (t h d) -> p t h d", t=TT, h=heads)
                t2 = rope_t[1][:, 0:n].rearrange("p (t h d) -> p t h d", t=TT, h=heads)
                half = HD // 2
                cos = rope_cos.unsqueeze(2).to_broadcast([P, TT, heads, HD])
                sin = rope_sin.unsqueeze(2).to_broadcast([P, TT, heads, HD])
                nc.vector.tensor_tensor(t1, src, cos, ALU.mult)
                nc.vector.tensor_tensor(t2[:, :, :, 0:half], src[:, :, :, half:HD], sin[:, :, :, 0:half], ALU.mult)
                link(nc.vector.tensor_tensor(t2[:, :, :, half:HD], src[:, :, :, 0:half], sin[:, :, :, half:HD], ALU.mult))
                nc.vector.tensor_tensor(src, t1, t2, ALU.add).then_inc(q_roped, 1)

            def ctx_rms(m):
                if m == 2:
                    dve.wait_ge(ssq_ready, 12)
                    mean_eps(5)
                    token_diagonals()

            ctx_tiles = [range(4), range(4, 8), range(8, KT), ()]
            for n in range(4):
                run_ahead(BLOCK["evq"] + n, (ctx_rms, one_tile("od_shift", 0), single("od_shift", 1), single("od_shift", 3))[n])
                norm_modulated(3, b_hi, b_lo, ctx_tiles[n])
                dve.wait_ge(acc_free, 2 + ACC["evq"] + n + 1)
                if n < 2:
                    head_norm(n, q_sb[n % 2].rearrange("p (h d) -> p h d", h=8), 0)
                rope(q_sb[n % 2].rearrange("p (t h d) -> p t h d", t=TT, h=FT), FT)
            for m in range(2):
                n = 4 + m

                run_ahead(BLOCK["evkv"] + m, lambda part: halves(
                    "od_shift", *((10 + 3 * part, 3) if m == 0 else ((22, 3), (25, 4), (29, 3), (32, 0))[part])))
                dve.wait_ge(acc_free, 2 + ACC["evkv"] + 2 * (m + 1))
                k3 = q_sb[n % 2]
                if m == 0:
                    head_norm(2, k3.rearrange("p (h d) -> p h d", h=8), 1)
                rope(k3[:, 0:512].rearrange("p (t h d) -> p t h d", t=TT, h=2), 2)
            mod_out(3, [(OD_SHIFT, col("od_mod_b", 0, KT))])

            def gate_diagonals(src):
                for j in range(4):
                    nc.vector.tensor_tensor(grow[:, BW * j:BW * (j + 1)].rearrange("p (f n) -> p f n", f=FT),
                                            ident[:].unsqueeze(1).to_broadcast([P, FT, P]),
                                            mod_cols[:, src, FT * j:FT * (j + 1)].unsqueeze(2).to_broadcast([P, FT, P]),
                                            ALU.mult).then_inc(diag_ready, 1)

            Z = BLOCK["evz"]

            def z_gating(i):
                dve.wait_ge(head_out, 2 + 4 * (i + 1))
                dve.wait_ge(acc_free, 2 + ACC["evz"] + i + 1)
                heads = q_T[:, span(4 * i, FT), :]
                nc.vector.tensor_tensor(heads, heads, z_gate, ALU.mult).then_inc(z_mul, 1)

            def z_split(i):
                dve.wait_ge(z_hi, i + 1)
                nc.vector.tensor_tensor(b_lo[:, span(4 * i, FT), :], q_T[:, span(4 * i, FT), :],
                                        b_hi[:, span(4 * i, FT), :].bitcast(F32), ALU.subtract).then_inc(z_ready, 1)

            def head_slots(i, windowed, first=False):
                for j in range(4):
                    scale_tile = one_tile("od_scale", 4 * i + j)
                    h = 4 * i + j
                    p = j % 2
                    ahead = Z + i + (j >= 2), (2 * j + 4) % STEPS
                    s3 = score2[p].rearrange("p (t k) -> p t k", t=TT)
                    dve.wait_ge(scores, HEAD2 + h + 1)
                    if windowed:
                        nc.vector.tensor_tensor(s3[:, :, 0:T], s3[:, :, 0:T], band, ALU.add).then_inc(biased, 1)
                        dve.wait_ge(biased, h + 1)
                    nc.vector.tensor_reduce(soft[:, p, 0:2], s3, AX.X, ALU.max).then_inc(head_max, 1)
                    dve.wait_ge(head_max, HEAD2 + h + 1)
                    if windowed:
                        nc.vector.tensor_scalar(soft[:, p, 2:4], soft[:, p, 0:2], -SCALE, neg_sink[:, span(h - 8, 1)],
                                                ALU.mult, ALU.min).then_inc(neg_max, 1)
                    else:
                        nc.vector.tensor_scalar(soft[:, p, 2:4], soft[:, p, 0:2], -SCALE, None, ALU.mult).then_inc(neg_max, 1)
                    if j == 1 and not first:
                        z_gating(i - 1)
                    dve.wait_ge(exp_done, HEAD2 + h + 1)
                    if windowed:
                        nc.vector.tensor_tensor(soft[:, p, 4:6], soft[:, p, 4:6], soft[:, p, 6:8], ALU.add).then_inc(sum_ready, 1)
                        dve.wait_ge(sum_ready, h - 7)
                    nc.vector.reciprocal(soft[:, p, 0:2], soft[:, p, 4:6]).then_inc(inv_ready, 1)
                    dve.wait_ge(inv_ready, HEAD2 + h + 1)
                    for tt in range(TT):
                        nc.vector.tensor_scalar(prob2[:, p, tt, :], prob2[:, p, tt, :], soft[:, p, tt:tt + 1], None,
                                                ALU.mult).then_inc(prob_ready, 1)
                    split_lo(ahead[0], [ahead[1]])
                    scale_tile(0)
                    if j == 3 and not first:
                        z_split(i - 1)
                    split_lo(ahead[0], [ahead[1] + 1])
                    scale_tile(2)

            head_slots(0, False, True)
            head_slots(1, False)
            with dve.Fori(2, 4) as i:
                head_slots(i, True)
            z_gating(3)
            z_split(3)
            dve.wait_ge(z_ready, 4)
            gate_diagonals(EV_GATE)

            for n in range(4):
                (run_ahead if n < 3 else most_ahead)(BLOCK["evo"] + n)
                if n == 0:
                    dve.wait_ge(row_ready, 4)
                gained("evo", 1, n, n % 2)
            dve.wait_ge(x_in, 48)
            dve.wait_ge(acc_free, 2 + ACC["odu"])
            post_norm(6)
            mod_out(4, [(OD_SCALE, col("od_mod_b", KT, KT))])
            link(nc.vector.scalar_tensor_tensor(mod_cols[:, OD_SCALE, :], mod_cols[:, OD_SCALE, :], 1.0, col("od_pre_g", 0, KT),
                                                ALU.add, ALU.mult))
            residual_norm(7, 16, BLOCK["odu"])
            norm_modulated(4, a_hi, a_lo)
            dve.wait_ge(table_in, 48)
            dve.wait_ge(a_ready, 5 * KT)
            nc.vector.memset(u_pad, 0.0).then_inc(u_zero, 1)
            def pool_windows(g):
                size = POOL_SIZES[g]
                bufs = (win_a, win_b)

                def add(level):
                    w, out_of = 2 ** (level + 1), 8 - 2 ** level
                    lo, hi = POOL_PAD - out_of, POOL_PAD + T + out_of
                    src = bufs[(level + 1) % 2] if level else u_pad
                    if level == 0:
                        e = nc.vector.tensor_tensor(bufs[0][:, :, lo:hi], src[:, :, lo - 1:hi - 1], src[:, :, lo:hi], ALU.add)
                    else:
                        e = nc.vector.tensor_tensor(bufs[level % 2][:, :, lo:hi], src[:, :, lo - w // 4:hi - w // 4],
                                                    src[:, :, lo + w // 4:hi + w // 4], ALU.add)
                    link(e)

                def part(m):
                    levels = size.bit_length() - 1
                    if m == 0:
                        dve.wait_ge(acc_free, 2 + ACC["odu"] + g + 1)
                    if m < 2:
                        for level in range(2 * m, min(2 * m + 2, levels)):
                            add(level)
                    if m == 2:
                        mean = bufs[(levels - 1) % 2][:, :, POOL_PAD:POOL_PAD + T]
                        link(nc.vector.tensor_tensor(mean, mean, inv_cnt[:, g, :].unsqueeze(1).to_broadcast([P, FT, T]), ALU.mult))
                        nc.vector.tensor_tensor(pooled, mean, u_pad[:, :, POOL_PAD:POOL_PAD + T], ALU.subtract).then_inc(u_pooled, 1)
                    if m == 3:
                        dve.wait_ge(u_hi, g + 1)
                        nc.vector.tensor_tensor(b_lo[:, FT * g:FT * (g + 1), :], pooled, b_hi[:, FT * g:FT * (g + 1), :].bitcast(F32),
                                                ALU.subtract).then_inc(u_ready, 1)
                return part

            gate_tiles = [one_tile("od_gate", 0), one_tile("od_gate", 1), single("od_gate", 2), single("od_gate", 4)]
            gate_tiles += [single("od_gate", 6 + 2 * n) for n in range(4)]
            for n in range(8):
                windows = pool_windows(n - 1) if 1 <= n <= 4 else None

                def beside(m):
                    if windows:
                        windows(m)
                    gate_tiles[n](m)
                run_ahead(BLOCK["odu"] + n, beside)
            b = BLOCK["pool"]
            dve.wait_ge(acc_free, 2 + ACC["pool"])
            for g in range(4):
                split_lo(b + (g >= 2), range(4 + 2 * g, 6 + 2 * g) if g < 2 else range(2 * g - 4, 2 * g - 2))
                if g < 2:
                    halves("od_gate", 28 + 2 * g, 2)
                dve.wait_ge(step_done, 4 + 8 * b + 2 * (g + 1))
                if g:
                    dve.wait_ge(p_ready, g)
                for f in range(FT):
                    e = nc.vector.scalar_tensor_tensor(gated[:, f, :], acc[g % 2][:, T * f:T * (f + 1)],
                                                       col("pool_scale", FT * g + f), silu_g[:, FT * g + f, :], ALU.mult, ALU.mult)
                e.then_inc(acc_free, 1)
                dve.wait_ge(p_hi, g + 1)
                nc.vector.tensor_tensor(a_lo[:, FT * g:FT * (g + 1), :], gated, a_hi[:, FT * g:FT * (g + 1), :].bitcast(F32),
                                        ALU.subtract).then_inc(p_ready, 1)
            mod_out(5, [(OD_GATE, col("od_mod_b", 2 * KT, KT))])
            link(nc.vector.tensor_tensor(mod_cols[:, OD_GATE, :], mod_cols[:, OD_GATE, :], col("od_post_g", 0, KT), ALU.mult))
            dve.wait_ge(p_ready, 4)
            gate_diagonals(OD_GATE)
            for n in range(4):
                b = BLOCK["odo"] + n
                split_lo(b, range(4, 8))
                if b < LAST_BLOCK:
                    split_lo(b + 1, range(4))
                if n == 0:
                    dve.wait_ge(row_ready, 8)
                gained("odo", 2, n, n % 2)
            dve.wait_ge(acc_free, 2 + ACC["odo"] + 4)
            post_norm(8)

        @block.tensor
        def _(pe):
            def step_feature(b, s, a2, hi, lo, first=None):
                first = s == 0 if first is None else first
                for t in range(KPS):
                    k = KPS * s + t
                    for f in range(FT):
                        o = a2[:, T * f:T * (f + 1)]
                        wh = w_hi[:, s % SLOTS, t, P * f:P * (f + 1)]
                        wl = w_lo[:, s % SLOTS, t, P * f:P * (f + 1)]
                        nc.tensor.matmul(o, wh, hi[:, k, :], start=first and t == 0 and f % 2 == 0, stop=False, skip_group_check=True)
                        nc.tensor.matmul(o, wh, lo[:, k, :], start=False, stop=False, skip_group_check=True)
                        last = nc.tensor.matmul(o, wl, hi[:, k, :], start=False, stop=t == KPS - 1, skip_group_check=True)
                return last

            def step_tokens(b, s, a2, hi, lo):
                for t in range(KPS):
                    k = KPS * s + t
                    for tt in range(TT):
                        o = a2[:, BW * tt:BW * (tt + 1)]
                        ah = hi[:, k, P * tt:P * (tt + 1)]
                        nc.tensor.matmul(o, ah, w_hi[:, s % SLOTS, t, :], start=s == 0 and t == 0, stop=False)
                        nc.tensor.matmul(o, ah, w_lo[:, s % SLOTS, t, :], start=False, stop=False)
                        last = nc.tensor.matmul(o, lo[:, k, P * tt:P * (tt + 1)], w_hi[:, s % SLOTS, t, :],
                                                start=False, stop=s == STEPS - 1 and t == KPS - 1)
                return last

            def product(b, a, par, form, hi, lo, ready=None, per=1, base=0):
                pe.wait_ge(acc_free, a + 1)
                for s in range(STEPS):
                    if ready is not None:
                        pe.wait_ge(ready, base + (KPS * s + KPS - 1) // per + 1)
                    pe.wait_ge(split_done, 8 * b + s + 9)
                    form(b, s, acc[par][:, :], hi, lo).then_inc(step_done, 1)

            def transposes(m, src, groups=range(KT // 2)):
                pe.wait_ge(scale_ready, TT * (m + 1))
                for j in groups:
                    if m < 2 and (m or j > 3):
                        pe.wait_ge(a_ready, KT * m + 2 * j - 6)
                    if m == 3 and j > 3:
                        pe.wait_ge(norm_tmp, KT + 2 * j - 2)
                    elif m >= 2 and (m > 2 or j > 3):
                        pe.wait_ge(norm_tmp, KT * (m - 2) + 2 * j - 6)
                    for k in range(2):
                        for tt in range(TT):
                            e = nc.tensor.matmul(norm_bank(m, 2 * j + k)[:, P * tt:P * (tt + 1)],
                                                 src[:, tt, P * (2 * j + k):P * (2 * j + k + 1)], token_diag[:, tt, :],
                                                 start=True, stop=True)
                    e.then_inc(tr_done, 1)

            def sum_mod(unit, vectors, u):
                pe.wait_ge(mod_acc, MOD_END[unit])
                if u:
                    pe.wait_ge(mod_cols_ready, u)
                for v in range(vectors):
                    for f in range(KT):
                        e = nc.tensor.matmul(aux[:, 3, KT * v + f:KT * v + f + 1], mod_sum[:, v, P * f:P * (f + 1)], ones[:, 0:1],
                                             start=True, stop=True)
                e.then_inc(mod_summed, 1)

            pe.sem_inc(step_done, SLOTS)
            pe.sem_inc(pv_done, 2)
            pe.wait_ge(const_in, 64)
            pe.wait_ge(ones_ready, 1)
            transposes(0, X)
            with pe.Fori(0, 2) as i:
                for par in range(2):
                    product(BLOCK["u"] + 2 * i + par, ACC["u"] + 2 * i + par, par, step_feature, a_hi, a_lo, a_ready)
            def qkv_step(n, s):
                b = BLOCK["qkv"] + n
                if s == 0:
                    pe.wait_ge(acc_free, ACC["qkv"] + n + 1)
                pe.wait_ge(split_done, 8 * b + s + 9)
                form = step_feature if n % 3 < 2 else step_tokens
                form(b, s, acc[n % 2][:, :], a_hi, a_lo).then_inc(step_done, 1)

            for n in range(3):
                for s in range(STEPS):
                    qkv_step(n, s)

            def head_slot1(m):
                p = m % 2
                if m < HEADS:
                    if m == 4:
                        pe.wait_ge(acc_free, 2 + ACC["qkv"] + 6)
                    pe.wait_ge(q_staged, m + 1)
                    for tt in range(TT):
                        e = nc.tensor.matmul(score1[p][:, T * tt:T * (tt + 1)], q_stage1[:, p, P * tt:P * (tt + 1)],
                                             qk_T[:, HEADS + m, :], start=True, stop=True)
                    e.then_inc(scores, 1)
                if m >= 1:
                    pe.wait_ge(prob_ready, TT * m)
                    if m >= 2:
                        pe.wait_ge(prob_T_ready, m - 1)
                    for k in range(TT):
                        for tt in range(TT):
                            e = nc.tensor.transpose(aux[:, 2, T * k + P * tt:T * k + P * (tt + 1)],
                                                    prob1[:, 1 - p, tt, P * k:P * (k + 1)], ident[:])
                    e.then_inc(prob_tr, 1)
                for k in range(3) if m < 4 else ():
                    qkv_step(3 + (6 * m + k) // STEPS, (6 * m + k) % STEPS)
                if m >= 1:
                    pe.wait_ge(v_staged, m)
                    pe.wait_ge(prob_T_ready, m)
                    if m >= 2:
                        pe.wait_ge(head_copied, m - 1)
                    for k in range(TT):
                        e = nc.tensor.matmul(aux[:, 3, 0:T], v_stage1[:, 1 - p, k, :], prob_T1[:, k, :], start=k == 0, stop=k == TT - 1)
                    e.then_inc(pv_done, 1)
                for k in range(3, 6) if m < 4 else ():
                    qkv_step(3 + (6 * m + k) // STEPS, (6 * m + k) % STEPS)

            def channel_sums(which, rows):
                for k in range(CONV_TILES):
                    e = nc.tensor.matmul(acc[which][:, 0:T], ones[:], rows[:, k, :], start=k == 0, stop=k == CONV_TILES - 1)
                e.then_inc(ln_sum, 1)

            for m in range(HEADS - 1):
                head_slot1(m)
            pe.wait_ge(conv_tap, CONV_TILES * TAPS)
            channel_sums(0, conv_y)
            head_slot1(HEADS - 1)
            pe.wait_ge(conv_sq_ready, 1)
            channel_sums(1, conv_sq)
            head_slot1(HEADS)
            pe.wait_ge(ln_act, 2)
            with pe.Fori(0, 2) as i:
                for par in range(2):
                    n = 2 * i + par
                    pe.wait_ge(acc_free, ACC["out"] + n + 1)
                    for s in range(STEPS):
                        pe.wait_ge(heads_ready if s < 4 else conv_ready, KPS * (s % 4) + KPS)
                        pe.wait_ge(split_done, 8 * (BLOCK["out"] + n) + s + 9)
                        step_tokens(BLOCK["out"] + n, s, acc[par][:, :], b_hi, b_lo).then_inc(step_done, 1)
            sum_mod("ev_gate", 1, 0)
            pe.wait_ge(mod_cols_ready, 1)
            transposes(1, X)
            pe.wait_ge(a_ready, 2 * KT)
            for g0, unit in ((0, "ev_shift"), (2, "ev_scale")):
                with pe.Fori(0, 2) as g:
                    with pe.Fori(0, 2) as i:
                        for par in range(2):
                            bi = 8 * (g + g0) + 2 * i + par
                            product(BLOCK["ff"] + bi, ACC["ff"] + bi, par, step_feature, a_hi, a_lo, a_ready, 1, KT)
                    with pe.Fori(0, 2) as i:
                        for par in range(2):
                            bi = 8 * (g + g0) + 4 + 2 * i + par
                            product(BLOCK["ff"] + bi, ACC["ff"] + bi, par, step_tokens, b_hi, b_lo, hid_ready, FT, 4 * (g + g0))
                sum_mod(unit, 2, 1 + g0 // 2)
            pe.wait_ge(mod_cols_ready, 3)
            transposes(2, X)

            def q_transposes(n, tiles):
                pe.wait_ge(q_roped, n + 1)
                if n:
                    pe.wait_ge(q_T_ready, n)
                else:
                    pe.wait_ge(norm_tmp, KT + 4)
                src = q_sb[n % 2]
                for x, (dst, s) in enumerate(tiles):
                    e = nc.tensor.transpose(aux[:, dst // 4, P * (dst % 4):P * (dst % 4 + 1)], src[:, P * s:P * (s + 1)], ident[:])
                e.then_inc(q_tr, 1)

            q_tiles = [(TT * h + tt, FT * tt + h) for h in range(FT) for tt in range(TT)]
            k_tiles = [(4 * h + tt, 2 * tt + h) for h in range(2) for tt in range(4)]
            for n in range(4):
                product(BLOCK["evq"] + n, ACC["evq"] + n, n % 2, step_tokens, a_hi, a_lo, a_ready, 1, 2 * KT)
                if n < 3:
                    transposes(3, Y, (range(2), range(2, 4), range(4, 8))[n])
                if n:
                    q_transposes(n - 1, q_tiles)
            for m in range(2):
                b = BLOCK["evkv"] + m
                pe.wait_ge(acc_free, ACC["evkv"] + 2 * m + 2)
                pe.wait_ge(a_ready, 4 * KT)
                for s in range(STEPS):
                    pe.wait_ge(split_done, 8 * b + s + 9)
                    step_tokens(b, s, acc[0][:, :], a_hi, a_lo)
                    step_tokens(b, s, acc[1][:, :], b_hi, b_lo).then_inc(step_done, 1)
                q_transposes(3 + m, q_tiles if m == 0 else k_tiles)
            sum_mod("od_shift", 1, 3)
            q_transposes(5, k_tiles)
            pe.wait_ge(q_T_ready, 6)
            pe.wait_ge(acc_free, 2 + ACC["evz"])
            pe.wait_ge(mod_cols_ready, 4)
            Z = BLOCK["evz"]

            def prob_transposes(h, j, half):
                p = j % 2
                pe.wait_ge(prob_ready, TT * (HEAD2 + h + 1))
                if half or not isinstance(h, int) or h > 0:
                    pe.wait_ge(prob_T_ready, HEADS + 2 * h + half)
                for k in range(2):
                    for tt in range(TT):
                        e = nc.tensor.transpose(aux[:, 2, T * k + P * tt:T * k + P * (tt + 1)],
                                                prob2[:, p, tt, P * (2 * half + k):P * (2 * half + k + 1)], ident[:])
                e.then_inc(prob_tr, 1)

            def weigh_v(h, i):
                pe.wait_ge(v_staged, HEADS + i + 1)
                pe.wait_ge(prob_T_ready, HEADS + 2 * h + 2)
                pe.wait_ge(head_out, 2 + h)
                for k in range(4):
                    e = nc.tensor.matmul(aux[:, 3, 0:T], v_stage2[:, k, :], prob_T2[:, k, :], start=k == 0, stop=k == 3)
                e.then_inc(pv_done, 1)

            def z_step(i, s):
                pe.wait_ge(split_done, 8 * (Z + i) + s + 9)
                step_feature(Z + i, s, acc[0][:, :], a_hi, a_lo).then_inc(step_done, 1)

            def head_slots(i, first=False):
                for j in range(4):
                    h = 4 * i + j
                    before = not first or j >= 1
                    pe.wait_ge(q_staged, HEADS + h + 1)
                    for tt in range(TT):
                        e = nc.tensor.matmul(score2[j % 2][:, 512 * tt:512 * (tt + 1)], q_stage2[:, j % 2, P * tt:P * (tt + 1)],
                                             k_T[:, span(i, 1), :].rearrange("p a t -> p (a t)"), start=True, stop=True)
                    e.then_inc(scores, 1)
                    if before:
                        prob_transposes(h - 1, j + 1, 0)
                    if j == 0 and not first:
                        pe.wait_ge(acc_free, 2 + ACC["evz"] + i)
                    z_step(i, 2 * j)
                    if before:
                        prob_transposes(h - 1, j + 1, 1)
                    z_step(i, 2 * j + 1)
                    if before:
                        weigh_v(h - 1, i - 1 if j == 0 else i)

            head_slots(0, True)
            with pe.Fori(1, 4) as i:
                head_slots(i)
            prob_transposes(15, 3, 0)
            prob_transposes(15, 3, 1)
            weigh_v(15, 3)

            def gate_rows(g):
                for j in range(4):
                    pe.wait_ge(diag_ready, 4 * g + j + 1)
                    nc.tensor.matmul(aux[:, j, :], ones[:], grow[:, BW * j:BW * (j + 1)], start=True, stop=True).then_inc(row_sum, 1)

            pe.wait_ge(acc_free, 2 + ACC["evo"])
            for n in range(4):
                product(BLOCK["evo"] + n, ACC["evo"] + n, n % 2, step_tokens, b_hi, b_lo, z_ready, FT, 0)
                if n == 0:
                    pe.wait_ge(head_out, 2 + 16)
                    gate_rows(0)
            pe.wait_ge(row_ready, 4)
            sum_mod("od_scale", 1, 4)
            pe.wait_ge(mod_cols_ready, 5)
            transposes(4, X)
            for g in range(4):
                product(BLOCK["odu"] + g, ACC["odu"] + g, g % 2, step_feature, a_hi, a_lo, a_ready, 1, 4 * KT)
            with pe.Fori(0, 2) as i:
                for par in range(2):
                    product(BLOCK["odg"] + 2 * i + par, ACC["odg"] + 2 * i + par, par, step_feature, a_hi, a_lo)
            b = BLOCK["pool"]
            for g in range(4):
                pe.wait_ge(acc_free, ACC["pool"] + g + 1)
                pe.wait_ge(u_ready, g + 1)
                for x in range(2):
                    s = 2 * g + x
                    pe.wait_ge(split_done, 8 * b + s + 9)
                    step_feature(b, s, acc[g % 2][:, :], b_hi, b_lo, first=x == 0).then_inc(step_done, 1)
            pe.wait_ge(norm_tmp, 3 * KT)
            sum_mod("od_gate", 1, 5)
            for n in range(4):
                product(BLOCK["odo"] + n, ACC["odo"] + n, n % 2, step_tokens, a_hi, a_lo, p_ready, FT, 0)
                if n == 0:
                    pe.wait_ge(mod_cols_ready, 6)
                    gate_rows(1)


def shape_constants():
    pos = np.arange(T)
    d = pos[:, None] - pos[None, :]
    dist = np.where(d >= 0, -d, -1e32).astype(np.float32)
    band = np.where(np.abs(d) <= WINDOW, 0.0, -1e30).astype(np.float32)
    freqs = HD // 4
    inv = (np.float32(10000.0) ** (-np.arange(freqs, dtype=np.float32) / np.float32(freqs))).astype(np.float32)
    row = (pos // GRID_W).astype(np.float32)
    column = (pos % GRID_W).astype(np.float32)
    ang = np.concatenate([row[:, None] * inv, column[:, None] * inv], axis=-1).astype(np.float32)
    cos = np.concatenate([np.cos(ang)] * 2, axis=-1).astype(np.float32)
    sin = np.concatenate([-np.sin(ang), np.sin(ang)], axis=-1).astype(np.float32)
    count = [np.clip(pos + w // 2, 0, T) - np.clip(pos - w // 2, 0, T) for w in POOL_SIZES]
    inv_count = np.stack([1.0 / c for c in count]).astype(np.float32).reshape(1, -1)
    tiles = lambda a: a.reshape(TT, P, -1).transpose(1, 0, 2).reshape(P, -1)
    return {
        "ident": np.eye(P, dtype=np.float32),
        "dist_neg": np.ascontiguousarray(tiles(dist)),
        "ev_table": np.ascontiguousarray(np.concatenate([tiles(cos), tiles(sin), tiles(band)], axis=1)),
        "od_table": np.ascontiguousarray(np.broadcast_to(inv_count, (P, inv_count.shape[1]))),
        "slope": np.broadcast_to((2.0 ** (-8.0 * np.arange(1, HEADS + 1) / HEADS) / SCALE).astype(np.float32), (P, HEADS)),
    }


def kernel(**inputs):
    import concourse.bacc as bacc
    from concourse.bass_utils import run_bass_kernel_spmd

    a = {n: np.asarray(v) for n, v in inputs.items()}
    consts = shape_constants()

    def column(v):
        return v.reshape(-1, P).T

    packed = {
        "g_mix_pre": column(a["g_mix_pre"]), "b_glu": column(a["b_glu"]), "b_dw": column(a["b_dw"]),
        "ln_g": column(a["ln_conv_g"]), "ln_b": column(a["ln_conv_b"]), "g_ffn_pre": column(a["g_ffn_pre"]),
        "c": column(a["c_2"]), "c_ctx": column(a["c_ctx_2"]), "ev_mod_b": column(a["ev_mod_b_2"]),
        "ev_pre_g": column(a["ev_pre_g_2"]), "ev_post_g": column(a["ev_post_g_2"]), "od_mod_b": column(a["od_mod_b_2"]),
        "od_pre_g": column(a["od_pre_g_2"]), "od_post_g": column(a["od_post_g_2"]), "pool_scale": column(a["od_pool_scale_2"]),
        "sink": np.broadcast_to(a["ev_sink_2"].reshape(1, HEADS), (P, HEADS)), "slope": consts.pop("slope"),
        "w_dw": a["w_dw"].reshape(TAPS, CONV_TILES, P).transpose(2, 1, 0).reshape(P, CONV_TILES * TAPS),
    }
    arrays = {
        "x": a["x"].reshape(T, D), "ctx": a["ctx_2"].reshape(T, D),
        "w_in": a["w_in"][0], "w_out": a["w_out"][0], "w_ff1": a["w_ff1"][0], "w_ff2": a["w_ff2"][0],
        "ev_mod_w": a["ev_mod_w_2"][0], "ev_w_in": a["ev_w_in_2"][0], "ev_w_out": a["ev_w_out_2"][0],
        "od_mod_w": a["od_mod_w_2"][0], "od_w_in": a["od_w_in_2"][0], "od_w_out": a["od_w_out_2"][0],
        "od_pool_w": a["od_pool_w_2"][0].reshape(D, BW),
        "g_mix_post": a["g_mix_post"].reshape(D), "g_ffn_post": a["g_ffn_post"].reshape(D),
        "q_norm": a["ev_q_norm_2"].reshape(HD), "k_norm": a["ev_k_norm_2"].reshape(HD),
        "cols": np.concatenate([packed[n] for n, _ in COLS], axis=1),
        **consts,
    }
    arrays = {f"in_{n}": np.ascontiguousarray(v) for n, v in arrays.items()}
    nc = bacc.Bacc("TRN2", target_bir_lowering=False, num_devices=1)
    io = {n[3:]: nc.dram_tensor(n, v.shape, mybir.dt.from_np(v.dtype), kind="ExternalInput").ap() for n, v in arrays.items()}
    out = nc.dram_tensor("out", (T, D), F32, kind="ExternalOutput").ap()
    build_program(nc, io, out)
    result = run_bass_kernel_spmd(nc, [arrays], core_ids=[0])
    return result.results[0]["out"].reshape(1, T, D)
```
